# Optimizing a Trainium2 kernel written in Bass

```python
import math
import jax, jax.numpy as jnp
from jax import lax
import numpy as np

D_MODEL = 1024
BATCH = 1
SEQ = 256
DEPTH = 2
DEC_BATCH = 8
DEC_SEQ = 4
PAST_LEN = 2048
PAGE_SIZE = 128

MIX = D_MODEL
HEAD_DIM = 64
A_W = MIX // 4
B_W = (3 * MIX) // 8
C_W = MIX - A_W - B_W
A_DK = HEAD_DIM
A_DV = HEAD_DIM
A_HEADS = A_W // A_DV
B_BD = HEAD_DIM
B_BLOCKS = B_W // B_BD
C_DK = HEAD_DIM
C_DV = HEAD_DIM
C_HEADS = C_W // C_DV
LRU_C = 8.0
CONV_W = 4
CHUNK = 64
DN_CONV_CH = 2 * C_HEADS * C_DK + C_W
IN_SPLITS = (A_HEADS * A_DK, A_HEADS * A_DK, A_W, A_W, B_W, B_W,
             C_HEADS * C_DK, C_HEADS * C_DK, C_W, C_W, C_HEADS, C_HEADS)
N_IN = sum(IN_SPLITS)
PEER_HEADS = 8
PEER_DQ = 128
PEER_NKEYS = 128
PEER_TOPK = 16
PEER_N = PEER_NKEYS * PEER_NKEYS
PEER_BLOCK = 256
EPS = 1e-6

kernel_name = 'hymba_hgrn2_rglru_gdn_peer_step'

def rmsnorm(x, g):
    xf = x.astype(jnp.float32)
    y = xf * lax.rsqrt(jnp.mean(xf * xf, axis=-1, keepdims=True) + EPS)
    return (y * g.astype(jnp.float32)).astype(x.dtype)

def gated_head_norm(o, z, g):
    of = o.astype(jnp.float32)
    y = of * lax.rsqrt(jnp.mean(of * of, axis=-1, keepdims=True) + EPS)
    return y * g.astype(jnp.float32) * jax.nn.silu(z.astype(jnp.float32))

def l2norm(x):
    return x * lax.rsqrt(jnp.sum(x * x, axis=-1, keepdims=True) + EPS)

def causal_conv(x, buf, w, b=None):
    xp = jnp.concatenate([buf.astype(x.dtype), x], axis=1)
    L = x.shape[1]
    y = xp[:, 0:L] * w[0]
    for k in range(1, CONV_W):
        y = y + xp[:, k:k + L] * w[k]
    if b is not None:
        y = y + b
    return y, xp[:, -(CONV_W - 1):]

def chunk_len(L):
    return CHUNK if L % CHUNK == 0 else L

def to_chunks(x, C):
    B, L = x.shape[:2]
    x = x.reshape((B, L // C, C) + x.shape[2:])
    if x.ndim == 5:
        return jnp.transpose(x, (1, 0, 3, 2, 4))
    return jnp.transpose(x, (1, 0, 3, 2))

def from_chunks(o):
    nc, B, H, C, d = o.shape
    return jnp.transpose(o, (1, 0, 3, 2, 4)).reshape(B, nc * C, H, d)

def hgrn2_chunked(q, k, v, log_f, S0):
    C = chunk_len(q.shape[1])
    mask = jnp.tril(jnp.ones((C, C), bool))[:, :, None]

    def step(S, inp):
        qc, kc, vc, lf = inp
        G = jnp.cumsum(lf, axis=2)
        Gl = G[:, :, -1]
        o_inter = jnp.einsum('bhik,bhkv->bhiv', qc * jnp.exp(G), S)
        diff = G[:, :, :, None, :] - G[:, :, None, :, :]
        decay = jnp.exp(jnp.where(mask, diff, -jnp.inf))
        A = jnp.einsum('bhik,bhjk,bhijk->bhij', qc, kc, decay)
        o = o_inter + jnp.einsum('bhij,bhjv->bhiv', A, vc)
        S = S * jnp.exp(Gl)[..., None] + jnp.einsum('bhjk,bhjv->bhkv', kc * jnp.exp(Gl[:, :, None, :] - G), vc)
        return S, o

    S, o = lax.scan(step, S0, (to_chunks(q, C), to_chunks(k, C), to_chunks(v, C), to_chunks(log_f, C)))
    return from_chunks(o), S

def delta_chunked(q, k, v, beta, g, S0):
    C = chunk_len(q.shape[1])
    strict = jnp.tril(jnp.ones((C, C), bool), -1)
    incl = jnp.tril(jnp.ones((C, C), bool))
    eye = jnp.eye(C, dtype=jnp.float32)

    def step(S, inp):
        qc, kc, vc, bc, gc = inp
        G = jnp.cumsum(gc, axis=-1)
        eG = jnp.exp(G)
        diff = G[..., :, None] - G[..., None, :]
        dec_s = jnp.exp(jnp.where(strict, diff, -jnp.inf))
        dec_i = jnp.exp(jnp.where(incl, diff, -jnp.inf))
        M = eye + bc[..., :, None] * jnp.einsum('bhik,bhjk->bhij', kc, kc) * dec_s
        rhs = bc[..., None] * (vc - eG[..., None] * jnp.einsum('bhik,bhkv->bhiv', kc, S))
        E = lax.linalg.triangular_solve(M, rhs, left_side=True, lower=True)
        qk = jnp.einsum('bhik,bhjk->bhij', qc, kc) * dec_i
        o = eG[..., None] * jnp.einsum('bhik,bhkv->bhiv', qc, S) + jnp.einsum('bhij,bhjv->bhiv', qk, E)
        Gl = G[..., -1]
        S = jnp.exp(Gl)[..., None, None] * S + jnp.einsum('bhjk,bhjv->bhkv', kc * jnp.exp(Gl[..., None] - G)[..., None], E)
        return S, o

    S, o = lax.scan(step, S0, (to_chunks(q, C), to_chunks(k, C), to_chunks(v, C), to_chunks(beta, C), to_chunks(g, C)))
    return from_chunks(o), S

def rglru_scan(a, b, h0):
    b = b.at[:, 0].add(a[:, 0] * h0)

    def comb(l, r):
        return (l[0] * r[0], r[0] * l[1] + r[1])

    _, h = lax.associative_scan(comb, (a, b), axis=1)
    return h, h[:, -1]

def split_cols(z):
    offs = [int(o) for o in np.cumsum(IN_SPLITS)[:-1]]
    return jnp.split(z, offs, axis=-1)

def mixer(h, st, lb, p):
    f32 = jnp.float32
    Bsz, L, _ = h.shape
    dt = h.dtype
    z = h @ p['w_in']
    aq, af, ai, ag, bx, by, cq, ck, cv, cz, cb, ca = split_cols(z)
    f = lb + (1.0 - lb) * jax.nn.sigmoid(af.astype(f32))
    qa = (jax.nn.silu(aq.astype(f32)) * A_DK ** -0.5).reshape(Bsz, L, A_HEADS, A_DK)
    ka = (1.0 - f).reshape(Bsz, L, A_HEADS, A_DK)
    lfa = jnp.log(f).reshape(Bsz, L, A_HEADS, A_DK)
    va = ai.astype(f32).reshape(Bsz, L, A_HEADS, A_DV)
    oa, S_a = hgrn2_chunked(qa, ka, va, lfa, st[0].astype(f32))
    oa = gated_head_norm(oa, ag.reshape(Bsz, L, A_HEADS, A_DV), p['a_norm_g']).reshape(Bsz, L, A_W).astype(dt)
    xc, buf_b = causal_conv(bx, st[2], p['lru_conv_w'], p['lru_conv_b'])
    xcf = xc.astype(f32)
    xblk = xcf.reshape(Bsz, L, B_BLOCKS, B_BD)
    r = jax.nn.sigmoid(jnp.einsum('blnd,nde->blne', xblk, p['lru_wa'].astype(f32)).reshape(Bsz, L, B_W) + p['lru_ba'])
    ig = jax.nn.sigmoid(jnp.einsum('blnd,nde->blne', xblk, p['lru_wx'].astype(f32)).reshape(Bsz, L, B_W) + p['lru_bx'])
    log_a = -LRU_C * r * jax.nn.softplus(-p['lru_L'].astype(f32))
    a = jnp.exp(log_a)
    bt = jnp.sqrt(-jnp.expm1(2.0 * log_a)) * ig * xcf
    hs, hT = rglru_scan(a, bt, st[1].astype(f32))
    ob = (hs * jax.nn.gelu(by.astype(f32))).astype(dt)
    qkv, buf_c = causal_conv(jnp.concatenate([cq, ck, cv], axis=-1), st[4], p['dn_conv_w'])
    qkv = jax.nn.silu(qkv.astype(f32))
    qc, kc, vc = jnp.split(qkv, [C_HEADS * C_DK, 2 * C_HEADS * C_DK], axis=-1)
    qc = l2norm(qc.reshape(Bsz, L, C_HEADS, C_DK)) * C_DK ** -0.5
    kc = l2norm(kc.reshape(Bsz, L, C_HEADS, C_DK))
    vc = vc.reshape(Bsz, L, C_HEADS, C_DV)
    beta = jax.nn.sigmoid(cb.astype(f32))
    gdec = -jnp.exp(p['dn_A_log'].astype(f32)) * jax.nn.softplus(ca.astype(f32) + p['dn_dt_bias'])
    oc, S_c = delta_chunked(qc, kc, vc, beta, gdec, st[3].astype(f32))
    oc = gated_head_norm(oc, cz.reshape(Bsz, L, C_HEADS, C_DV), p['dn_norm_g']).reshape(Bsz, L, C_W).astype(dt)
    out = jnp.concatenate([oa, ob, oc], axis=-1) @ p['w_out']
    new_st = (S_a.astype(st[0].dtype), hT.astype(st[1].dtype), buf_b.astype(st[2].dtype),
              S_c.astype(st[3].dtype), buf_c.astype(st[4].dtype))
    return out, new_st

def peer(h, wq, k1, k2, u, v):
    Bsz, L, D = h.shape
    T = Bsz * L
    nblk = -(-T // PEER_BLOCK)
    hb = jnp.pad(h.reshape(T, D), ((0, nblk * PEER_BLOCK - T), (0, 0))).reshape(nblk, PEER_BLOCK, D)
    half = PEER_DQ // 2

    def blk(xb):
        q = (xb @ wq).reshape(-1, PEER_HEADS, 2, half)
        s1 = jnp.einsum('thd,nd->thn', q[:, :, 0], k1)
        s2 = jnp.einsum('thd,nd->thn', q[:, :, 1], k2)
        v1, i1 = lax.top_k(s1, PEER_TOPK)
        v2, i2 = lax.top_k(s2, PEER_TOPK)
        cand = (v1[..., :, None] + v2[..., None, :]).reshape(-1, PEER_HEADS, PEER_TOPK * PEER_TOPK)
        cidx = (i1[..., :, None] * PEER_NKEYS + i2[..., None, :]).reshape(-1, PEER_HEADS, PEER_TOPK * PEER_TOPK)
        sc, pos = lax.top_k(cand, PEER_TOPK)
        idx = jnp.take_along_axis(cidx, pos, axis=-1)
        gw = jax.nn.softmax(sc.astype(jnp.float32), axis=-1)
        act = jax.nn.gelu(jnp.einsum('thkd,td->thk', jnp.take(u, idx, axis=0), xb).astype(jnp.float32))
        return jnp.einsum('thk,thkd->td', (gw * act).astype(xb.dtype), jnp.take(v, idx, axis=0))

    y = lax.map(blk, hb).reshape(-1, D)[:T]
    return y.reshape(Bsz, L, D)

def trunk(x, c, states, stk, lb_all, final_norm_g):
    new = [[] for _ in range(5)]
    for l in range(DEPTH):
        p = {name: arr[l] for name, arr in stk.items()}
        mod = jax.nn.silu(c) @ p['w_ada'] + p['b_ada']
        sh1, sc1, gt1, sh2, sc2, gt2 = jnp.split(mod, 6, axis=-1)
        h = rmsnorm(x, p['norm1_g']) * (1.0 + sc1[:, None]) + sh1[:, None]
        mo, st = mixer(h, tuple(s[l] for s in states), lb_all[l], p)
        x = x + gt1[:, None] * mo
        h = rmsnorm(x, p['norm2_g']) * (1.0 + sc2[:, None]) + sh2[:, None]
        x = x + gt2[:, None] * peer(h, p['peer_wq'], p['peer_k1'], p['peer_k2'], p['peer_u'], p['peer_v'])
        for j in range(5):
            new[j].append(st[j])
    y = rmsnorm(x, final_norm_g)
    return y, [jnp.stack(n) for n in new]

def setup_inputs(seed: int = 0) -> dict:
    key = jax.random.key(seed)
    ks = iter(jax.random.split(key, 48))
    f32 = jnp.float32

    def nrm(shape, s):
        return jax.random.normal(next(ks), shape, f32) * s

    a0 = jax.random.uniform(next(ks), (DEPTH, B_W), f32, 0.9, 0.999)
    sa = a0 ** (1.0 / LRU_C)
    dtv = jnp.exp(jax.random.uniform(next(ks), (DEPTH, C_HEADS), f32, math.log(1e-3), math.log(0.1)))
    return {
        'x_prompt': nrm((BATCH, SEQ, D_MODEL), 1.0),
        'x_sample': nrm((DEC_BATCH, DEC_SEQ, D_MODEL), 1.0),
        'state_hgrn': nrm((DEPTH, DEC_BATCH, A_HEADS, A_DK, A_DV), 0.5),
        'state_lru_h': nrm((DEPTH, DEC_BATCH, B_W), 0.5),
        'state_lru_conv': nrm((DEPTH, DEC_BATCH, CONV_W - 1, B_W), 1.0),
        'state_dn': nrm((DEPTH, DEC_BATCH, C_HEADS, C_DK, C_DV), 0.3),
        'state_dn_conv': nrm((DEPTH, DEC_BATCH, CONV_W - 1, DN_CONV_CH), 1.0),
        'c_prompt': nrm((BATCH, D_MODEL), 1.0),
        'c_sample': nrm((DEC_BATCH, D_MODEL), 1.0),
        'w_ada': nrm((DEPTH, D_MODEL, 6 * D_MODEL), 0.5 * D_MODEL ** -0.5),
        'b_ada': nrm((DEPTH, 6 * D_MODEL), 0.01),
        'norm1_g': 1.0 + nrm((DEPTH, D_MODEL), 0.01),
        'norm2_g': 1.0 + nrm((DEPTH, D_MODEL), 0.01),
        'w_in': nrm((DEPTH, D_MODEL, N_IN), D_MODEL ** -0.5),
        'lb_param': nrm((DEPTH, A_HEADS * A_DK), 0.1),
        'a_norm_g': 1.0 + nrm((DEPTH, A_DV), 0.01),
        'lru_conv_w': nrm((DEPTH, CONV_W, B_W), CONV_W ** -0.5),
        'lru_conv_b': nrm((DEPTH, B_W), 0.01),
        'lru_wa': nrm((DEPTH, B_BLOCKS, B_BD, B_BD), B_BD ** -0.5),
        'lru_ba': nrm((DEPTH, B_W), 0.01),
        'lru_wx': nrm((DEPTH, B_BLOCKS, B_BD, B_BD), B_BD ** -0.5),
        'lru_bx': nrm((DEPTH, B_W), 0.01),
        'lru_L': jnp.log(sa) - jnp.log1p(-sa),
        'dn_conv_w': nrm((DEPTH, CONV_W, DN_CONV_CH), CONV_W ** -0.5),
        'dn_A_log': jnp.log(jax.random.uniform(next(ks), (DEPTH, C_HEADS), f32, 1.0, 16.0)),
        'dn_dt_bias': dtv + jnp.log(-jnp.expm1(-dtv)),
        'dn_norm_g': 1.0 + nrm((DEPTH, C_DV), 0.01),
        'w_out': nrm((DEPTH, MIX, D_MODEL), MIX ** -0.5),
        'peer_wq': nrm((DEPTH, D_MODEL, PEER_HEADS * PEER_DQ), D_MODEL ** -0.5),
        'peer_k1': nrm((DEPTH, PEER_NKEYS, PEER_DQ // 2), (PEER_DQ // 2) ** -0.5),
        'peer_k2': nrm((DEPTH, PEER_NKEYS, PEER_DQ // 2), (PEER_DQ // 2) ** -0.5),
        'peer_u': nrm((DEPTH, PEER_N, D_MODEL), D_MODEL ** -0.5),
        'peer_v': nrm((DEPTH, PEER_N, D_MODEL), PEER_HEADS ** -0.5),
        'final_norm_g': 1.0 + nrm((D_MODEL,), 0.01),
    }

def reference(x_prompt, x_sample, state_hgrn, state_lru_h, state_lru_conv, state_dn, state_dn_conv,
              c_prompt, c_sample, w_ada, b_ada, norm1_g, norm2_g, w_in, lb_param, a_norm_g,
              lru_conv_w, lru_conv_b, lru_wa, lru_ba, lru_wx, lru_bx, lru_L,
              dn_conv_w, dn_A_log, dn_dt_bias, dn_norm_g, w_out,
              peer_wq, peer_k1, peer_k2, peer_u, peer_v, final_norm_g):
    stk = dict(w_ada=w_ada, b_ada=b_ada, norm1_g=norm1_g, norm2_g=norm2_g, w_in=w_in,
               a_norm_g=a_norm_g, lru_conv_w=lru_conv_w, lru_conv_b=lru_conv_b,
               lru_wa=lru_wa, lru_ba=lru_ba, lru_wx=lru_wx, lru_bx=lru_bx, lru_L=lru_L,
               dn_conv_w=dn_conv_w, dn_A_log=dn_A_log, dn_dt_bias=dn_dt_bias, dn_norm_g=dn_norm_g,
               w_out=w_out, peer_wq=peer_wq, peer_k1=peer_k1, peer_k2=peer_k2,
               peer_u=peer_u, peer_v=peer_v)
    lbs = jax.nn.softmax(lb_param.astype(jnp.float32), axis=0)
    lb_all = jnp.cumsum(lbs, axis=0) - lbs[0]
    sample_states = (state_hgrn, state_lru_h, state_lru_conv, state_dn, state_dn_conv)
    prompt_states = tuple(jnp.zeros((DEPTH, BATCH) + s.shape[2:], s.dtype) for s in sample_states)
    y_prompt, pst = trunk(x_prompt, c_prompt, prompt_states, stk, lb_all, final_norm_g)
    y_sample, sst = trunk(x_sample, c_sample, sample_states, stk, lb_all, final_norm_g)
    p_hgrn, p_lru_h, p_lru_conv, p_dn, p_dn_conv = pst
    s_hgrn, s_lru_h, s_lru_conv, s_dn, s_dn_conv = sst
    return (y_prompt, y_sample, p_hgrn, p_lru_h, p_lru_conv, p_dn, p_dn_conv,
            s_hgrn, s_lru_h, s_lru_conv, s_dn, s_dn_conv)


_drawn_inputs = setup_inputs


def setup_inputs(seed=0):
    import zlib

    import numpy as np

    out = dict(_drawn_inputs(seed))
    spreads = {}
    factors = {'norm1_g': 3.355,
     'norm2_g': 34.157,
     'a_norm_g': 43.443,
     'lru_ba': 40.606,
     'lru_bx': 31.147,
     'dn_norm_g': 36.712,
     'final_norm_g': 31.381,
     'lru_conv_b': 5.018}
    for name, (base, spread) in spreads.items():
        noise = np.random.default_rng([zlib.crc32(name.encode()), seed]).standard_normal(out[name].shape)
        drawn = base * np.exp(spread * noise) if base else spread * noise
        out[name] = __import__('jax').numpy.asarray(drawn.astype(out[name].dtype))
    for name, factor in factors.items():
        out[name] = (out[name] * factor).astype(out[name].dtype)
    return out
```

```python
from contextlib import ExitStack, contextmanager

import concourse.bass as bass
from concourse import mybir

F32 = mybir.dt.float32
U32 = mybir.dt.uint32
ALU = mybir.AluOpType
ACT = mybir.ActivationFunctionType
AX = mybir.AxisListType.X
ds = bass.ds

P = 128
D = 1024
KD = D // P
DEPTH = 2
NP = 256
NB, NS = 8, 4
NT = NP + NB * NS
EPS = 1e-6
HD = 64
CONV = 4
A_PAIRS, B_TILES, C_PAIRS = 2, 3, 3
C_HEADS = 6
HEADS, NKEYS, TOPK = 8, 128, 16

RING = 4
ADA_TILES = 6 * KD
IN_TILES = 26
T_ADA = 0
T_IN = T_ADA + ADA_TILES
T_BETA = T_IN + IN_TILES
T_GATE = T_BETA + 1
T_OUT = T_GATE + 1
T_QUERY = T_OUT + KD
T_U = T_QUERY + KD
T_V = T_U + NKEYS
TILES = T_V + NKEYS
SILU_Z = [0, 1, 6, 7, 23, 24, 25]
PLAIN_Z = [4, 5, 8, 9, 10, 14, 15, 16, 17, 18, 19, 20, 21, 22]
SIGM_Z = [2, 3]
GELU_Z = [11, 12, 13]
Z_ORDER = SILU_Z + PLAIN_Z + SIGM_Z + GELU_Z

XP = CONV - 1 + NP
XS = CONV - 1 + NS
XW = XP + NB * XS
YW = XW - (CONV - 1)
SS = NS + 1
SW = NP + NB * SS

SMALL = {}
_at = 0
for _name, _n in (("norm1", KD), ("norm2", KD), ("b_ada", 6 * KD), ("lru_w", B_TILES * CONV), ("lru_b", B_TILES),
                  ("dn_w", 9 * CONV), ("ba", B_TILES), ("bx", B_TILES), ("lru_L", B_TILES), ("a_norm", 1),
                  ("dn_norm", 1), ("a_log", C_HEADS), ("dt_bias", C_HEADS), ("final", KD), ("lb", DEPTH * A_PAIRS),
                  ("lb_on", 1), ("keys", NKEYS), ("lru_h", B_TILES * NB),
                  ("lru_conv", B_TILES * NB * (CONV - 1)), ("dn_conv", 9 * NB * (CONV - 1))):
    SMALL[_name] = (_at, _at + _n)
    _at += _n
SMALL_W = _at
MIXC = {}
_at = 0
for _name, _n in (("block_ones", P), ("levels", 7 * P), ("tri", P), ("tri_s", 32), ("neg", P), ("neg_s", 32),
                  ("window", 2 * 127), ("batch_cols", NB * 32), ("batch_rows", NB)):
    MIXC[_name] = (_at, _at + _n)
    _at += _n
MIXC_W = _at
KEEP_W = 3 * P + 1
OUTS = {}
_at = 0
for _name, _n in (("p_h", B_TILES), ("s_h", B_TILES * NB), ("p_lc", B_TILES * 3), ("s_lc", B_TILES * NB * 3),
                  ("p_dc", 9 * 3), ("s_dc", 9 * NB * 3)):
    OUTS[_name] = (_at, _at + _n)
    _at += _n
OUTS_W = _at
STATE_W = (A_PAIRS + C_PAIRS) * (1 + NB) * HD
LOG1P = [1.0 / k for k in (13, 11, 9, 7, 5, 3)]


class Chain:

    def __init__(self, eng, sem, base=0):
        self.eng, self.sem, self.base, self.n = eng, sem, base, 0

    def __call__(self, ins):
        self.n += 1
        ins.then_inc(self.sem, 1)
        self.eng.wait_ge(self.sem, self.base + self.n)


def hold(eng, sem, value, spare):
    eng.wait_ge(sem, value)
    eng.sem_inc(spare, 1)


class Area:

    def __init__(self, tensor, at=0):
        self.tensor, self.at = tensor, at

    def take(self, *shape, dtype=None):
        n = 1
        for s in shape:
            n *= s
        ap = self.tensor[:, self.at:self.at + n]
        self.at += n
        assert self.at <= self.tensor.shape[1]
        if dtype is not None:
            ap = ap.bitcast(dtype)
        names = "abcd"[:len(shape)]
        if len(shape) > 1:
            ap = ap.rearrange(f"p ({' '.join(names)}) -> p {' '.join(names)}", **dict(zip(names, shape)))
        return ap


def spread(ap, axis, n):
    ap = ap.unsqueeze(axis)
    shape = list(ap.shape)
    shape[axis] = n
    return ap.broadcast_to(shape)


def batched(ap):
    return ap.rearrange("p k (b s) -> p k b s", b=NB)


@contextmanager
def signals(nc, names):
    with ExitStack() as ctx:
        sems = {n: ctx.enter_context(nc.semaphore(n)) for n in names.split()}
        yield sems
        for s in sems.values():
            nc.sync.sem_clear(s)
        nc.all_engine_barrier()


class Memory:

    def __init__(self, nc, ctx):
        def sb(name, shape, dtype=F32):
            return ctx.enter_context(nc.sbuf_tensor(name, shape, dtype))

        self.x = sb("x_res", [P, KD, NT])
        self.h = sb("h_norm", [P, KD, NT])
        self.ring = sb("ring", [P, RING, D])
        self.keep = sb("keep", [P, KEEP_W])
        self.small = sb("small", [P, SMALL_W])
        self.mod = sb("mod", [P, 6 * KD, 1 + NB])
        self.gain = sb("gain", [P, 2, KD, 1 + NB])
        self.cond = sb("cond", [P, KD, 1 + NB])
        self.rms = sb("rms", [P, NT])
        self.sel = sb("sel", [P, 3, 3, HEADS * TOPK])
        self.selT = sb("selT", [P, 3, NT])
        self.onehot = sb("onehot", [P, 2, 6, P])
        self.cols = sb("cols", [P, 12])
        self.big = sb("big", [P, NKEYS * NT])
        self.act = self.big[:, :].rearrange("p (e t) -> p e t", t=NT)
        self.ident = self.keep[:, 0:P]
        self.ones = self.keep[:, P:2 * P]
        self.iota = self.keep[:, 2 * P:3 * P]
        self.eps = self.keep[:, 3 * P:3 * P + 1]
        self.loaded = [ctx.enter_context(nc.semaphore(f"tile_loaded{i}")) for i in range(RING)]
        self.done = [ctx.enter_context(nc.semaphore(f"tile_done{i}")) for i in range(RING)]
        a = Area(self.big)
        self.mixc = a.take(MIXC_W)
        self.zact = a.take(14, NT)
        self.tok = a.take(3, 2 * C_HEADS)
        self.beta = a.take(3, C_HEADS)
        self.decay = a.take(3, C_HEADS)
        self.qkv = a.take(9, NT)
        self.mixed = a.take(KD, NT)
        self.outs = a.take(OUTS_W)
        self.states = a.take(A_PAIRS + C_PAIRS, 1 + NB, HD)
        self.state0 = a.take(A_PAIRS + C_PAIRS, NB, HD)
        self.after_local = a.at
        self.xb = a.take(B_TILES, XW)
        self.xc = a.take(9, XW)
        self.square = a.take(KD, NT)
        self.free = a.at
        t = Area(self.big, 80 * NT)
        self.query = t.take(HEADS, NT)
        self.score = t.take(3, 2 * HEADS, NKEYS)
        self.cand = t.take(HEADS, TOPK * TOPK)
        self.best = t.take(2 * HEADS, TOPK)
        self.besti = t.take(2 * HEADS, TOPK, dtype=U32)
        self.bestf = t.take(2 * HEADS, TOPK)
        self.pos = t.take(HEADS * TOPK, dtype=U32)
        self.posp = t.take(HEADS * TOPK, dtype=U32)
        self.posf = t.take(HEADS * TOPK)
        self.hit = t.take(HEADS * TOPK, TOPK)

    def par(self, name):
        return self.small[:, SMALL[name][0]:SMALL[name][1]]

    def mix(self, name):
        return self.mixc[:, MIXC[name][0]:MIXC[name][1]]

    def out(self, name):
        return self.outs[:, OUTS[name][0]:OUTS[name][1]]

    def tile(self, n):
        return self.ring[:, n % RING, :].rearrange("p (k n) -> p k n", k=KD)

    def wait_tile(self, eng, n):
        eng.wait_ge(self.loaded[n % RING], 16 * (n // RING + 1))

    def wait_done(self, eng, n):
        eng.wait_ge(self.done[n % RING], n // RING + 1)


def load_tiles(eng, m, stream, l, first, end):
    for n in range(first, end):
        if n >= RING:
            m.wait_done(eng, n - RING)
        eng.dma_start(m.ring[:, n % RING, :], stream[l, n, :, :]).then_inc(m.loaded[n % RING], 16)


def load_many(eng, m, stream, l, first, end):
    turns = (end - first) // RING
    with eng.Fori(0, turns) as g:
        for j in range(RING):
            n = first + j
            eng.wait_ge(m.done[n % RING], g + n // RING)
            eng.dma_start(m.ring[:, n % RING, :], stream[l, g * RING + n, :, :]).then_inc(m.loaded[n % RING], 16)
    load_tiles(eng, m, stream, l, first + turns * RING, end)


def modulate(link, m, which, last=None):
    v, shift = link.eng, 3 * which * KD
    link(v.tensor_tensor(m.h[:, :, :], m.x[:, :, :], spread(m.rms[:, :], 1, KD), ALU.mult))
    for k in range(KD):
        link(v.tensor_scalar(m.h[:, k, 0:NP], m.h[:, k, 0:NP], m.gain[:, which, k, 0:1],
                             m.mod[:, shift + k, 0:1], ALU.mult, ALU.add))
    hs = batched(m.h[:, :, NP:NT])
    link(v.tensor_tensor(hs, hs, spread(m.gain[:, which, :, 1:], 3, NS), ALU.mult))
    v.tensor_tensor(hs, hs, spread(m.mod[:, shift:shift + KD, 1:], 3, NS), ALU.add).then_inc(last, 1)


def setup_block(nc, m, x_in, c_in, keep_in):
    with signals(nc, "in_loaded cond_ready") as s, nc.Block() as block:
        @block.sync
        def _(sp):
            sp.dma_start(m.cond[:, :, :], c_in).then_inc(s["in_loaded"], 16)
            sp.dma_start(m.keep[:, :], keep_in).then_inc(s["in_loaded"], 16)
            sp.dma_start(m.x[:, :, :], x_in).then_inc(s["in_loaded"], 16)

        @block.scalar
        def _(act):
            act.wait_ge(s["in_loaded"], 48)
            act.activation(m.cond[:, :, :], m.cond[:, :, :], ACT.Silu).then_inc(s["cond_ready"], 1)
            act.wait_ge(s["cond_ready"], 1)


def project_block(nc, m, l, stream, small_in, mixc_in, state_in):
    names = ("small_loaded mixc_loaded states_loaded squares_ready sums_ready root_ready mod_summed mod_ready "
             "h_ready step z_out pads_ready")
    with signals(nc, names) as s, nc.psum_tensor("ps_z", [P, 4, 512], F32) as ps_z, \
            nc.psum_tensor("ps_sum", [P, 512], F32) as ps_sum, nc.psum_tensor("ps_mod", [P, 512], F32) as ps_mod, \
            nc.Block() as block:
        tok_ps = ps_sum

        @block.sync
        def _(sp):
            load_tiles(sp, m, stream, l, 0, RING)
            sp.dma_start(m.small[:, :], small_in[l, :, :]).then_inc(s["small_loaded"], 16)
            sp.dma_start(m.mixc[:, :], mixc_in).then_inc(s["mixc_loaded"], 16)
            sp.dma_start(m.state0[:, :, :, :].rearrange("p a b c -> p (a b c)"), state_in[l, :, :]).then_inc(
                s["states_loaded"], 16)
            load_many(sp, m, stream, l, RING, T_OUT)
            load_tiles(sp, m, stream, l, T_OUT, T_OUT + RING - 1)
            sp.wait_ge(s["mixc_loaded"], 16)
            sp.wait_ge(s["states_loaded"], 16)

        @block.scalar
        def _(act):
            act.activation(m.square[:, :, :], m.x[:, :, :], ACT.Square).then_inc(s["squares_ready"], 1)
            act.wait_ge(s["sums_ready"], 1)
            act.activation(m.rms[:, :], ps_sum[:, 0:NT], ACT.Sqrt, bias=m.eps, scale=1.0 / D).then_inc(s["root_ready"], 1)
            for n, z in enumerate(Z_ORDER):
                m.wait_done(act, T_IN + n)
                src = ps_z[:, n % 4, 0:NT]
                if z in PLAIN_Z and z not in (4, 5):
                    ext = m.xb[:, z - 8, :] if z < 14 else m.xc[:, z - 14, :]
                    act.activation(ext[:, CONV - 1:XP], src[:, 0:NP], ACT.Copy)
                    act.activation(ext[:, XP:XW].rearrange("p (b s) -> p b s", b=NB)[:, :, CONV - 1:],
                                   src[:, NP:NT].rearrange("p (b s) -> p b s", b=NB), ACT.Copy).then_inc(s["z_out"], 1)
                else:
                    f = ACT.Silu if z in SILU_Z else ACT.Sigmoid if z in SIGM_Z else ACT.Gelu_apprx_tanh if z in GELU_Z else ACT.Copy
                    slot = z if z < 8 else z - 3 if z < 14 else z - 12
                    act.activation(m.zact[:, slot, :], src, f).then_inc(s["z_out"], 1)
            m.wait_done(act, T_BETA)
            act.activation(m.tok[:, 0:2, :], tok_ps[:, 0:4 * C_HEADS].rearrange("p (t c) -> p t c", t=2), ACT.Copy)
            act.wait_ge(s["pads_ready"], 4)
            act.activation(m.tok[0:32, 2, :], tok_ps[0:32, 4 * C_HEADS:6 * C_HEADS], ACT.Copy).then_inc(s["z_out"], 1)
            act.wait_ge(s["z_out"], IN_TILES + 1)

        @block.gpsimd
        def _(pool):
            pool.wait_ge(s["small_loaded"], 16)
            for ext, name, n in ((m.xb, "lru_conv", B_TILES), (m.xc, "dn_conv", 9)):
                pool.tensor_copy(ext[:, :, XP:XW].rearrange("p k (b s) -> p k b s", b=NB)[:, :, :, 0:CONV - 1],
                                 m.par(name).rearrange("p (k b s) -> p k b s", k=n, b=NB)).then_inc(s["pads_ready"], 1)
            pool.memset(m.xb[:, :, 0:CONV - 1], 0.0)
            pool.memset(m.xc[:, :, 0:CONV - 1], 0.0).then_inc(s["pads_ready"], 1)
            pool.memset(m.tok[:, 2, :], 0.0).then_inc(s["pads_ready"], 1)
            pool.wait_ge(s["pads_ready"], 4)

        @block.vector
        def _(v):
            link = Chain(v, s["step"])
            v.wait_ge(s["root_ready"], 1)
            link(v.reciprocal(m.rms[:, :], m.rms[:, :]))
            v.wait_ge(s["small_loaded"], 16)
            v.wait_ge(s["mod_summed"], 1)
            link(v.tensor_tensor(m.mod[:, :, :], ps_mod[:, 0:ADA_TILES * 9].rearrange("p (t c) -> p t c", c=9),
                                 spread(m.par("b_ada"), 2, 1 + NB), ALU.add))
            for w, name in ((0, "norm1"), (1, "norm2")):
                scale = m.mod[:, (3 * w + 1) * KD:(3 * w + 2) * KD, :]
                link(v.scalar_tensor_tensor(m.gain[:, w, :, :], scale, 1.0, spread(m.par(name), 2, 1 + NB),
                                            ALU.add, ALU.mult))
            modulate(link, m, 0, s["h_ready"])
            v.wait_ge(s["h_ready"], 1)

        @block.tensor
        def _(pe):
            pe.wait_ge(s["squares_ready"], 1)
            for k in range(KD):
                mm = pe.matmul(ps_sum[:, 0:NT], m.ones, m.square[:, k, :], start=(k == 0), stop=(k == KD - 1))
            mm.then_inc(s["sums_ready"], 1)
            for n in range(ADA_TILES):
                m.wait_tile(pe, n)
                w = m.tile(n)
                for k in range(KD):
                    mm = pe.matmul(ps_mod[:, 9 * n:9 * n + 9], w[:, k, :], m.cond[:, k, :], start=(k == 0), stop=(k == KD - 1))
                mm.then_inc(m.done[n % RING], 1)
                if n == ADA_TILES - 1:
                    m.wait_done(pe, n)
                    pe.sem_inc(s["mod_summed"], 1)
            pe.wait_ge(s["h_ready"], 1)
            for n in range(IN_TILES):
                t = T_IN + n
                m.wait_tile(pe, t)
                if n >= 4:
                    pe.wait_ge(s["z_out"], n - 3)
                w = m.tile(t)
                for k in range(KD):
                    mm = pe.matmul(ps_z[:, n % 4, 0:NT], w[:, k, :], m.h[:, k, :], start=(k == 0), stop=(k == KD - 1))
                mm.then_inc(m.done[t % RING], 1)
            m.wait_tile(pe, T_BETA)
            pe.wait_ge(s["root_ready"], 1)
            w = m.tile(T_BETA)
            for t, (a, b) in enumerate(((0, 128), (128, 256), (256, 288))):
                for k in range(KD):
                    mm = pe.matmul(tok_ps[0:b - a, 12 * t:12 * t + 12], m.h[:, k, a:b], w[:, k, 0:12],
                                   start=(k == 0), stop=(k == KD - 1))
            mm.then_inc(m.done[T_BETA % RING], 1)


def local_block(nc, m, l, stream):
    names = ("step act_step conv_b conv_c xb_ready gates_out soft_in soft_exp decay_ready a_ready root_in root_ready "
             "qkv_ready qk_squares qk_sums qk_root tail resets_ready outs_ready")
    with signals(nc, names) as s, nc.psum_tensor("ps_q", [P, 8, 512], F32) as ps, nc.Block() as block:
        f = Area(m.big, m.free)
        yb = f.take(B_TILES, XW)
        yc = f.take(9, XW)
        xcb = f.take(B_TILES, NT)
        rgate = f.take(B_TILES, NT)
        igate = f.take(B_TILES, NT)
        a = f.take(B_TILES, NT)
        th = f.take(B_TILES, NT)
        aext = f.take(B_TILES, SW)
        bext = f.take(B_TILES, SW)
        hext = f.take(B_TILES, SW)
        sp_in = f.take(B_TILES + 3 * C_HEADS)
        sp_w = f.take(B_TILES + 3 * C_HEADS)
        sp_s = f.take(B_TILES + 3 * C_HEADS)
        sp_z = f.take(B_TILES + 3 * C_HEADS)
        sp_p = f.take(B_TILES + 3 * C_HEADS)
        alog = f.take(C_HEADS)
        sq = f.take(6, NT)

        def ysamp(y):
            return y[:, :, XP:XW].rearrange("p k (b s) -> p k b s", b=NB)[:, :, :, 0:NS]

        @block.sync
        def _(sp):
            load_tiles(sp, m, stream, l, T_OUT + RING - 1, T_OUT + RING)

        @block.tensor
        def _(pe):
            m.wait_tile(pe, T_GATE)
            pe.wait_ge(s["xb_ready"], 2)
            w = m.ring[:, T_GATE % RING, :]
            for g in range(2):
                for t in range(B_TILES):
                    n = g * B_TILES + t
                    mm = pe.matmul(ps[:, n, 0:NT], w[:, n * P:(n + 1) * P], xcb[:, t, :], start=True, stop=True)
            mm.then_inc(m.done[T_GATE % RING], 1)
            pe.wait_ge(s["qk_squares"], 1)
            pe.wait_ge(s["gates_out"], 2)
            for n in range(6):
                mm = pe.matmul(ps[:, n, 0:NT], m.mix("block_ones"), sq[:, n, :], start=True, stop=True)
            mm.then_inc(s["qk_sums"], 1)

        @block.scalar
        def _(act):
            act.wait_ge(s["soft_in"], 1)
            act.activation(sp_w, sp_w, ACT.Exp, scale=-1.0)
            act.activation(alog, m.par("a_log"), ACT.Exp).then_inc(s["soft_exp"], 1)
            act.activation(m.beta[:, :, :], m.tok[:, :, 0:C_HEADS], ACT.Sigmoid)
            m.wait_done(act, T_GATE)
            for g, (dst, bias) in enumerate(((rgate, "ba"), (igate, "bx"))):
                for t in range(B_TILES):
                    i = act.activation(dst[:, t, :], ps[:, g * B_TILES + t, 0:NT], ACT.Sigmoid,
                                       bias=m.par(bias)[:, t:t + 1])
                i.then_inc(s["gates_out"], 1)
            act.wait_ge(s["gates_out"], 2)
            act.wait_ge(s["decay_ready"], 1)
            for t in range(B_TILES):
                act.activation(th[:, t, :], rgate[:, t, :], ACT.Tanh, scale=sp_in[:, t:t + 1])
            for t in range(B_TILES):
                i = act.activation(a[:, t, :], rgate[:, t, :], ACT.Exp, scale=sp_in[:, t:t + 1])
            i.then_inc(s["a_ready"], 1)
            act.wait_ge(s["conv_c"], 1)
            act.activation(m.qkv[:, :, 0:NP], yc[:, :, 0:NP], ACT.Silu)
            act.activation(batched(m.qkv[:, :, NP:NT]), ysamp(yc), ACT.Silu).then_inc(s["qkv_ready"], 1)
            act.wait_ge(s["qkv_ready"], 1)
            act.activation(sq[:, :, :], m.qkv[:, 0:6, :], ACT.Square).then_inc(s["qk_squares"], 1)
            act.wait_ge(s["root_in"], 1)
            act.activation(th[:, :, :], th[:, :, :], ACT.Sqrt, scale=-1.0).then_inc(s["root_ready"], 1)
            act.wait_ge(s["qk_sums"], 1)
            act.activation(sq[:, :, :], ps[:, 0:6, 0:NT], ACT.Sqrt, bias=m.eps).then_inc(s["qk_root"], 1)

        @block.gpsimd
        def _(pool):
            pool.memset(aext[:, :, 0:1], 0.0)
            pool.memset(aext[:, :, NP:SW].rearrange("p k (b s) -> p k b s", b=NB)[:, :, :, 0:1], 0.0)
            pool.tensor_copy(bext[:, :, NP:SW].rearrange("p k (b s) -> p k b s", b=NB)[:, :, :, 0],
                             m.par("lru_h").rearrange("p (k b) -> p k b", k=B_TILES)).then_inc(s["resets_ready"], 1)
            for ext, pn, sn, n in ((m.xb, "p_lc", "s_lc", B_TILES), (m.xc, "p_dc", "s_dc", 9)):
                pool.tensor_copy(m.out(pn).rearrange("p (k c) -> p k c", k=n), ext[:, :, XP - 3:XP])
                i = pool.tensor_copy(m.out(sn).rearrange("p (k b c) -> p k b c", k=n, b=NB),
                                 ext[:, :, XP:XW].rearrange("p k (b s) -> p k b s", b=NB)[:, :, :, NS:NS + 3])
            i.then_inc(s["outs_ready"], 1)
            pool.wait_ge(s["outs_ready"], 1)
            pool.wait_ge(s["resets_ready"], 1)

        @block.vector
        def _(v):
            link = Chain(v, s["step"])

            def conv(y, ext, t, w, bias=None):
                if bias is None:
                    link(v.tensor_scalar(y[:, t, 0:YW], ext[:, t, 0:YW], w[:, 4 * t:4 * t + 1], None, ALU.mult))
                else:
                    link(v.tensor_scalar(y[:, t, 0:YW], ext[:, t, 0:YW], w[:, 4 * t:4 * t + 1], bias, ALU.mult, ALU.add))
                for k in range(1, CONV):
                    link(v.scalar_tensor_tensor(y[:, t, 0:YW], ext[:, t, k:k + YW], w[:, 4 * t + k:4 * t + k + 1],
                                                y[:, t, 0:YW], ALU.mult, ALU.add))

            nsp = B_TILES
            link(v.tensor_scalar(sp_in[:, 0:nsp], m.par("lru_L"), -1.0, None, ALU.mult))
            link(v.tensor_tensor(sp_in[:, nsp:].rearrange("p (t h) -> p t h", t=3), m.tok[:, :, C_HEADS:],
                                 spread(m.par("dt_bias"), 1, 3), ALU.add))
            link(v.tensor_scalar(sp_w, sp_in, -1.0, None, ALU.mult))
            v.tensor_tensor(sp_w, sp_w, sp_in, ALU.max).then_inc(s["soft_in"], 1)
            v.wait_ge(s["soft_in"], 1)
            for t in range(B_TILES):
                conv(yb, m.xb, t, m.par("lru_w"), m.par("lru_b")[:, t:t + 1])
            v.tensor_copy(xcb[:, :, 0:NP], yb[:, :, 0:NP]).then_inc(s["xb_ready"], 1)
            v.tensor_copy(batched(xcb[:, :, NP:NT]), ysamp(yb)).then_inc(s["xb_ready"], 1)
            v.wait_ge(s["soft_exp"], 1)
            link(v.tensor_scalar(sp_z, sp_w, 2.0, None, ALU.add))
            link(v.reciprocal(sp_z, sp_z))
            link(v.tensor_tensor(sp_s, sp_w, sp_z, ALU.mult))
            link(v.tensor_tensor(sp_z, sp_s, sp_s, ALU.mult))
            link(v.tensor_scalar(sp_p, sp_z, 1.0 / 15, None, ALU.mult))
            for c in LOG1P:
                link(v.scalar_tensor_tensor(sp_p, sp_p, c, sp_z, ALU.add, ALU.mult))
            link(v.scalar_tensor_tensor(sp_p, sp_p, 1.0, sp_s, ALU.add, ALU.mult))
            link(v.tensor_scalar(sp_s, sp_in, 0.0, None, ALU.max))
            link(v.scalar_tensor_tensor(sp_in, sp_p, 2.0, sp_s, ALU.mult, ALU.add))
            link(v.scalar_tensor_tensor(m.decay[:, :, :], sp_in[:, nsp:].rearrange("p (t h) -> p t h", t=3), -1.0,
                                        spread(alog, 1, 3), ALU.mult, ALU.mult))
            v.tensor_scalar(sp_in[:, 0:nsp], sp_in[:, 0:nsp], -8.0, None, ALU.mult).then_inc(s["decay_ready"], 1)
            for t in range(9):
                conv(yc, m.xc, t, m.par("dn_w"))
            v.sem_inc(s["conv_c"], 1)
            v.wait_ge(s["a_ready"], 1)
            v.wait_ge(s["resets_ready"], 1)
            link(v.tensor_tensor(xcb[:, :, :], xcb[:, :, :], igate[:, :, :], ALU.mult))
            link(v.tensor_tensor(igate[:, :, :], a[:, :, :], a[:, :, :], ALU.mult))
            v.scalar_tensor_tensor(th[:, :, :], igate[:, :, :], 1.0, th[:, :, :], ALU.add, ALU.mult).then_inc(s["root_in"], 1)
            link(v.tensor_copy(aext[:, :, 1:NP], a[:, :, 1:NP]))
            link(v.tensor_copy(aext[:, :, NP:SW].rearrange("p k (b s) -> p k b s", b=NB)[:, :, :, 1:], batched(a[:, :, NP:NT])))
            v.wait_ge(s["root_ready"], 1)
            link(v.tensor_tensor(bext[:, :, 0:NP], th[:, :, 0:NP], xcb[:, :, 0:NP], ALU.mult))
            link(v.tensor_tensor(bext[:, :, NP:SW].rearrange("p k (b s) -> p k b s", b=NB)[:, :, :, 1:],
                                 batched(th[:, :, NP:NT]), batched(xcb[:, :, NP:NT]), ALU.mult))
            link(v.tensor_tensor_scan(flat(hext), flat(aext), flat(bext), 0.0, ALU.mult, ALU.add))
            hs = hext[:, :, NP:SW].rearrange("p k (b s) -> p k b s", b=NB)
            link(v.tensor_tensor(m.mixed[:, 2:5, 0:NP], hext[:, :, 0:NP], m.zact[:, 8:11, 0:NP], ALU.mult))
            link(v.tensor_tensor(batched(m.mixed[:, 2:5, NP:NT]), hs[:, :, :, 1:], batched(m.zact[:, 8:11, NP:NT]), ALU.mult))
            link(v.tensor_copy(m.out("p_h"), hext[:, :, NP - 1]))
            link(v.tensor_copy(m.out("s_h").rearrange("p (k b) -> p k b", k=B_TILES), hs[:, :, :, NS]))
            v.wait_ge(s["qk_root"], 1)
            link(v.reciprocal(sq[:, :, :], sq[:, :, :]))
            link(v.scalar_tensor_tensor(flat(m.qkv[:, 0:3, :]), flat(m.qkv[:, 0:3, :]), HD ** -0.5, flat(sq[:, 0:3, :]),
                                        ALU.mult, ALU.mult))
            link(v.tensor_tensor(m.qkv[:, 3:6, :], m.qkv[:, 3:6, :], sq[:, 3:6, :], ALU.mult))


def hgrn_block(nc, m, l):
    names = "step act_step sel_ready v_ready f_ready kv_ready scan_ready qs_ready spread_ready out_ready zero_ready lb_ready lb_out states_out pair_summed"
    STEP = 2
    with signals(nc, names) as s, nc.psum_tensor("ps_v", [P, 2, STEP, 512], F32) as ps_v, \
            nc.psum_tensor("ps_o", [P, 2, 512], F32) as ps_o, nc.Block() as block:
        f = Area(m.big, m.free)
        fext = f.take(A_PAIRS, STEP, SW)
        kext = f.take(A_PAIRS, SW)
        vext = f.take(A_PAIRS, SW)
        qext = f.take(A_PAIRS, SW)
        kv = f.take(2, STEP, SW)
        scan = f.take(2, STEP, SW)
        qs = f.take(2, STEP, SW)
        pick = f.take(2, STEP, P)
        place = f.take(2, STEP, P)
        lb = f.take(A_PAIRS)
        omlb = f.take(A_PAIRS)
        zero = f.take(P)
        fcol = f.take(A_PAIRS, NT)

        def samples(ap):
            return ap[:, NP:SW].rearrange("p (b s) -> p b s", b=NB)

        def toks(ap):
            return ap[:, NP:NT].rearrange("p (b s) -> p b s", b=NB)

        head_rows = m.ident.rearrange("p (h v) -> p h v", h=2)
        window = m.mix("window").rearrange("p (h c) -> p h c", h=2)

        @block.scalar
        def _(act):
            act.wait_ge(s["lb_ready"], 1)
            act.activation(lb, lb, ACT.Sigmoid).then_inc(s["lb_out"], 1)
            act.sem_inc(s["states_out"], 2)
            for pair in range(A_PAIRS):
                with act.Fori(0, HD // STEP // 2) as i:
                    for half in range(2):
                        n = i * 2 + half + pair * (HD // STEP)
                        v0 = i * (2 * STEP) + half * STEP
                        act.wait_ge(s["out_ready"], n + 1)
                        for j in range(STEP):
                            act.activation(pick[:, half, j, :].rearrange("p (h k) -> p h k", h=2),
                                           head_rows[:, :, ds(v0 + j, 1)].broadcast_to([P, 2, HD]), ACT.Copy)
                            c = act.activation(place[:, half, j, :].rearrange("p (h k) -> p h k", h=2),
                                               window[:, :, ds(v0 * -1 + (63 - j), HD)], ACT.Copy)
                        c.then_inc(s["sel_ready"], 1)
                        act.wait_ge(s["scan_ready"], n + 3)
                        act.activation(m.states[:, pair, 0, ds(v0, STEP)], scan[:, half, :, NP - 1], ACT.Copy)
                        act.activation(m.states[:, pair, 1:, ds(v0, STEP)].rearrange("p b v -> p v b"),
                                       scan[:, half, :, NP:SW].rearrange("p v (b s) -> p v b s", b=NB)[:, :, :, NS],
                                       ACT.Copy).then_inc(s["states_out"], 1)

        @block.gpsimd
        def _(pool):
            pool.sem_inc(s["qs_ready"], 2)
            for pair in range(A_PAIRS):
                pool.wait_ge(s["f_ready"], pair + 1)
                with pool.Fori(0, HD // STEP // 2) as i:
                    for half in range(2):
                        n = i * 2 + half + pair * (HD // STEP)
                        pool.wait_ge(s["scan_ready"], n + 3)
                        pool.wait_ge(s["out_ready"], n + 1)
                        pool.tensor_tensor(qs[:, half, :, :], scan[:, half, :, :], spread(qext[:, pair, :], 1, STEP),
                                           ALU.mult).then_inc(s["qs_ready"], 1)

        @block.vector
        def _(v):
            link = Chain(v, s["step"])
            link(v.memset(zero, 0.0))
            v.sem_inc(s["zero_ready"], 1)
            v.tensor_tensor(lb, m.par("lb")[:, A_PAIRS:2 * A_PAIRS], m.par("lb")[:, 0:A_PAIRS], ALU.subtract).then_inc(
                s["lb_ready"], 1)
            v.wait_ge(s["lb_out"], 1)
            dlb = m.par("lb_on")
            link(v.tensor_scalar(lb, lb, dlb, None, ALU.mult))
            link(v.tensor_scalar(omlb, lb, -1.0, 1.0, ALU.mult, ALU.add))
            for pair in range(A_PAIRS):
                col = fcol[:, pair, :]
                link(v.tensor_scalar(col, m.zact[:, 2 + pair, :], omlb[:, pair:pair + 1], lb[:, pair:pair + 1],
                                     ALU.mult, ALU.add))
                for c, src in ((fext[:, pair, 0, :], col), (vext[:, pair, :], m.zact[:, 4 + pair, :]),
                               (qext[:, pair, :], m.zact[:, pair, :])):
                    k = HD ** -0.5 if src is not col and c.offset == qext[:, pair, :].offset else 1.0
                    link(v.memset(samples(c)[:, :, 0:1], 0.0))
                    link(v.tensor_scalar(c[:, 0:NP], src[:, 0:NP], k, None, ALU.mult))
                    link(v.tensor_scalar(samples(c)[:, :, 1:], toks(src), k, None, ALU.mult))
                link(v.tensor_scalar(kext[:, pair, :], fext[:, pair, 0, :], -1.0, 1.0, ALU.mult, ALU.add))
                link(v.memset(fext[:, pair, 0, 0:1], 0.0))
                link(v.tensor_copy(fext[:, pair, 1, :], fext[:, pair, 0, :]))
                v.sem_inc(s["f_ready"], 1)
            v.sem_inc(s["kv_ready"], 2)
            v.sem_inc(s["scan_ready"], 2)
            for pair in range(A_PAIRS):
                with v.Fori(0, HD // STEP // 2) as i:
                    for half in range(2):
                        n = i * 2 + half + pair * (HD // STEP)
                        v.wait_ge(s["spread_ready"], n + 1)
                        v.wait_ge(s["scan_ready"], n + 1)
                        v.tensor_tensor(kv[:, half, :, :], ps_v[:, half, :, 0:SW], spread(kext[:, pair, :], 1, STEP),
                                        ALU.mult).then_inc(s["kv_ready"], 1)
                        v.wait_ge(s["kv_ready"], n + 3)
                        v.wait_ge(s["qs_ready"], n + 1)
                        v.wait_ge(s["states_out"], n + 1)
                        v.tensor_tensor_scan(flat(scan[:, half, :, :]), flat(fext[:, pair, :, :]), flat(kv[:, half, :, :]),
                                             0.0, ALU.mult, ALU.add).then_inc(s["scan_ready"], 1)
            v.wait_ge(s["pair_summed"], A_PAIRS)
            for pair in range(A_PAIRS):
                o = ps_o[:, pair, 0:SW]
                link(v.tensor_copy(m.mixed[:, pair, 0:NP], o[:, 0:NP]))
                link(v.tensor_copy(toks(m.mixed[:, pair, :]), samples(o)[:, :, 1:]))

        @block.tensor
        def _(pe):
            pe.wait_ge(s["zero_ready"], 1)
            pe.sem_inc(s["out_ready"], 2)
            for pair in range(A_PAIRS):
                pe.wait_ge(s["f_ready"], pair + 1)
                pe.matmul(ps_o[:, pair, 0:SW], zero, vext[:, pair, :], start=True, stop=False)

                def spread_v(i, half):
                    n = i * 2 + half + pair * (HD // STEP)
                    v0 = i * (2 * STEP) + half * STEP
                    pe.wait_ge(s["sel_ready"], n + 1)
                    pe.wait_ge(s["kv_ready"], n + 1)
                    for j in range(STEP):
                        pe.matmul(ps_v[:, half, j, 0:SW], pick[:, half, j, :], vext[:, pair, :], start=True, stop=False)
                        mm = pe.matmul(ps_v[:, half, j, NP:SW:SS], m.ident, m.state0[:, pair, :, ds(v0 + j, 1)].squeeze(2),
                                       start=False, stop=True)
                    mm.then_inc(s["spread_ready"], 1)

                def sum_k(i, half):
                    n = i * 2 + half + pair * (HD // STEP)
                    pe.wait_ge(s["qs_ready"], n + 3)
                    for j in range(STEP):
                        mm = pe.matmul(ps_o[:, pair, 0:SW], place[:, half, j, :], qs[:, half, j, :], start=False, stop=False)
                    mm.then_inc(s["out_ready"], 1)

                with pe.Fori(0, HD // STEP // 2) as i:
                    spread_v(i, 0)
                    spread_v(i, 1)
                    sum_k(i, 0)
                    sum_k(i, 1)
                pe.matmul(ps_o[:, pair, 0:SW], zero, vext[:, pair, :], start=False, stop=True).then_inc(s["pair_summed"], 1)


def flat(ap):
    return ap.rearrange("p a b -> p (a b)")


def delta_block(nc, m, l):
    GROUPS = ((0, P, 0), (P, P, 1), (NP, NB * NS, 2))
    names = ("step act_step ps_a ps_b ps_c ps_d gcol_out eg_ready kb_ready raw_ready pair_free x_ready x_out tu_ready "
             "tu_done kd_ps kd_out r_ps r_out e_ps e_out o_ps s_ps s_out a_free em_ready dt_ready dte_ready gp_ready "
             "glast_ready glast_exp scaled masked kd_mul r_sum nk_masked")
    H = C_HEADS
    with signals(nc, names) as s, nc.psum_tensor("ps_1", [P, 1024], F32) as ps1, \
            nc.psum_tensor("ps_2", [P, 1024], F32) as ps2, nc.psum_tensor("ps_3", [P, 1024], F32) as ps3, \
            nc.psum_tensor("ps_4", [P, 1024], F32) as ps4, nc.Block() as block:
        f = Area(m.big, m.after_local)

        def by_group(tiles):
            return [f.take(tiles, n) for _, n, _ in GROUPS]

        gcol = f.take(3, H)
        dt = f.take(H, P)
        gp = f.take(C_PAIRS, P)
        eg = by_group(C_PAIRS)
        gl = f.take(C_PAIRS, P)
        kb = f.take(C_PAIRS, P)
        vb = by_group(C_PAIRS)
        nke = by_group(C_PAIRS)
        qe = by_group(C_PAIRS)
        kd = by_group(C_PAIRS)
        ntm = by_group(H)
        ptm = by_group(H)
        tm = by_group(H)
        um = by_group(H)
        emb = Area(m.big, f.at).take(H, NB, HD)
        xm = f.take(2, H, P)
        cm = f.take(2, H, P)
        kdt = f.take(3, H, HD)
        rm = f.take(H, HD)
        em = f.take(H, HD)
        nkm = f.take(C_PAIRS, NB, NB * NS)
        state = f.take(C_PAIRS, HD)

        def head(ap, h, n):
            r = (h % 2) * HD
            return ap[r:r + HD, h // 2, 0:n]

        def at(ap, h, width, n):
            c = (h % 2) * 512 + (h // 2) * width
            return ap[:, c:c + n]

        def heads(ap, width, n):
            return ap.rearrange("p (r q c) -> p q r c", r=2, c=width)[:, 0:C_PAIRS, :, 0:n]

        def by_pair(ap):
            return ap.rearrange("p (q r) c -> p q r c", r=2)

        def half(ap, r, n):
            return ap.rearrange("p (r q c) -> p r q c", r=2, c=P)[r * HD:(r + 1) * HD, r, 0:C_PAIRS, 0:n]

        def levels(n):
            return 7 if n == P else 2

        @block.tensor
        def _(pe):
            for g, (t0, n, tt) in enumerate(GROUPS):
                tri = m.mix("tri") if n == P else m.mix("tri_s")
                if g:
                    pe.wait_ge(s["gp_ready"], g)
                    pe.wait_ge(s["kb_ready"], g)
                    pe.wait_ge(s["masked"], g)
                for h in range(H):
                    pe.matmul(at(ps1, h, P, n), m.decay[0:n, tt, h:h + 1].broadcast_to([n, P]), tri[0:n, 0:n],
                              start=True, stop=True)
                pe.matmul(ps3[0:n, 0:H], tri[0:n, 0:n], m.decay[0:n, tt, :], start=True, stop=True)
                for h in range(H):
                    mm = pe.matmul(at(ps2, h, P, n), m.beta[0:n, tt, h:h + 1].broadcast_to([n, P]),
                                   m.ident[0:n, 0:n], start=True, stop=True)
                mm.then_inc(s["ps_a"], 1)
                pe.wait_ge(s["kb_ready"], g + 1)
                pe.wait_ge(s["gcol_out"], g + 1)
                for h in range(H):
                    k = head(m.qkv[:, 3:6, t0:t0 + n], h, n)
                    pe.matmul(at(ps3, h, P, n)[0:n], k, head(kb, h, n), start=True, stop=True)
                    mm = pe.matmul(at(ps4, h, P, n)[0:n], k, head(m.qkv[:, 0:3, t0:t0 + n], h, n), start=True, stop=True)
                mm.then_inc(s["raw_ready"], 1)
            pe.wait_ge(s["masked"], 3)
            turn = 0
            last_turn = [None, None]
            for g0 in ((0, 1), (2,)):
                for lv in range(levels(GROUPS[g0[0]][1])):
                    for b, g in enumerate(g0):
                        n = GROUPS[g][1]
                        px, pt = (ps1, ps2) if b == 0 else (ps3, ps4)
                        pe.wait_ge(s["scaled"], turn + 1)
                        if last_turn[b] is not None:
                            pe.wait_ge(s["tu_done"], last_turn[b] + 1)
                        last_turn[b] = turn
                        for h in range(H):
                            mm = pe.matmul(at(px, h, P, n)[0:n], cm[0:n, b, h, 0:n], tm[g][0:n, h, 0:n], start=True, stop=True)
                        mm.then_inc(s["x_ready"], 1)
                        pe.wait_ge(s["x_out"], turn + 1)
                        for h in range(H):
                            pe.matmul(at(pt, h, P, n)[0:n], um[g][0:n, h, 0:n], xm[0:n, b, h, 0:n], start=True, stop=True)
                            mm = pe.matmul(at(px, h, P, n)[0:n], xm[0:n, b, h, 0:n], um[g][0:n, h, 0:n], start=True, stop=True)
                        mm.then_inc(s["tu_ready"], 1)
                        turn += 1
            for g, (t0, n, tt) in enumerate(GROUPS):
                pe.wait_ge(s["tu_done"], turn)
                if g:
                    pe.wait_ge(s["kd_out"], g)
                for h in range(H):
                    r = (h % 2) * HD
                    mm = pe.matmul(at(ps1, h, HD, HD)[0:n], head(kd[g][:, :, :], h, n), m.ident[r:r + HD, r:r + HD],
                                   start=True, stop=True)
                mm.then_inc(s["kd_ps"], 1)
            pe.wait_ge(s["nk_masked"], 1)
            for g, (t0, n, tt) in enumerate(GROUPS):
                if g == 0:
                    pe.wait_ge(s["kd_out"], 3)
                pe.wait_ge(s["s_out"], g + 1)
                for h in range(H):
                    r = (h % 2) * HD
                    out = at(ps2, h, HD, HD)[0:n]
                    pe.matmul(out, head(vb[g][:, :, :], h, n), m.ident[r:r + HD, r:r + HD], start=True, stop=False)
                    if n == P:
                        mm = pe.matmul(out, head(nke[g][:, :, :], h, n), state[r:r + HD, h // 2, :], start=False, stop=True)
                    else:
                        for b in range(NB):
                            mm = pe.matmul(out, nkm[r:r + HD, h // 2, b, :], m.state0[r:r + HD, A_PAIRS + h // 2, b, :],
                                           start=False, stop=(b == NB - 1))
                mm.then_inc(s["r_ps"], 1)
                pe.wait_ge(s["r_out"], g + 1)
                for h in range(H):
                    mm = pe.matmul(at(ps3, h, HD, HD)[0:n], um[g][0:n, h, 0:n], rm[0:n, h, :], start=True, stop=True)
                mm.then_inc(s["e_ps"], 1)
                pe.wait_ge(s["e_out"], g + 1)
                if g:
                    pe.wait_ge(s["act_step"], g)
                for h in range(H):
                    r = (h % 2) * HD
                    out = ps4[r:r + HD, (h // 2) * P:(h // 2) * P + n]
                    pe.matmul(out, em[0:n, h, :], ptm[g][0:n, h, 0:n], start=True, stop=False)
                    if n == P:
                        mm = pe.matmul(out, state[r:r + HD, h // 2, :], head(qe[g][:, :, :], h, n), start=False, stop=True)
                    else:
                        for b in range(NB):
                            mm = pe.matmul(out[:, NS * b:NS * b + NS], m.state0[r:r + HD, A_PAIRS + h // 2, b, :],
                                           head(qe[g][:, :, :], h, n)[:, NS * b:NS * b + NS], start=False, stop=(b == NB - 1))
                mm.then_inc(s["o_ps"], 1)
                if n == P:
                    for h in range(H):
                        r = (h % 2) * HD
                        mm = pe.matmul(ps1[r:r + HD, (h // 2) * HD:(h // 2 + 1) * HD], kdt[0:n, g, h, :], em[0:n, h, :],
                                       start=True, stop=True)
                    mm.then_inc(s["s_ps"], 1)
                else:
                    pe.wait_ge(s["em_ready"], 1)
                    for h in range(H):
                        r = (h % 2) * HD
                        bank = (ps1[:, 0:512], ps1[:, 512:1024], ps2[:, 0:512])[h // 2]
                        mm = pe.matmul(bank[r:r + HD, :], kdt[0:n, g, h, :], emb[0:n, h, :, :], start=True, stop=True)
                    mm.then_inc(s["s_ps"], 1)

        @block.scalar
        def _(act):
            for g, (t0, n, tt) in enumerate(GROUPS):
                act.wait_ge(s["ps_a"], g + 1)
                for r in range(2):
                    i = act.activation(gp[r * HD:(r + 1) * HD, :, 0:n], half(ps1, r, n), ACT.Copy)
                i.then_inc(s["gp_ready"], 1)
                act.wait_ge(s["gp_ready"], g + 1)
                act.activation(eg[g][:, :, 0:n], gp[:, :, 0:n], ACT.Exp).then_inc(s["eg_ready"], 1)
                act.wait_ge(s["dt_ready"], g + 1)
                act.activation(dt[0:n, :, 0:n], dt[0:n, :, 0:n], ACT.Exp).then_inc(s["dte_ready"], 1)
                act.wait_ge(s["glast_ready"], g + 1)
                act.activation(gl[:, :, 0:n], gl[:, :, 0:n], ACT.Exp).then_inc(s["glast_exp"], 1)
                act.wait_ge(s["kd_mul"], g + 1)
            turn = 0
            for g0 in ((0, 1), (2,)):
                for lv in range(levels(GROUPS[g0[0]][1])):
                    for b, g in enumerate(g0):
                        n = GROUPS[g][1]
                        px = ps1 if b == 0 else ps3
                        act.wait_ge(s["x_ready"], turn + 1)
                        act.activation(by_pair(xm[0:n, b, :, 0:n]), heads(px, P, n)[0:n], ACT.Copy).then_inc(s["x_out"], 1)
                        turn += 1
            for g, (t0, n, tt) in enumerate(GROUPS):
                act.wait_ge(s["kd_ps"], g + 1)
                act.activation(by_pair(kdt[0:n, g, :, :]), heads(ps1, HD, HD)[0:n], ACT.Copy).then_inc(s["kd_out"], 1)
            for g, (t0, n, tt) in enumerate(GROUPS):
                act.wait_ge(s["r_ps"], g + 1)
                act.activation(by_pair(rm[0:n, :, :]), heads(ps2, HD, HD)[0:n], ACT.Copy).then_inc(s["r_out"], 1)
                act.wait_ge(s["e_ps"], g + 1)
                if g:
                    act.wait_ge(s["s_ps"], g)
                act.activation(by_pair(em[0:n, :, :]), heads(ps3, HD, HD)[0:n], ACT.Copy).then_inc(s["e_out"], 1)
                act.wait_ge(s["o_ps"], g + 1)
                i = act.activation(m.mixed[:, 5:8, t0:t0 + n],
                                   ps4[:, 0:3 * P].rearrange("p (q c) -> p q c", q=3)[:, :, 0:n], ACT.Copy)
                i.then_inc(s["act_step"], 1)
                act.wait_ge(s["act_step"], g + 1)

        @block.vector
        def _(v):
            link = Chain(v, s["step"])
            for g, (t0, n, tt) in enumerate(GROUPS):
                neg = m.mix("neg") if n == P else m.mix("neg_s")
                last = n - 1
                v.wait_ge(s["ps_a"], g + 1)
                v.tensor_copy(gcol[0:n, g, :], ps3[0:n, 0:H]).then_inc(s["gcol_out"], 1)
                v.wait_ge(s["gcol_out"], g + 1)
                v.wait_ge(s["gp_ready"], g + 1)
                for h in range(H):
                    i = v.scalar_tensor_tensor(dt[0:n, h, 0:n], at(ps1, h, P, n)[0:n], gcol[0:n, g, h:h + 1],
                                               neg[0:n, 0:n], ALU.subtract, ALU.add)
                i.then_inc(s["dt_ready"], 1)
                for r in range(2):
                    rows = slice(r * HD, (r + 1) * HD)
                    link(v.tensor_tensor(kb[rows, :, 0:n], m.qkv[rows, 3:6, t0:t0 + n], half(ps2, r, n), ALU.mult))
                    link(v.tensor_tensor(vb[g][rows, :, 0:n], m.qkv[rows, 6:9, t0:t0 + n], half(ps2, r, n), ALU.mult))
                v.sem_inc(s["kb_ready"], 1)
                v.wait_ge(s["gp_ready"], g + 1)
                if n == P:
                    link(v.tensor_tensor(gl[:, :, 0:n], gp[:, :, last:n].broadcast_to([P, C_PAIRS, n]), gp[:, :, 0:n], ALU.subtract))
                else:
                    for q in range(C_PAIRS):
                        a = gp[:, q, 0:n].rearrange("p (b s) -> p b s", b=NB)
                        link(v.tensor_tensor(gl[:, q, 0:n].rearrange("p (b s) -> p b s", b=NB),
                                             a[:, :, NS - 1:NS].broadcast_to([P, NB, NS]), a, ALU.subtract))
                v.sem_inc(s["glast_ready"], 1)
                v.wait_ge(s["eg_ready"], g + 1)
                for q in range(C_PAIRS):
                    link(v.scalar_tensor_tensor(nke[g][:, q, 0:n], kb[:, q, 0:n], -1.0, eg[g][:, q, 0:n], ALU.mult, ALU.mult))
                link(v.tensor_tensor(qe[g][:, :, 0:n], m.qkv[:, 0:3, t0:t0 + n], eg[g][:, :, 0:n], ALU.mult))
                v.wait_ge(s["glast_exp"], g + 1)
                v.tensor_tensor(kd[g][:, :, 0:n], m.qkv[:, 3:6, t0:t0 + n], gl[:, :, 0:n], ALU.mult).then_inc(s["kd_mul"], 1)
                v.wait_ge(s["raw_ready"], g + 1)
                v.wait_ge(s["dte_ready"], g + 1)
                link(v.tensor_tensor(by_pair(ntm[g][0:n, :, 0:n]), heads(ps3, P, n)[0:n], by_pair(dt[0:n, :, 0:n]), ALU.mult))
                link(v.tensor_tensor(by_pair(ptm[g][0:n, :, 0:n]), heads(ps4, P, n)[0:n], by_pair(dt[0:n, :, 0:n]), ALU.mult))
                link(v.tensor_copy(tm[g][0:n, :, 0:n], spread(m.ident[0:n, 0:n], 1, H)))
                link(v.tensor_copy(um[g][0:n, :, 0:n], spread(m.ident[0:n, 0:n], 1, H)))
                v.sem_inc(s["masked"], 1)
            turn = 0
            order = []
            for g0 in ((0, 1), (2,)):
                for lv in range(levels(GROUPS[g0[0]][1])):
                    for b, g in enumerate(g0):
                        order.append((lv, b, g))

            def mask(turn):
                lv, b, g = order[turn]
                n = GROUPS[g][1]
                if turn >= 2:
                    v.wait_ge(s["x_ready"], turn - 1 if order[turn - 1][1] != b else turn)
                link(v.tensor_tensor(cm[0:n, b, :, 0:n], ntm[g][0:n, :, 0:n],
                                     spread(m.mix("levels")[0:n, lv * P:lv * P + n], 1, H), ALU.mult))
                v.sem_inc(s["scaled"], 1)

            mask(0)
            mask(1)
            for turn, (lv, b, g) in enumerate(order):
                n = GROUPS[g][1]
                px, pt = (ps1, ps2) if b == 0 else (ps3, ps4)
                v.wait_ge(s["tu_ready"], turn + 1)
                link(v.tensor_tensor(by_pair(tm[g][0:n, :, 0:n]), by_pair(tm[g][0:n, :, 0:n]), heads(pt, P, n)[0:n], ALU.subtract))
                link(v.tensor_tensor(by_pair(um[g][0:n, :, 0:n]), by_pair(um[g][0:n, :, 0:n]), heads(px, P, n)[0:n], ALU.subtract))
                v.sem_inc(s["tu_done"], 1)
                if turn + 2 < len(order):
                    mask(turn + 2)
            for q in range(C_PAIRS):
                link(v.tensor_tensor(nkm[:, q, :, :], spread(nke[2][:, q, 0:NB * NS], 1, NB),
                                     m.mix("batch_cols").rearrange("p (b t) -> p b t", b=NB), ALU.mult))
            v.sem_inc(s["nk_masked"], 1)
            link(v.memset(state[:, :, :], 0.0))
            v.sem_inc(s["s_out"], 1)
            for g, (t0, n, tt) in enumerate(GROUPS):
                if n == P:
                    v.wait_ge(s["s_ps"], g + 1)
                    for q in range(C_PAIRS):
                        link(v.scalar_tensor_tensor(state[:, q, :], state[:, q, :], eg[g][:, q, n - 1:n],
                                                    ps1[:, q * HD:(q + 1) * HD], ALU.mult, ALU.add))
                    if g == 1:
                        link(v.tensor_copy(m.states[:, A_PAIRS:, 0, :], state[:, :, :]))
                    v.sem_inc(s["s_out"], 1)
                else:
                    v.wait_ge(s["e_out"], g + 1)
                    for h in range(H):
                        link(v.tensor_tensor(emb[0:n, h, :, :], spread(em[0:n, h, :], 1, NB),
                                             spread(m.mix("batch_rows")[0:n, :], 2, HD), ALU.mult))
                    v.sem_inc(s["em_ready"], 1)
                    v.wait_ge(s["s_ps"], g + 1)
                    for q in range(C_PAIRS):
                        bank = (ps1[:, 0:512], ps1[:, 512:1024], ps2[:, 0:512])[q].rearrange("p (b v) -> p b v", b=NB)
                        last = eg[g][:, q, 0:n].rearrange("p (b s) -> p b s", b=NB)[:, :, NS - 1:NS].broadcast_to([P, NB, HD])
                        new = m.states[:, A_PAIRS + q, 1:, :]
                        link(v.tensor_tensor(new, m.state0[:, A_PAIRS + q, :, :], last, ALU.mult))
                        link(v.tensor_tensor(new, new, bank, ALU.add))


def residual(link, m, which, psum, tmp):
    v, gate = link.eng, (3 * which + 2) * KD
    for k in range(KD):
        link(v.scalar_tensor_tensor(m.x[:, k, 0:NP], psum[:, k, 0:NP], m.mod[:, gate + k, 0:1], m.x[:, k, 0:NP],
                                    ALU.mult, ALU.add))
    link(v.tensor_tensor(batched(tmp), batched(psum[:, :, NP:NT]), spread(m.mod[:, gate:gate + KD, 1:], 3, NS), ALU.mult))
    link(v.tensor_tensor(m.x[:, :, NP:NT], m.x[:, :, NP:NT], tmp, ALU.add))


def output_block(nc, m, l, stream, small_out, state_out):
    names = ("step squares_ready sums_ready root_ready normed summed x_ready squares2 sums2 root2 h_ready query_out "
             "outs_saved states_saved")
    tiles = (0, 1, 5, 6, 7)
    with signals(nc, names) as s, nc.psum_tensor("ps_w", [P, 8, 512], F32) as ps, nc.Block() as block:
        f = Area(m.big, m.free)
        sq = f.take(5, NT)
        tmp = f.take(KD, NB * NS)

        @block.sync
        def _(sp):
            sp.dma_start(small_out[l, :, :], m.outs[:, :]).then_inc(s["outs_saved"], 16)
            sp.dma_start(state_out[l, :, :], m.states.rearrange("p a b c -> p (a b c)")).then_inc(s["states_saved"], 16)
            load_tiles(sp, m, stream, l, T_OUT + RING, T_U + RING)
            sp.wait_ge(s["outs_saved"], 16)
            sp.wait_ge(s["states_saved"], 16)

        @block.scalar
        def _(act):
            act.activation(sq[:, 0:2, :], m.mixed[:, 0:2, :], ACT.Square)
            act.activation(sq[:, 2:5, :], m.mixed[:, 5:8, :], ACT.Square).then_inc(s["squares_ready"], 1)
            act.wait_ge(s["sums_ready"], 1)
            act.activation(sq[:, :, :], ps[:, 0:5, 0:NT], ACT.Sqrt, bias=m.eps, scale=1.0 / HD).then_inc(s["root_ready"], 1)
            act.wait_ge(s["x_ready"], 1)
            act.activation(m.square[:, :, :], m.x[:, :, :], ACT.Square).then_inc(s["squares2"], 1)
            act.wait_ge(s["sums2"], 1)
            act.activation(m.rms[:, :], ps[:, 0, 0:NT], ACT.Sqrt, bias=m.eps, scale=1.0 / D).then_inc(s["root2"], 1)
            for h in range(HEADS):
                m.wait_done(act, T_QUERY + h)
                act.activation(m.query[:, h, :], ps[:, (h + 1) % 8, 0:NT], ACT.Copy).then_inc(s["query_out"], 1)
            act.wait_ge(s["query_out"], HEADS)

        @block.vector
        def _(v):
            link = Chain(v, s["step"])
            v.wait_ge(s["root_ready"], 1)
            link(v.reciprocal(sq[:, :, :], sq[:, :, :]))
            for n, t in enumerate(tiles):
                g = m.par("a_norm") if t < 2 else m.par("dn_norm")
                gate = m.zact[:, 6 + t, :] if t < 2 else m.zact[:, 11 + t - 5, :]
                link(v.scalar_tensor_tensor(m.mixed[:, t, :], m.mixed[:, t, :], g, sq[:, n, :], ALU.mult, ALU.mult))
                link(v.tensor_tensor(m.mixed[:, t, :], m.mixed[:, t, :], gate, ALU.mult))
            v.sem_inc(s["normed"], 1)
            m.wait_done(v, T_QUERY - 4)
            m.wait_done(v, T_QUERY - 3)
            m.wait_done(v, T_QUERY - 2)
            m.wait_done(v, T_QUERY - 1)
            residual(link, m, 0, ps, tmp)
            v.sem_inc(s["x_ready"], 1)
            v.wait_ge(s["root2"], 1)
            link(v.reciprocal(m.rms[:, :], m.rms[:, :]))
            modulate(link, m, 1, s["h_ready"])
            v.wait_ge(s["h_ready"], 1)

        @block.tensor
        def _(pe):
            pe.wait_ge(s["squares_ready"], 1)
            for n in range(5):
                mm = pe.matmul(ps[:, n, 0:NT], m.mix("block_ones"), sq[:, n, :], start=True, stop=True)
            mm.then_inc(s["sums_ready"], 1)
            pe.wait_ge(s["normed"], 1)
            for n in range(KD):
                m.wait_tile(pe, T_OUT + n)
                w = m.tile(T_OUT + n)
                for k in range(KD):
                    mm = pe.matmul(ps[:, n, 0:NT], w[:, k, :], m.mixed[:, k, :], start=(k == 0), stop=(k == KD - 1))
                mm.then_inc(m.done[(T_OUT + n) % RING], 1)
            pe.wait_ge(s["squares2"], 1)
            for k in range(KD):
                mm = pe.matmul(ps[:, 0, 0:NT], m.ones, m.square[:, k, :], start=(k == 0), stop=(k == KD - 1))
            mm.then_inc(s["sums2"], 1)
            pe.wait_ge(s["h_ready"], 1)
            for h in range(HEADS):
                m.wait_tile(pe, T_QUERY + h)
                w = m.tile(T_QUERY + h)
                for k in range(KD):
                    mm = pe.matmul(ps[:, (h + 1) % 8, 0:NT], w[:, k, :], m.h[:, k, :], start=(k == 0), stop=(k == KD - 1))
                mm.then_inc(m.done[(T_QUERY + h) % RING], 1)


def experts_block(nc, m, l, stream):
    TT = 96
    HALF = (T_V - T_U) // RING * 5 // 8
    names = "step score_ps score_out found act_out"
    with signals(nc, names) as s, nc.psum_tensor("ps_s", [P, 2048], F32) as ps_s, \
            nc.psum_tensor("ps_u", [P, 4, 512], F32) as ps_u, nc.Block() as block:

        @block.sync
        def _(sp):
            load_many(sp, m, stream, l, T_U + RING, T_V + RING)

        @block.tensor
        def _(pe):
            for tt in range(3):
                if tt:
                    pe.wait_ge(s["score_out"], tt)
                for h in range(HEADS):
                    for side in range(2):
                        r, c = side * 64, (side * HEADS + h) * NKEYS
                        mm = pe.matmul(ps_s[0:TT, c:c + NKEYS], m.query[r:r + 64, h, tt * TT:(tt + 1) * TT],
                                       m.par("keys")[r:r + 64, :], start=True, stop=True)
                mm.then_inc(s["score_ps"], 1)
            with pe.Fori(0, NKEYS // RING) as g:
                for j in range(RING):
                    t = T_U + j
                    pe.wait_ge(m.loaded[t % RING], g * 16 + 16 * (t // RING + 1))
                    pe.wait_ge(s["act_out"], g * RING + (j + 1))
                    w = m.tile(t)
                    for k in range(KD):
                        mm = pe.matmul(ps_u[:, j, 0:NT], w[:, k, :], m.h[:, k, :], start=(k == 0), stop=(k == KD - 1))
                    mm.then_inc(m.done[t % RING], 1)

        @block.scalar
        def _(act):
            act.sem_inc(s["act_out"], RING)
            for tt in range(3):
                act.wait_ge(s["score_ps"], tt + 1)
                act.activation(m.score[0:TT, tt, :, :].rearrange("p a b -> p (a b)"), ps_s[0:TT, :], ACT.Copy).then_inc(
                    s["score_out"], 1)
            for a, b in ((0, HALF), (HALF, NKEYS // RING)):
                with act.Fori(a, b) as g:
                    for j in range(RING):
                        t = T_U + j
                        act.wait_ge(m.done[t % RING], g + (t // RING + 1))
                        act.activation(m.act[:, ds(g * RING + j, 1), :].squeeze(1), ps_u[:, j, 0:NT],
                                       ACT.Gelu_apprx_tanh).then_inc(s["act_out"], 1)
                if a == 0:
                    act.wait_ge(s["found"], 3)

        @block.vector
        def _(v):
            link = Chain(v, s["step"])
            sides = m.score[0:TT, :, :, :]
            r = slice(0, TT)

            def top16(values, best, index):
                link(v.max(best[:, 0:8], values))
                v.max_index(index[:, 0:8], best[:, 0:8], values)
                link(v.match_replace(values, best[:, 0:8], values, -3.4e38))
                link(v.max(best[:, 8:16], values))
                link(v.max_index(index[:, 8:16], best[:, 8:16], values))

            for tt in range(3):
                v.wait_ge(s["score_out"], tt + 1)
                for n in range(2 * HEADS):
                    top16(sides[:, tt, n, :], m.best[r, n, :], m.besti[r, n, :])
                link(v.tensor_copy(m.bestf[r, :, :], m.besti[r, :, :]))
                b = m.best[r, :, :].rearrange("p (s h) k -> p s h k", s=2)
                c = m.cand[r, :, :].rearrange("p h (a b) -> p h a b", a=TOPK)
                link(v.tensor_tensor(c, spread(b[:, 0, :, :], 3, TOPK), spread(b[:, 1, :, :], 2, TOPK), ALU.add))
                score = m.sel[r, 2, tt, :].rearrange("p (h k) -> p h k", h=HEADS)
                pos = m.pos[r, :].rearrange("p (h k) -> p h k", h=HEADS)
                for h in range(HEADS):
                    top16(m.cand[r, h, :], score[:, h, :], pos[:, h, :])
                link(v.tensor_tensor(m.posf[r, :].rearrange("p (h k) -> p h k", h=HEADS), score,
                                     score[:, :, 0:1].broadcast_to([TT, HEADS, TOPK]), ALU.subtract))
                link(v.tensor_copy(m.sel[r, 2, tt, :], m.posf[r, :]))
                for side, op, arg in ((0, ALU.logical_shift_right, 4), (1, ALU.bitwise_and, 15)):
                    link(v.tensor_single_scalar(m.posp[r, :], m.pos[r, :], arg, op))
                    link(v.tensor_copy(m.posf[r, :], m.posp[r, :]))
                    link(v.tensor_tensor(m.hit[r, :, :], spread(m.posf[r, :], 2, TOPK), spread(m.iota[r, 0:TOPK], 1, HEADS * TOPK),
                                         ALU.is_equal))
                    keys = m.bestf[r, side * HEADS:(side + 1) * HEADS, :]
                    hit = m.hit[r, :, :].rearrange("p (h k) a -> p h k a", h=HEADS)
                    link(v.tensor_tensor(hit, hit, spread(keys, 2, TOPK), ALU.mult))
                    link(v.tensor_reduce(m.sel[r, side, tt, :], m.hit[r, :, :], AX, ALU.add))
                v.sem_inc(s["found"], 1)


def gates_block(nc, m, l):
    TT = 96
    GROUP = 4
    TURN = 12
    names = "step exp_ready gates_ready turned turned_out act_step first_ready second_ready cols_ready gate_ps weighted held"
    with signals(nc, names) as s, nc.psum_tensor("ps_t", [P, 2, 512], F32) as ps_t, \
            nc.psum_tensor("ps_g", [P, 3, GROUP, P], F32) as ps_g, nc.Block() as block:
        e = m.sel[0:TT, 2, :, :].rearrange("p t (h k) -> p t h k", h=HEADS)
        total = m.rms[0:TT, 0:3 * HEADS].rearrange("p (t h) -> p t h", h=HEADS)
        half = TURN // 2

        @block.scalar
        def _(act):
            act.activation(m.sel[0:TT, 2, :, :], m.sel[0:TT, 2, :, :], ACT.Exp).then_inc(s["exp_ready"], 1)
            for kind in range(3):
                act.wait_ge(s["turned"], kind + 1)
                act.activation(m.selT[:, kind, :], ps_t[:, kind % 2, 0:NT], ACT.Copy).then_inc(s["turned_out"], 1)
            act.wait_ge(s["turned_out"], 3)

        @block.tensor
        def _(pe):
            pe.sem_inc(s["gate_ps"], 3)
            for kind in range(3):
                if kind == 2:
                    pe.wait_ge(s["turned_out"], 1)
                    pe.wait_ge(s["gates_ready"], 1)
                for tt in range(3):
                    mm = pe.transpose(ps_t[:, kind % 2, tt * TT:(tt + 1) * TT], m.sel[0:TT, kind, tt, :], m.ident[0:TT, 0:TT])
                mm.then_inc(s["turned"], 1)
            with pe.Fori(0, NT // TURN) as i:
                for g in range(TURN // GROUP):
                    pe.wait_ge(s["weighted"], i * 3 + (g + 1))
                    for c in range(GROUP):
                        j = g * GROUP + c
                        if c % 2 == 0:
                            pe.wait_ge(s["first_ready"], i * half + (j // 2 + 1 + 3))
                            pe.wait_ge(s["second_ready"], i * half + (j // 2 + 1 + 3))
                        mm = pe.matmul(ps_g[:, g, c, :], m.onehot[:, 0, j % 6, :], m.onehot[:, 1, j % 6, :], start=True, stop=True)
                        if c % 2:
                            mm.then_inc(s["gate_ps"], 1)

        @block.gpsimd
        def _(pool):
            pool.sem_inc(s["second_ready"], 3)
            pool.wait_ge(s["turned_out"], 3)
            with pool.Fori(0, NT // TURN) as i:
                hold(pool, s["second_ready"], i * half + 3, s["held"])
                pool.tensor_copy(m.cols[:, :], m.selT[:, 1, ds(i * TURN, TURN)]).then_inc(s["cols_ready"], 1)
                hold(pool, s["cols_ready"], i + 1, s["held"])
                for j in range(TURN):
                    if j % 2 == 0:
                        hold(pool, s["gate_ps"], i * half + (j // 2 + 1), s["held"])
                    o = pool.tensor_scalar(m.onehot[:, 1, j % 6, :], m.iota, m.cols[:, j:j + 1], None, ALU.is_equal)
                    if j % 2:
                        o.then_inc(s["second_ready"], 1)

        @block.vector
        def _(v):
            link = Chain(v, s["step"])
            v.wait_ge(s["exp_ready"], 1)
            link(v.tensor_reduce(total, e, AX, ALU.add))
            link(v.reciprocal(total, total))
            v.tensor_tensor(e, e, spread(total, 3, TOPK), ALU.mult).then_inc(s["gates_ready"], 1)
            v.wait_ge(s["turned_out"], 3)
            v.sem_inc(s["first_ready"], 3)
            v.sem_inc(s["weighted"], 3)

            def onehots(i, j):
                v.wait_ge(s["gate_ps"], i * half + (j // 2 + 1))
                for c in (j, j + 1):
                    o = v.tensor_scalar(m.onehot[:, 0, c % 6, :], m.iota, m.selT[:, 0, ds(i * TURN + c, 1)],
                                        m.selT[:, 2, ds(i * TURN + c, 1)], ALU.is_equal, ALU.mult)
                o.then_inc(s["first_ready"], 1)

            with v.Fori(0, NT // TURN) as i:
                for g in range(TURN // GROUP):
                    onehots(i, g * GROUP)
                    onehots(i, g * GROUP + 2)
                    v.wait_ge(s["gate_ps"], i * half + (2 * g + 2 + 3))
                    a = m.act[:, :, ds(i * TURN + g * GROUP, GROUP)]
                    v.tensor_tensor(a, a, ps_g[:, g, :, :].rearrange("p t e -> p e t"), ALU.mult).then_inc(s["weighted"], 1)


def combine_block(nc, m, l, stream):
    names = "step zeroed summed"
    with signals(nc, names) as s, nc.psum_tensor("ps_y", [P, 8, 512], F32) as ps, nc.Block() as block:
        tmp = m.h[:, :, 0:NB * NS]
        zero = m.sel[:, 0, 0, :]

        @block.sync
        def _(sp):
            load_many(sp, m, stream, l, T_V + RING, TILES)

        @block.tensor
        def _(pe):
            pe.wait_ge(s["zeroed"], 1)
            for k in range(KD):
                pe.matmul(ps[:, k, 0:NT], zero, m.h[:, k, :], start=True, stop=False)
            with pe.Fori(0, NKEYS // RING) as g:
                for j in range(RING):
                    t = T_V + j
                    pe.wait_ge(m.loaded[t % RING], g * 16 + 16 * (t // RING + 1))
                    w = m.tile(t)
                    for k in range(KD):
                        mm = pe.matmul(ps[:, k, 0:NT], w[:, k, :], m.act[:, ds(g * RING + j, 1), :].squeeze(1),
                                       start=False, stop=False)
                    mm.then_inc(m.done[t % RING], 1)
            for k in range(KD):
                mm = pe.matmul(ps[:, k, 0:NT], zero, m.h[:, k, :], start=False, stop=True)
            mm.then_inc(s["summed"], 1)

        @block.vector
        def _(v):
            link = Chain(v, s["step"])
            v.memset(zero, 0.0).then_inc(s["zeroed"], 1)
            v.wait_ge(s["summed"], 1)
            residual(link, m, 1, ps, tmp)


def final_block(nc, m, y_out):
    with signals(nc, "step squares_ready sums_ready root_ready y_ready saved") as s, \
            nc.psum_tensor("ps_f", [P, 512], F32) as ps, nc.Block() as block:
        @block.scalar
        def _(act):
            act.activation(m.square[:, :, :], m.x[:, :, :], ACT.Square).then_inc(s["squares_ready"], 1)
            act.wait_ge(s["sums_ready"], 1)
            act.activation(m.rms[:, :], ps[:, 0:NT], ACT.Sqrt, bias=m.eps, scale=1.0 / D).then_inc(s["root_ready"], 1)

        @block.tensor
        def _(pe):
            pe.wait_ge(s["squares_ready"], 1)
            for k in range(KD):
                mm = pe.matmul(ps[:, 0:NT], m.ones, m.square[:, k, :], start=(k == 0), stop=(k == KD - 1))
            mm.then_inc(s["sums_ready"], 1)

        @block.vector
        def _(v):
            link = Chain(v, s["step"])
            v.wait_ge(s["root_ready"], 1)
            link(v.reciprocal(m.rms[:, :], m.rms[:, :]))
            for k in range(KD):
                i = v.scalar_tensor_tensor(m.h[:, k, :], m.x[:, k, :], m.par("final")[:, k:k + 1], m.rms[:, :],
                                           ALU.mult, ALU.mult)
            i.then_inc(s["y_ready"], 1)

        @block.sync
        def _(sp):
            sp.wait_ge(s["y_ready"], 1)
            sp.dma_start(y_out, m.h[:, :, :]).then_inc(s["saved"], 16)
            sp.wait_ge(s["saved"], 16)


def build(nc, stream, small_in, mixc_in, keep_in, state_in, x_in, c_in, y_out, small_out, state_out):
    with ExitStack() as ctx:
        m = Memory(nc, ctx)
        setup_block(nc, m, x_in, c_in, keep_in)
        with nc.Fori(0, DEPTH) as l:
            project_block(nc, m, l, stream, small_in, mixc_in, state_in)
            local_block(nc, m, l, stream)
            hgrn_block(nc, m, l)
            delta_block(nc, m, l)
            output_block(nc, m, l, stream, small_out, state_out)
            experts_block(nc, m, l, stream)
            gates_block(nc, m, l)
            combine_block(nc, m, l, stream)
            for sem in m.loaded + m.done:
                nc.sync.sem_clear(sem)
            nc.all_engine_barrier()
        final_block(nc, m, y_out)


def host_layout(a):
    import numpy as np
    f = np.float32

    def cols(w):
        n = w.shape[2] // P
        return w.reshape(DEPTH, KD, P, n, P).transpose(0, 3, 2, 1, 4).reshape(DEPTH, n, P, D)

    stream = np.zeros((DEPTH, TILES, P, D), f)
    stream[:, T_ADA:T_IN] = cols(a["w_ada"])
    stream[:, T_IN:T_BETA] = cols(a["w_in"][:, :, :IN_TILES * P])[:, Z_ORDER]
    stream[:, T_BETA].reshape(DEPTH, P, KD, P)[:, :, :, :12] = \
        a["w_in"][:, :, IN_TILES * P:].reshape(DEPTH, KD, P, 12).transpose(0, 2, 1, 3)
    gate = stream[:, T_GATE].reshape(DEPTH, P, 8, P)
    for g, name in enumerate(("lru_wa", "lru_wx")):
        for t in range(B_TILES):
            for r in range(2):
                rows = slice(r * HD, (r + 1) * HD)
                gate[:, rows, g * B_TILES + t, rows] = a[name][:, 2 * t + r]
    stream[:, T_OUT:T_QUERY] = cols(a["w_out"])
    stream[:, T_QUERY:T_U] = cols(a["peer_wq"])
    stream[:, T_U:T_V] = a["peer_u"].reshape(DEPTH, NKEYS, NKEYS, KD, P).transpose(0, 2, 4, 3, 1).reshape(DEPTH, NKEYS, P, D)
    stream[:, T_V:] = a["peer_v"].reshape(DEPTH, NKEYS, NKEYS, D).transpose(0, 2, 1, 3)

    small = np.zeros((DEPTH, P, SMALL_W), f)

    def put(name, value):
        small[:, :, SMALL[name][0]:SMALL[name][1]] = value

    def feat(v):
        return v.reshape(DEPTH, -1, P).transpose(0, 2, 1)

    put("norm1", feat(a["norm1_g"]))
    put("norm2", feat(a["norm2_g"]))
    put("b_ada", feat(a["b_ada"]))
    put("lru_w", a["lru_conv_w"].reshape(DEPTH, CONV, B_TILES, P).transpose(0, 3, 2, 1).reshape(DEPTH, P, -1))
    put("lru_b", feat(a["lru_conv_b"]))
    put("dn_w", a["dn_conv_w"].reshape(DEPTH, CONV, 9, P).transpose(0, 3, 2, 1).reshape(DEPTH, P, -1))
    put("ba", feat(a["lru_ba"]))
    put("bx", feat(a["lru_bx"]))
    put("lru_L", feat(a["lru_L"]))
    put("a_norm", np.concatenate([a["a_norm_g"]] * 2, 1)[:, :, None])
    put("dn_norm", np.concatenate([a["dn_norm_g"]] * 2, 1)[:, :, None])
    put("a_log", a["dn_A_log"][:, None, :])
    put("dt_bias", a["dn_dt_bias"][:, None, :])
    put("final", a["final_norm_g"].reshape(KD, P).T[None])
    put("lb", np.concatenate([a["lb_param"][n].reshape(A_PAIRS, P).T for n in range(DEPTH)], 1)[None])
    put("lb_on", (np.arange(DEPTH) > 0).astype(f)[:, None, None])
    put("keys", np.concatenate([a["peer_k1"], a["peer_k2"]], 2).transpose(0, 2, 1))
    put("lru_h", a["state_lru_h"].reshape(DEPTH, NB, B_TILES, P).transpose(0, 3, 2, 1).reshape(DEPTH, P, -1))
    for name, key, n in (("lru_conv", "state_lru_conv", B_TILES), ("dn_conv", "state_dn_conv", 9)):
        put(name, a[key].reshape(DEPTH, NB, CONV - 1, n, P).transpose(0, 4, 3, 1, 2).reshape(DEPTH, P, -1))

    mixc = np.zeros((P, MIXC_W), f)

    def const(name, value):
        v = np.asarray(value, f)
        mixc[:v.shape[0], MIXC[name][0]:MIXC[name][1]] = v

    j, i = np.arange(P)[:, None], np.arange(P)[None, :]
    const("block_ones", j // HD == i // HD)
    const("levels", np.concatenate([(j >> (b + 1) == i >> (b + 1)) & ((j >> b) % 2 == 0) & ((i >> b) % 2 == 1)
                                    for b in range(7)], 1))
    same = (j // NS == i // NS) & (j <= i)
    const("tri", j <= i)
    const("tri_s", same[:32, :32])
    const("neg", np.where(j <= i, 0.0, -1e30))
    const("neg_s", np.where(same, 0.0, -1e30)[:32, :32])
    window = np.zeros((P, 2, 127), f)
    window[:HD, 0, 63] = window[HD:, 1, 63] = 1.0
    const("window", window.reshape(P, -1))
    tok = np.arange(NB * NS) // NS
    const("batch_cols", np.tile((np.arange(NB)[:, None] == tok[None, :]).reshape(1, -1), (P, 1)))
    const("batch_rows", tok[:, None] == np.arange(NB)[None, :])
    keep = np.concatenate([np.eye(P), np.ones((P, P)), np.tile(np.arange(P), (P, 1)), np.full((P, 1), EPS)], 1).astype(f)

    def heads(v, n):
        return v.reshape(DEPTH, NB, n, 2, HD, HD).transpose(0, 3, 4, 2, 1, 5).reshape(DEPTH, P, -1)

    state = np.concatenate([heads(a["state_hgrn"], A_PAIRS), heads(a["state_dn"], C_PAIRS)], 2)
    x = np.concatenate([a["x_prompt"].reshape(NP, D), a["x_sample"].reshape(NB * NS, D)], 0)
    c = np.concatenate([a["c_prompt"], a["c_sample"]], 0)
    return {"stream": stream, "small": small, "mixc": mixc, "keep": keep, "state": np.ascontiguousarray(state),
            "x": np.ascontiguousarray(x.reshape(NT, KD, P).transpose(2, 1, 0)),
            "c": np.ascontiguousarray(c.reshape(1 + NB, KD, P).transpose(2, 1, 0))}


OUTPUTS = {"y": (P, KD, NT), "small_out": (DEPTH, P, OUTS_W), "state_out": (DEPTH, P, STATE_W)}


def host_outputs(r):
    import numpy as np
    y = r["y"].transpose(2, 1, 0).reshape(NT, D)
    so = {k: r["small_out"][:, :, a:b] for k, (a, b) in OUTS.items()}
    st = r["state_out"].reshape(DEPTH, 2, HD, A_PAIRS + C_PAIRS, 1 + NB, HD).transpose(0, 4, 3, 1, 2, 5)

    def heads(b0, b1, q0, q1):
        v = st[:, b0:b1, q0:q1]
        return np.ascontiguousarray(v.reshape(DEPTH, b1 - b0, 2 * (q1 - q0), HD, HD))

    def conv(v, n, nb):
        return np.ascontiguousarray(v.reshape(DEPTH, P, n, nb, 3).transpose(0, 3, 4, 2, 1).reshape(DEPTH, nb, 3, n * P))

    def vec(v, nb):
        return np.ascontiguousarray(v.reshape(DEPTH, P, B_TILES, nb).transpose(0, 3, 2, 1).reshape(DEPTH, nb, B_TILES * P))

    ap, cp = A_PAIRS, A_PAIRS + C_PAIRS
    return (np.ascontiguousarray(y[:NP].reshape(1, NP, D)), np.ascontiguousarray(y[NP:].reshape(NB, NS, D)),
            heads(0, 1, 0, ap), vec(so["p_h"], 1), conv(so["p_lc"], B_TILES, 1), heads(0, 1, ap, cp), conv(so["p_dc"], 9, 1),
            heads(1, 1 + NB, 0, ap), vec(so["s_h"], NB), conv(so["s_lc"], B_TILES, NB), heads(1, 1 + NB, ap, cp),
            conv(so["s_dc"], 9, NB))


def kernel(**inputs):
    import numpy as np
    import concourse.bacc as bacc
    from concourse.bass_utils import run_bass_kernel_spmd

    arrays = host_layout({k: np.asarray(v) for k, v in inputs.items()})
    nc = bacc.Bacc("TRN2", target_bir_lowering=False, num_devices=1)
    ins = [nc.dram_tensor(f"in_{k}", v.shape, F32, kind="ExternalInput").ap() for k, v in arrays.items()]
    outs = [nc.dram_tensor(f"out_{k}", v, F32, kind="ExternalOutput").ap() for k, v in OUTPUTS.items()]
    build(nc, *ins, *outs)
    r = run_bass_kernel_spmd(nc, [{f"in_{k}": v for k, v in arrays.items()}], core_ids=[0]).results[0]
    return host_outputs({k: r[f"out_{k}"] for k in OUTPUTS})
```

```python
from contextlib import ExitStack, contextmanager

import concourse.bass as bass
from concourse import mybir

F32 = mybir.dt.float32
U32 = mybir.dt.uint32
ALU = mybir.AluOpType
ACT = mybir.ActivationFunctionType
AX = mybir.AxisListType.X
ds = bass.ds

P = 128
D = 1024
KD = D // P
DEPTH = 2
NP = 256
NB, NS = 8, 4
NT = NP + NB * NS
EPS = 1e-6
HD = 64
CONV = 4
A_PAIRS, B_TILES, C_PAIRS = 2, 3, 3
C_HEADS = 6
HEADS, NKEYS, TOPK = 8, 128, 16

RING = 4
ADA_TILES = 6 * KD
IN_TILES = 26
T_ADA = 0
T_IN = T_ADA + ADA_TILES
T_BETA = T_IN + IN_TILES
T_GATE = T_BETA + 1
T_OUT = T_GATE + 1
T_QUERY = T_OUT + KD
T_U = T_QUERY + KD
T_V = T_U + NKEYS
TILES = T_V + NKEYS
SILU_Z = [0, 1, 6, 7, 23, 24, 25]
PLAIN_Z = [4, 5, 8, 9, 10, 14, 15, 16, 17, 18, 19, 20, 21, 22]
SIGM_Z = [2, 3]
GELU_Z = [11, 12, 13]
Z_ORDER = SILU_Z + PLAIN_Z + SIGM_Z + GELU_Z

XP = CONV - 1 + NP
XS = CONV - 1 + NS
XW = XP + NB * XS
YW = XW - (CONV - 1)
SS = NS + 1
SW = NP + NB * SS

SMALL = {}
_at = 0
for _name, _n in (("norm1", KD), ("norm2", KD), ("b_ada", 6 * KD), ("lru_w", B_TILES * CONV), ("lru_b", B_TILES),
                  ("dn_w", 9 * CONV), ("ba", B_TILES), ("bx", B_TILES), ("lru_L", B_TILES), ("a_norm", 1),
                  ("dn_norm", 1), ("a_log", C_HEADS), ("dt_bias", C_HEADS), ("final", KD), ("lb", DEPTH * A_PAIRS),
                  ("lb_on", 1), ("keys", NKEYS), ("lru_h", B_TILES * NB),
                  ("lru_conv", B_TILES * NB * (CONV - 1)), ("dn_conv", 9 * NB * (CONV - 1))):
    SMALL[_name] = (_at, _at + _n)
    _at += _n
SMALL_W = _at
MIXC = {}
_at = 0
for _name, _n in (("block_ones", P), ("levels", 7 * P), ("tri", P), ("tri_s", 32), ("neg", P), ("neg_s", 32),
                  ("batch_cols", NB * 32), ("batch_rows", NB), ("block_rows", P // 8)):
    MIXC[_name] = (_at, _at + _n)
    _at += _n
MIXC_W = _at
KEEP_W = 3 * P + 1
OUTS = {}
_at = 0
for _name, _n in (("p_h", B_TILES), ("s_h", B_TILES * NB), ("p_lc", B_TILES * 3), ("s_lc", B_TILES * NB * 3),
                  ("p_dc", 9 * 3), ("s_dc", 9 * NB * 3)):
    OUTS[_name] = (_at, _at + _n)
    _at += _n
OUTS_W = _at
STATE_W = (A_PAIRS + C_PAIRS) * (1 + NB) * HD
LOG1P = [1.0 / k for k in (13, 11, 9, 7, 5, 3)]


class Chain:

    def __init__(self, eng, sem, base=0):
        self.eng, self.sem, self.base, self.n = eng, sem, base, 0

    def __call__(self, ins):
        self.n += 1
        ins.then_inc(self.sem, 1)
        self.eng.wait_ge(self.sem, self.base + self.n)


def hold(eng, sem, value, spare):
    eng.wait_ge(sem, value)
    eng.sem_inc(spare, 1)


class Area:

    def __init__(self, tensor, at=0):
        self.tensor, self.at = tensor, at

    def take(self, *shape, dtype=None):
        n = 1
        for s in shape:
            n *= s
        ap = self.tensor[:, self.at:self.at + n]
        self.at += n
        assert self.at <= self.tensor.shape[1]
        if dtype is not None:
            ap = ap.bitcast(dtype)
        names = "abcd"[:len(shape)]
        if len(shape) > 1:
            ap = ap.rearrange(f"p ({' '.join(names)}) -> p {' '.join(names)}", **dict(zip(names, shape)))
        return ap


def spread(ap, axis, n):
    ap = ap.unsqueeze(axis)
    shape = list(ap.shape)
    shape[axis] = n
    return ap.broadcast_to(shape)


def batched(ap):
    return ap.rearrange("p k (b s) -> p k b s", b=NB)


@contextmanager
def signals(nc, names):
    with ExitStack() as ctx:
        sems = {n: ctx.enter_context(nc.semaphore(n)) for n in names.split()}
        yield sems
        for s in sems.values():
            nc.sync.sem_clear(s)
        nc.all_engine_barrier()


class Memory:

    def __init__(self, nc, ctx):
        def sb(name, shape, dtype=F32):
            return ctx.enter_context(nc.sbuf_tensor(name, shape, dtype))

        self.x = sb("x_res", [P, KD, NT])
        self.h = sb("h_norm", [P, KD, NT])
        self.ring = sb("ring", [P, RING, D])
        self.keep = sb("keep", [P, KEEP_W])
        self.small = sb("small", [P, SMALL_W])
        self.mod = sb("mod", [P, 6 * KD, 1 + NB])
        self.gain = sb("gain", [P, 2, KD, 1 + NB])
        self.cond = sb("cond", [P, KD, 1 + NB])
        self.rms = sb("rms", [P, NT])
        self.sel = sb("sel", [P, 3, 3, HEADS * TOPK])
        self.selT = sb("selT", [P, 3, NT])
        self.onehot = sb("onehot", [P, 2, 6, P])
        self.cols = sb("cols", [P, 12])
        self.big = sb("big", [P, NKEYS * NT])
        self.act = self.big[:, :].rearrange("p (e t) -> p e t", t=NT)
        self.ident = self.keep[:, 0:P]
        self.ones = self.keep[:, P:2 * P]
        self.iota = self.keep[:, 2 * P:3 * P]
        self.eps = self.keep[:, 3 * P:3 * P + 1]
        self.loaded = [ctx.enter_context(nc.semaphore(f"tile_loaded{i}")) for i in range(RING)]
        self.done = [ctx.enter_context(nc.semaphore(f"tile_done{i}")) for i in range(RING)]
        a = Area(self.big)
        self.mixc = a.take(MIXC_W)
        self.zact = a.take(14, NT)
        self.tok = a.take(3, 2 * C_HEADS)
        self.beta = a.take(3, C_HEADS)
        self.decay = a.take(3, C_HEADS)
        self.qkv = a.take(9, NT)
        self.mixed = a.take(KD, NT)
        self.outs = a.take(OUTS_W)
        self.states = a.take(A_PAIRS + C_PAIRS, 1 + NB, HD)
        self.state0 = a.take(A_PAIRS + C_PAIRS, NB, HD)
        self.after_local = a.at
        self.xb = a.take(B_TILES, XW)
        self.xc = a.take(9, XW)
        self.square = a.take(KD, NT)
        self.free = a.at
        t = Area(self.big, 80 * NT)
        self.query = t.take(HEADS, NT)
        self.score = t.take(3, 2 * HEADS, NKEYS)
        self.cand = t.take(HEADS, TOPK * TOPK)
        self.best = t.take(2 * HEADS, TOPK)
        self.besti = t.take(2 * HEADS, TOPK, dtype=U32)
        self.bestf = t.take(2 * HEADS, TOPK)
        self.pos = t.take(HEADS * TOPK, dtype=U32)
        self.posp = t.take(HEADS * TOPK, dtype=U32)
        self.posf = t.take(HEADS * TOPK)
        self.hit = t.take(HEADS * TOPK, TOPK)

    def par(self, name):
        return self.small[:, SMALL[name][0]:SMALL[name][1]]

    def mix(self, name):
        return self.mixc[:, MIXC[name][0]:MIXC[name][1]]

    def out(self, name):
        return self.outs[:, OUTS[name][0]:OUTS[name][1]]

    def tile(self, n):
        return self.ring[:, n % RING, :].rearrange("p (k n) -> p k n", k=KD)

    def wait_tile(self, eng, n):
        eng.wait_ge(self.loaded[n % RING], 16 * (n // RING + 1))

    def wait_done(self, eng, n):
        eng.wait_ge(self.done[n % RING], n // RING + 1)


def load_tiles(eng, m, stream, l, first, end):
    for n in range(first, end):
        if n >= RING:
            m.wait_done(eng, n - RING)
        eng.dma_start(m.ring[:, n % RING, :], stream[l, n, :, :]).then_inc(m.loaded[n % RING], 16)


def load_many(eng, m, stream, l, first, end):
    turns = (end - first) // RING
    with eng.Fori(0, turns) as g:
        for j in range(RING):
            n = first + j
            eng.wait_ge(m.done[n % RING], g + n // RING)
            eng.dma_start(m.ring[:, n % RING, :], stream[l, g * RING + n, :, :]).then_inc(m.loaded[n % RING], 16)
    load_tiles(eng, m, stream, l, first + turns * RING, end)


def modulate(link, m, which, last=None):
    v, shift = link.eng, 3 * which * KD
    link(v.tensor_tensor(m.h[:, :, :], m.x[:, :, :], spread(m.rms[:, :], 1, KD), ALU.mult))
    for k in range(KD):
        link(v.tensor_scalar(m.h[:, k, 0:NP], m.h[:, k, 0:NP], m.gain[:, which, k, 0:1],
                             m.mod[:, shift + k, 0:1], ALU.mult, ALU.add))
    hs = batched(m.h[:, :, NP:NT])
    link(v.tensor_tensor(hs, hs, spread(m.gain[:, which, :, 1:], 3, NS), ALU.mult))
    v.tensor_tensor(hs, hs, spread(m.mod[:, shift:shift + KD, 1:], 3, NS), ALU.add).then_inc(last, 1)


def setup_block(nc, m, x_in, c_in, keep_in):
    with signals(nc, "in_loaded cond_ready") as s, nc.Block() as block:
        @block.sync
        def _(sp):
            sp.dma_start(m.cond[:, :, :], c_in).then_inc(s["in_loaded"], 16)
            sp.dma_start(m.keep[:, :], keep_in).then_inc(s["in_loaded"], 16)
            sp.dma_start(m.x[:, :, :], x_in).then_inc(s["in_loaded"], 16)

        @block.scalar
        def _(act):
            act.wait_ge(s["in_loaded"], 48)
            act.activation(m.cond[:, :, :], m.cond[:, :, :], ACT.Silu).then_inc(s["cond_ready"], 1)
            act.wait_ge(s["cond_ready"], 1)


def project_block(nc, m, l, stream, small_in, mixc_in, state_in):
    names = ("small_loaded mixc_loaded states_loaded squares_ready sums_ready root_ready mod_summed mod_ready "
             "h_ready step z_out pads_ready")
    with signals(nc, names) as s, nc.psum_tensor("ps_z", [P, 4, 512], F32) as ps_z, \
            nc.psum_tensor("ps_sum", [P, 512], F32) as ps_sum, nc.psum_tensor("ps_mod", [P, 512], F32) as ps_mod, \
            nc.Block() as block:
        tok_ps = ps_sum

        @block.sync
        def _(sp):
            load_tiles(sp, m, stream, l, 0, RING)
            sp.dma_start(m.small[:, :], small_in[l, :, :]).then_inc(s["small_loaded"], 16)
            sp.dma_start(m.mixc[:, :], mixc_in).then_inc(s["mixc_loaded"], 16)
            sp.dma_start(m.state0[:, :, :, :].rearrange("p a b c -> p (a b c)"), state_in[l, :, :]).then_inc(
                s["states_loaded"], 16)
            load_many(sp, m, stream, l, RING, T_OUT)
            load_tiles(sp, m, stream, l, T_OUT, T_OUT + RING - 1)
            sp.wait_ge(s["mixc_loaded"], 16)
            sp.wait_ge(s["states_loaded"], 16)

        @block.scalar
        def _(act):
            act.activation(m.square[:, :, :], m.x[:, :, :], ACT.Square).then_inc(s["squares_ready"], 1)
            act.wait_ge(s["sums_ready"], 1)
            act.activation(m.rms[:, :], ps_sum[:, 0:NT], ACT.Sqrt, bias=m.eps, scale=1.0 / D).then_inc(s["root_ready"], 1)
            for n, z in enumerate(Z_ORDER):
                m.wait_done(act, T_IN + n)
                src = ps_z[:, n % 4, 0:NT]
                if z in PLAIN_Z and z not in (4, 5):
                    ext = m.xb[:, z - 8, :] if z < 14 else m.xc[:, z - 14, :]
                    act.activation(ext[:, CONV - 1:XP], src[:, 0:NP], ACT.Copy)
                    act.activation(ext[:, XP:XW].rearrange("p (b s) -> p b s", b=NB)[:, :, CONV - 1:],
                                   src[:, NP:NT].rearrange("p (b s) -> p b s", b=NB), ACT.Copy).then_inc(s["z_out"], 1)
                else:
                    f = ACT.Silu if z in SILU_Z else ACT.Sigmoid if z in SIGM_Z else ACT.Gelu_apprx_tanh if z in GELU_Z else ACT.Copy
                    slot = z if z < 8 else z - 3 if z < 14 else z - 12
                    act.activation(m.zact[:, slot, :], src, f).then_inc(s["z_out"], 1)
            m.wait_done(act, T_BETA)
            act.activation(m.tok[:, 0:2, :], tok_ps[:, 0:4 * C_HEADS].rearrange("p (t c) -> p t c", t=2), ACT.Copy)
            act.wait_ge(s["pads_ready"], 4)
            act.activation(m.tok[0:32, 2, :], tok_ps[0:32, 4 * C_HEADS:6 * C_HEADS], ACT.Copy).then_inc(s["z_out"], 1)
            act.wait_ge(s["z_out"], IN_TILES + 1)

        @block.gpsimd
        def _(pool):
            pool.wait_ge(s["small_loaded"], 16)
            for ext, name, n in ((m.xb, "lru_conv", B_TILES), (m.xc, "dn_conv", 9)):
                pool.tensor_copy(ext[:, :, XP:XW].rearrange("p k (b s) -> p k b s", b=NB)[:, :, :, 0:CONV - 1],
                                 m.par(name).rearrange("p (k b s) -> p k b s", k=n, b=NB)).then_inc(s["pads_ready"], 1)
            pool.memset(m.xb[:, :, 0:CONV - 1], 0.0)
            pool.memset(m.xc[:, :, 0:CONV - 1], 0.0).then_inc(s["pads_ready"], 1)
            pool.memset(m.tok[:, 2, :], 0.0).then_inc(s["pads_ready"], 1)
            pool.wait_ge(s["pads_ready"], 4)

        @block.vector
        def _(v):
            link = Chain(v, s["step"])
            v.wait_ge(s["root_ready"], 1)
            link(v.reciprocal(m.rms[:, :], m.rms[:, :]))
            v.wait_ge(s["small_loaded"], 16)
            v.wait_ge(s["mod_summed"], 1)
            link(v.tensor_tensor(m.mod[:, :, :], ps_mod[:, 0:ADA_TILES * 9].rearrange("p (t c) -> p t c", c=9),
                                 spread(m.par("b_ada"), 2, 1 + NB), ALU.add))
            for w, name in ((0, "norm1"), (1, "norm2")):
                scale = m.mod[:, (3 * w + 1) * KD:(3 * w + 2) * KD, :]
                link(v.scalar_tensor_tensor(m.gain[:, w, :, :], scale, 1.0, spread(m.par(name), 2, 1 + NB),
                                            ALU.add, ALU.mult))
            modulate(link, m, 0, s["h_ready"])
            v.wait_ge(s["h_ready"], 1)

        @block.tensor
        def _(pe):
            pe.wait_ge(s["squares_ready"], 1)
            for k in range(KD):
                mm = pe.matmul(ps_sum[:, 0:NT], m.ones, m.square[:, k, :], start=(k == 0), stop=(k == KD - 1))
            mm.then_inc(s["sums_ready"], 1)
            for n in range(ADA_TILES):
                m.wait_tile(pe, n)
                w = m.tile(n)
                for k in range(KD):
                    mm = pe.matmul(ps_mod[:, 9 * n:9 * n + 9], w[:, k, :], m.cond[:, k, :], start=(k == 0), stop=(k == KD - 1))
                mm.then_inc(m.done[n % RING], 1)
                if n == ADA_TILES - 1:
                    m.wait_done(pe, n)
                    pe.sem_inc(s["mod_summed"], 1)
            pe.wait_ge(s["h_ready"], 1)
            for n in range(IN_TILES):
                t = T_IN + n
                m.wait_tile(pe, t)
                if n >= 4:
                    pe.wait_ge(s["z_out"], n - 3)
                w = m.tile(t)
                for k in range(KD):
                    mm = pe.matmul(ps_z[:, n % 4, 0:NT], w[:, k, :], m.h[:, k, :], start=(k == 0), stop=(k == KD - 1))
                mm.then_inc(m.done[t % RING], 1)
            m.wait_tile(pe, T_BETA)
            pe.wait_ge(s["root_ready"], 1)
            w = m.tile(T_BETA)
            for t, (a, b) in enumerate(((0, 128), (128, 256), (256, 288))):
                for k in range(KD):
                    mm = pe.matmul(tok_ps[0:b - a, 12 * t:12 * t + 12], m.h[:, k, a:b], w[:, k, 0:12],
                                   start=(k == 0), stop=(k == KD - 1))
            mm.then_inc(m.done[T_BETA % RING], 1)


def local_block(nc, m, l, stream):
    names = ("step act_step conv_b conv_c xb_ready gates_out soft_in soft_exp decay_ready a_ready root_in root_ready "
             "qkv_ready qk_squares qk_sums qk_root tail resets_ready outs_ready")
    with signals(nc, names) as s, nc.psum_tensor("ps_q", [P, 8, 512], F32) as ps, nc.Block() as block:
        f = Area(m.big, m.free)
        yb = f.take(B_TILES, XW)
        yc = f.take(9, XW)
        xcb = f.take(B_TILES, NT)
        rgate = f.take(B_TILES, NT)
        igate = f.take(B_TILES, NT)
        a = f.take(B_TILES, NT)
        th = f.take(B_TILES, NT)
        aext = f.take(B_TILES, SW)
        bext = f.take(B_TILES, SW)
        hext = f.take(B_TILES, SW)
        sp_in = f.take(B_TILES + 3 * C_HEADS)
        sp_w = f.take(B_TILES + 3 * C_HEADS)
        sp_s = f.take(B_TILES + 3 * C_HEADS)
        sp_z = f.take(B_TILES + 3 * C_HEADS)
        sp_p = f.take(B_TILES + 3 * C_HEADS)
        alog = f.take(C_HEADS)
        sq = f.take(6, NT)

        def ysamp(y):
            return y[:, :, XP:XW].rearrange("p k (b s) -> p k b s", b=NB)[:, :, :, 0:NS]

        @block.sync
        def _(sp):
            load_tiles(sp, m, stream, l, T_OUT + RING - 1, T_OUT + RING)

        @block.tensor
        def _(pe):
            m.wait_tile(pe, T_GATE)
            pe.wait_ge(s["xb_ready"], 2)
            w = m.ring[:, T_GATE % RING, :]
            for g in range(2):
                for t in range(B_TILES):
                    n = g * B_TILES + t
                    mm = pe.matmul(ps[:, n, 0:NT], w[:, n * P:(n + 1) * P], xcb[:, t, :], start=True, stop=True)
            mm.then_inc(m.done[T_GATE % RING], 1)
            pe.wait_ge(s["qk_squares"], 1)
            pe.wait_ge(s["gates_out"], 2)
            for n in range(6):
                mm = pe.matmul(ps[:, n, 0:NT], m.mix("block_ones"), sq[:, n, :], start=True, stop=True)
            mm.then_inc(s["qk_sums"], 1)

        @block.scalar
        def _(act):
            act.wait_ge(s["soft_in"], 1)
            act.activation(sp_w, sp_w, ACT.Exp, scale=-1.0)
            act.activation(alog, m.par("a_log"), ACT.Exp).then_inc(s["soft_exp"], 1)
            act.activation(m.beta[:, :, :], m.tok[:, :, 0:C_HEADS], ACT.Sigmoid)
            m.wait_done(act, T_GATE)
            for g, (dst, bias) in enumerate(((rgate, "ba"), (igate, "bx"))):
                for t in range(B_TILES):
                    i = act.activation(dst[:, t, :], ps[:, g * B_TILES + t, 0:NT], ACT.Sigmoid,
                                       bias=m.par(bias)[:, t:t + 1])
                i.then_inc(s["gates_out"], 1)
            act.wait_ge(s["gates_out"], 2)
            act.wait_ge(s["decay_ready"], 1)
            for t in range(B_TILES):
                act.activation(th[:, t, :], rgate[:, t, :], ACT.Tanh, scale=sp_in[:, t:t + 1])
            for t in range(B_TILES):
                i = act.activation(a[:, t, :], rgate[:, t, :], ACT.Exp, scale=sp_in[:, t:t + 1])
            i.then_inc(s["a_ready"], 1)
            act.wait_ge(s["conv_c"], 1)
            act.activation(m.qkv[:, :, 0:NP], yc[:, :, 0:NP], ACT.Silu)
            act.activation(batched(m.qkv[:, :, NP:NT]), ysamp(yc), ACT.Silu).then_inc(s["qkv_ready"], 1)
            act.wait_ge(s["qkv_ready"], 1)
            act.activation(sq[:, :, :], m.qkv[:, 0:6, :], ACT.Square).then_inc(s["qk_squares"], 1)
            act.wait_ge(s["root_in"], 1)
            act.activation(th[:, :, :], th[:, :, :], ACT.Sqrt, scale=-1.0).then_inc(s["root_ready"], 1)
            act.wait_ge(s["qk_sums"], 1)
            act.activation(sq[:, :, :], ps[:, 0:6, 0:NT], ACT.Sqrt, bias=m.eps).then_inc(s["qk_root"], 1)

        @block.gpsimd
        def _(pool):
            pool.memset(aext[:, :, 0:1], 0.0)
            pool.memset(aext[:, :, NP:SW].rearrange("p k (b s) -> p k b s", b=NB)[:, :, :, 0:1], 0.0)
            pool.tensor_copy(bext[:, :, NP:SW].rearrange("p k (b s) -> p k b s", b=NB)[:, :, :, 0],
                             m.par("lru_h").rearrange("p (k b) -> p k b", k=B_TILES)).then_inc(s["resets_ready"], 1)
            for ext, pn, sn, n in ((m.xb, "p_lc", "s_lc", B_TILES), (m.xc, "p_dc", "s_dc", 9)):
                pool.tensor_copy(m.out(pn).rearrange("p (k c) -> p k c", k=n), ext[:, :, XP - 3:XP])
                i = pool.tensor_copy(m.out(sn).rearrange("p (k b c) -> p k b c", k=n, b=NB),
                                 ext[:, :, XP:XW].rearrange("p k (b s) -> p k b s", b=NB)[:, :, :, NS:NS + 3])
            i.then_inc(s["outs_ready"], 1)
            pool.wait_ge(s["outs_ready"], 1)
            pool.wait_ge(s["resets_ready"], 1)

        @block.vector
        def _(v):
            link = Chain(v, s["step"])

            def conv(y, ext, t, w, bias=None):
                if bias is None:
                    link(v.tensor_scalar(y[:, t, 0:YW], ext[:, t, 0:YW], w[:, 4 * t:4 * t + 1], None, ALU.mult))
                else:
                    link(v.tensor_scalar(y[:, t, 0:YW], ext[:, t, 0:YW], w[:, 4 * t:4 * t + 1], bias, ALU.mult, ALU.add))
                for k in range(1, CONV):
                    link(v.scalar_tensor_tensor(y[:, t, 0:YW], ext[:, t, k:k + YW], w[:, 4 * t + k:4 * t + k + 1],
                                                y[:, t, 0:YW], ALU.mult, ALU.add))

            nsp = B_TILES
            link(v.tensor_scalar(sp_in[:, 0:nsp], m.par("lru_L"), -1.0, None, ALU.mult))
            link(v.tensor_tensor(sp_in[:, nsp:].rearrange("p (t h) -> p t h", t=3), m.tok[:, :, C_HEADS:],
                                 spread(m.par("dt_bias"), 1, 3), ALU.add))
            link(v.tensor_scalar(sp_w, sp_in, -1.0, None, ALU.mult))
            v.tensor_tensor(sp_w, sp_w, sp_in, ALU.max).then_inc(s["soft_in"], 1)
            v.wait_ge(s["soft_in"], 1)
            for t in range(B_TILES):
                conv(yb, m.xb, t, m.par("lru_w"), m.par("lru_b")[:, t:t + 1])
            v.tensor_copy(xcb[:, :, 0:NP], yb[:, :, 0:NP]).then_inc(s["xb_ready"], 1)
            v.tensor_copy(batched(xcb[:, :, NP:NT]), ysamp(yb)).then_inc(s["xb_ready"], 1)
            v.wait_ge(s["soft_exp"], 1)
            link(v.tensor_scalar(sp_z, sp_w, 2.0, None, ALU.add))
            link(v.reciprocal(sp_z, sp_z))
            link(v.tensor_tensor(sp_s, sp_w, sp_z, ALU.mult))
            link(v.tensor_tensor(sp_z, sp_s, sp_s, ALU.mult))
            link(v.tensor_scalar(sp_p, sp_z, 1.0 / 15, None, ALU.mult))
            for c in LOG1P:
                link(v.scalar_tensor_tensor(sp_p, sp_p, c, sp_z, ALU.add, ALU.mult))
            link(v.scalar_tensor_tensor(sp_p, sp_p, 1.0, sp_s, ALU.add, ALU.mult))
            link(v.tensor_scalar(sp_s, sp_in, 0.0, None, ALU.max))
            link(v.scalar_tensor_tensor(sp_in, sp_p, 2.0, sp_s, ALU.mult, ALU.add))
            link(v.scalar_tensor_tensor(m.decay[:, :, :], sp_in[:, nsp:].rearrange("p (t h) -> p t h", t=3), -1.0,
                                        spread(alog, 1, 3), ALU.mult, ALU.mult))
            v.tensor_scalar(sp_in[:, 0:nsp], sp_in[:, 0:nsp], -8.0, None, ALU.mult).then_inc(s["decay_ready"], 1)
            for t in range(9):
                conv(yc, m.xc, t, m.par("dn_w"))
            v.sem_inc(s["conv_c"], 1)
            v.wait_ge(s["a_ready"], 1)
            v.wait_ge(s["resets_ready"], 1)
            link(v.tensor_tensor(xcb[:, :, :], xcb[:, :, :], igate[:, :, :], ALU.mult))
            link(v.tensor_tensor(igate[:, :, :], a[:, :, :], a[:, :, :], ALU.mult))
            v.scalar_tensor_tensor(th[:, :, :], igate[:, :, :], 1.0, th[:, :, :], ALU.add, ALU.mult).then_inc(s["root_in"], 1)
            link(v.tensor_copy(aext[:, :, 1:NP], a[:, :, 1:NP]))
            link(v.tensor_copy(aext[:, :, NP:SW].rearrange("p k (b s) -> p k b s", b=NB)[:, :, :, 1:], batched(a[:, :, NP:NT])))
            v.wait_ge(s["root_ready"], 1)
            link(v.tensor_tensor(bext[:, :, 0:NP], th[:, :, 0:NP], xcb[:, :, 0:NP], ALU.mult))
            link(v.tensor_tensor(bext[:, :, NP:SW].rearrange("p k (b s) -> p k b s", b=NB)[:, :, :, 1:],
                                 batched(th[:, :, NP:NT]), batched(xcb[:, :, NP:NT]), ALU.mult))
            link(v.tensor_tensor_scan(flat(hext), flat(aext), flat(bext), 0.0, ALU.mult, ALU.add))
            hs = hext[:, :, NP:SW].rearrange("p k (b s) -> p k b s", b=NB)
            link(v.tensor_tensor(m.mixed[:, 2:5, 0:NP], hext[:, :, 0:NP], m.zact[:, 8:11, 0:NP], ALU.mult))
            link(v.tensor_tensor(batched(m.mixed[:, 2:5, NP:NT]), hs[:, :, :, 1:], batched(m.zact[:, 8:11, NP:NT]), ALU.mult))
            link(v.tensor_copy(m.out("p_h"), hext[:, :, NP - 1]))
            link(v.tensor_copy(m.out("s_h").rearrange("p (k b) -> p k b", k=B_TILES), hs[:, :, :, NS]))
            v.wait_ge(s["qk_root"], 1)
            link(v.reciprocal(sq[:, :, :], sq[:, :, :]))
            link(v.scalar_tensor_tensor(flat(m.qkv[:, 0:3, :]), flat(m.qkv[:, 0:3, :]), HD ** -0.5, flat(sq[:, 0:3, :]),
                                        ALU.mult, ALU.mult))
            link(v.tensor_tensor(m.qkv[:, 3:6, :], m.qkv[:, 3:6, :], sq[:, 3:6, :], ALU.mult))


def hgrn_block(nc, m, l):
    C = 8
    BLOCKS = NP // C
    TB = P // C
    TOK = ((0, P), (P, P), (NP, NB * NS))
    names = ("step pool_step lb_ready lb_out f_ready gates_ready qt_ready pairs_ready sums_ready kt_ready turned "
             "kt_out vm_ready u_ready u_out scan_ready inter_ready products_ready")
    with signals(nc, names) as s, nc.psum_tensor("ps_sums", [P, 2, 2, 512], F32) as ps_sums, \
            nc.psum_tensor("ps_outer", [P, 4, 512], F32) as ps_outer, nc.Block() as block:
        f = Area(m.big, m.after_local)
        lb = f.take(A_PAIRS)
        omlb = f.take(A_PAIRS)
        gate = [None] + [f.take(A_PAIRS, NT) for _ in range(1, C)]
        key = f.take(A_PAIRS, NT)
        q = f.take(A_PAIRS, NT)
        start0 = f.take(A_PAIRS, NT)
        start1 = f.take(A_PAIRS, NT)
        since = f.take(A_PAIRS, NT)
        qt = f.take(A_PAIRS, NT)
        kt = f.take(A_PAIRS, NT)
        pair_p = f.take(2, 2 * NP)
        pair_s = f.take(2, 2 * NB * NS)
        prod_p = f.take(2 * NP)
        prod_s = f.take(2 * NB * NS)
        ktt = f.take(3, A_PAIRS, P)
        vtok = f.take(3, A_PAIRS * P)
        vm = f.take(2, 4, TB // 2, HD)
        after = f.take(A_PAIRS, BLOCKS, HD)
        v = m.zact[:, 4:6, :]
        o = m.mixed[:, 0:2, :]

        def blocks(x, sample, lo, hi):
            x, c = (x[:, :, NP:NT], NS) if sample else (x[:, :, 0:NP], C)
            return x.rearrange("p a (n c) -> p a n c", c=c)[:, :, :, lo:hi]

        def compact(x, sample, d):
            n = NS - d if sample else C - d
            w = A_PAIRS * (NB if sample else BLOCKS) * n
            return x[:, 0:w].rearrange("p (a n c) -> p a n c", a=A_PAIRS, c=n)

        def kinds(d):
            return (False, True) if d < NS else (False,)

        def length(sample):
            return NS if sample else C

        @block.scalar
        def _(act):
            act.wait_ge(s["lb_ready"], 1)
            act.activation(lb, lb, ACT.Sigmoid).then_inc(s["lb_out"], 1)
            for tt in range(3):
                n = TOK[tt][1]
                act.wait_ge(s["turned"], tt + 1)
                act.activation(flat(ktt[0:n, tt, :, :]), ps_outer[0:n, tt, 0:2 * P], ACT.Copy).then_inc(s["kt_out"], 1)
            act.wait_ge(s["scan_ready"], 4)
            act.activation(m.states[:, 0:A_PAIRS, 0, :], after[:, :, BLOCKS - 1, :], ACT.Copy)

        @block.gpsimd
        def _(pool):
            link = Chain(pool, s["pool_step"])
            pool.wait_ge(s["f_ready"], 1)
            for d in range(2, C):
                for sample in kinds(d):
                    n = length(sample)
                    link(pool.tensor_tensor(blocks(gate[d], sample, d, n), blocks(gate[d - 1], sample, d, n),
                                            blocks(gate[1], sample, 1, n - d + 1), ALU.mult))
                pool.sem_inc(s["pairs_ready"], 1)
            for sample in (False, True):
                n = length(sample)
                link(pool.tensor_copy(blocks(kt, sample, n - 1, n), blocks(key, sample, n - 1, n)))
                for d in range(1, n):
                    link(pool.tensor_tensor(blocks(kt, sample, n - 1 - d, n - d), blocks(key, sample, n - 1 - d, n - d),
                                            blocks(gate[d], sample, n - 1, n), ALU.mult))
            pool.sem_inc(s["kt_ready"], 1)
            pool.wait_ge(s["gates_ready"], 1)
            pool.tensor_tensor(qt[:, :, :], q[:, :, :], since[:, :, :], ALU.mult).then_inc(s["qt_ready"], 1)

        @block.tensor
        def _(pe):
            def distance(d):
                pe.wait_ge(s["products_ready"], d + 1)
                for sample in kinds(d):
                    w = A_PAIRS * (NB * (NS - d) if sample else BLOCKS * (C - d))
                    src = (pair_s if sample else pair_p)[:, d % 2, 0:w]
                    mm = pe.matmul(ps_sums[:, d % 2, int(sample), 0:w], m.mix("block_ones"), src, start=True, stop=True)
                mm.then_inc(s["sums_ready"], 1)

            distance(0)
            distance(1)
            pe.wait_ge(s["kt_ready"], 1)
            for tt, (t0, n) in enumerate(TOK):
                for pair in range(A_PAIRS):
                    pe.transpose(ps_outer[0:n, tt, pair * P:(pair + 1) * P], kt[:, pair, t0:t0 + n], m.ident)
                for pair in range(A_PAIRS):
                    mm = pe.transpose(ps_outer[0:n, tt, (2 + pair) * P:(3 + pair) * P], v[:, pair, t0:t0 + n], m.ident)
                mm.then_inc(s["turned"], 1)
            for d in range(2, C):
                distance(d)
            for tt in range(2):
                for hb in range(2):
                    turn = 2 * tt + hb
                    pe.wait_ge(s["vm_ready"], turn + 1)
                    for pair in range(A_PAIRS):
                        n = 2 * turn + pair
                        if n >= 4:
                            pe.wait_ge(s["u_out"], n - 3)
                        for r in range(2):
                            rows = slice(r * HD, (r + 1) * HD)
                            mm = pe.matmul(ps_outer[rows, n % 4, :], ktt[:, tt, pair, rows],
                                           vm[:, turn % 2, 2 * pair + r, :, :], start=True, stop=True)
                        mm.then_inc(s["u_ready"], 1)
            pe.wait_ge(s["vm_ready"], 5)
            pe.wait_ge(s["u_out"], 8)
            for pair in range(A_PAIRS):
                for r in range(2):
                    rows = slice(r * HD, (r + 1) * HD)
                    mm = pe.matmul(ps_outer[rows, pair, :], ktt[0:NB * NS, 2, pair, rows], vm[0:NB * NS, 0, 2 * pair + r, :, :],
                                   start=True, stop=True)
            mm.then_inc(s["u_ready"], 1)
            pe.wait_ge(s["qt_ready"], 1)
            for b in range(NB):
                t = NP + NS * b
                for pair in range(A_PAIRS):
                    for r in range(2):
                        rows = slice(r * HD, (r + 1) * HD)
                        pe.matmul(ps_sums[rows, 0, pair, t:t + NS], m.state0[rows, pair, b, :], qt[rows, pair, t:t + NS],
                                  start=True, stop=True)
            for b in range(1, BLOCKS):
                if b % (TB // 2) == 1:
                    pe.wait_ge(s["scan_ready"], b // (TB // 2) + 1)
                for pair in range(A_PAIRS):
                    for r in range(2):
                        rows = slice(r * HD, (r + 1) * HD)
                        mm = pe.matmul(ps_sums[rows, 0, pair, C * b:C * b + C], after[rows, pair, b - 1, :],
                                       qt[rows, pair, C * b:C * b + C], start=True, stop=True)
            mm.then_inc(s["inter_ready"], 1)

        @block.vector
        def _(ve):
            link = Chain(ve, s["step"])
            ve.tensor_tensor(lb, m.par("lb")[:, A_PAIRS:2 * A_PAIRS], m.par("lb")[:, 0:A_PAIRS], ALU.subtract).then_inc(
                s["lb_ready"], 1)
            ve.wait_ge(s["lb_out"], 1)
            link(ve.tensor_scalar(lb, lb, m.par("lb_on"), None, ALU.mult))
            link(ve.tensor_scalar(omlb, lb, -1.0, 1.0, ALU.mult, ALU.add))
            for pair in range(A_PAIRS):
                link(ve.tensor_scalar(gate[1][:, pair, :], m.zact[:, 2 + pair, :], omlb[:, pair:pair + 1],
                                      lb[:, pair:pair + 1], ALU.mult, ALU.add))
            link(ve.tensor_scalar(key[:, :, :], gate[1][:, :, :], -1.0, 1.0, ALU.mult, ALU.add))
            ve.sem_inc(s["f_ready"], 1)
            link(ve.tensor_scalar(q[:, :, :], m.zact[:, 0:2, :], HD ** -0.5, None, ALU.mult))

            def pairs(d):
                if d >= 2:
                    ve.wait_ge(s["pairs_ready"], d - 1)
                for sample in kinds(d):
                    n = length(sample)
                    dst = compact((pair_s if sample else pair_p)[:, d % 2, :], sample, d)
                    if d == 0:
                        link(ve.tensor_tensor(dst, blocks(q, sample, 0, n), blocks(key, sample, 0, n), ALU.mult))
                    else:
                        link(ve.tensor_tensor(dst, blocks(q, sample, d, n), blocks(gate[d], sample, d, n), ALU.mult))
                        link(ve.tensor_tensor(dst, dst, blocks(key, sample, 0, n - d), ALU.mult))
                ve.sem_inc(s["products_ready"], 1)

            def values(d):
                ve.wait_ge(s["sums_ready"], d + 1)
                for sample in kinds(d):
                    n = length(sample)
                    a = compact(ps_sums[:, d % 2, int(sample), :], sample, d)
                    if d == 0:
                        link(ve.tensor_tensor(blocks(o, sample, 0, n), a, blocks(v, sample, 0, n), ALU.mult))
                    else:
                        tmp = compact(prod_s if sample else prod_p, sample, d)
                        link(ve.tensor_tensor(tmp, a, blocks(v, sample, 0, n - d), ALU.mult))
                        link(ve.tensor_tensor(blocks(o, sample, d, n), blocks(o, sample, d, n), tmp, ALU.add))

            def mask_v(turn):
                if turn < 4:
                    tt, hb, n = turn // 2, turn % 2, P
                    mask = m.mix("block_rows")[:, hb * TB // 2:(hb + 1) * TB // 2]
                else:
                    tt, n, mask = 2, NB * NS, m.mix("batch_rows")[0:NB * NS, :]
                if turn >= 2:
                    ve.wait_ge(s["u_ready"], 2 * turn - 2)
                for h in range(4):
                    i = ve.tensor_tensor(vm[0:n, turn % 2, h, :, :],
                                         spread(vtok[0:n, tt, h * HD:(h + 1) * HD], 1, TB // 2),
                                         spread(mask[0:n], 2, HD), ALU.mult)
                i.then_inc(s["vm_ready"], 1)

            pairs(0)
            pairs(1)
            values(0)
            link(ve.tensor_copy(start0[:, :, :], gate[1][:, :, :]))
            link(ve.memset(start1[:, :, :], 0.0))
            for sample in (False, True):
                link(ve.memset(blocks(start0, sample, 0, 1), 0.0))
                link(ve.tensor_copy(blocks(start1, sample, 0, 1), blocks(gate[1], sample, 0, 1)))
            ve.tensor_tensor_scan(flat(since), flat(start0), flat(start1), 0.0, ALU.mult, ALU.add).then_inc(
                s["gates_ready"], 1)
            for d in range(2, C):
                pairs(d)
                values(d - 1)
            values(C - 1)
            ve.wait_ge(s["kt_out"], 3)
            for tt, (t0, n) in enumerate(TOK):
                link(ve.tensor_copy(vtok[0:n, tt, :], ps_outer[0:n, tt, 2 * P:4 * P]))
            mask_v(0)
            mask_v(1)
            for turn in range(4):
                ve.wait_ge(s["u_ready"], 2 * turn + 2)
                for j in range(TB // 2):
                    b = turn * TB // 2 + j
                    for pair in range(A_PAIRS):
                        new, add = after[:, pair, b, :], ps_outer[:, (2 * turn + pair) % 4, j * HD:(j + 1) * HD]
                        if b == 0:
                            i = ve.tensor_copy(new, add)
                        else:
                            i = ve.scalar_tensor_tensor(new, after[:, pair, b - 1, :],
                                                        since[:, pair, C * b + C - 1:C * b + C], add, ALU.mult, ALU.add)
                        link(i)
                ve.sem_inc(s["scan_ready"], 1)
                ve.sem_inc(s["u_out"], 2)
                if turn < 3:
                    mask_v(turn + 2)
            ve.wait_ge(s["u_ready"], 9)
            for pair in range(A_PAIRS):
                new = m.states[:, pair, 1:, :]
                last = blocks(since, True, NS - 1, NS)[:, pair, :, :].broadcast_to([P, NB, HD])
                link(ve.tensor_tensor(new, m.state0[:, pair, :, :], last, ALU.mult))
                link(ve.tensor_tensor(new, new, ps_outer[:, pair, :].rearrange("p (b v) -> p b v", b=NB), ALU.add))
            ve.wait_ge(s["inter_ready"], 1)
            link(ve.tensor_tensor(o[:, :, C:], o[:, :, C:], ps_sums[:, 0, :, C:NT], ALU.add))


def flat(ap):
    return ap.rearrange("p a b -> p (a b)")


def delta_block(nc, m, l):
    GROUPS = ((0, P, 0), (P, P, 1), (NP, NB * NS, 2))
    names = ("step act_step ps_a ps_b ps_c ps_d gcol_out eg_ready kb_ready raw_ready pair_free x_ready x_out tu_ready "
             "tu_done kd_ps kd_out r_ps r_out e_ps e_out o_ps s_ps s_out a_free em_ready dt_ready dte_ready gp_ready "
             "glast_ready glast_exp scaled masked kd_mul r_sum nk_masked")
    H = C_HEADS
    with signals(nc, names) as s, nc.psum_tensor("ps_1", [P, 1024], F32) as ps1, \
            nc.psum_tensor("ps_2", [P, 1024], F32) as ps2, nc.psum_tensor("ps_3", [P, 1024], F32) as ps3, \
            nc.psum_tensor("ps_4", [P, 1024], F32) as ps4, nc.Block() as block:
        f = Area(m.big, m.after_local)

        def by_group(tiles):
            return [f.take(tiles, n) for _, n, _ in GROUPS]

        gcol = f.take(3, H)
        dt = f.take(H, P)
        gp = f.take(C_PAIRS, P)
        eg = by_group(C_PAIRS)
        gl = f.take(C_PAIRS, P)
        kb = f.take(C_PAIRS, P)
        vb = by_group(C_PAIRS)
        nke = by_group(C_PAIRS)
        qe = by_group(C_PAIRS)
        kd = by_group(C_PAIRS)
        ntm = by_group(H)
        ptm = by_group(H)
        tm = by_group(H)
        um = by_group(H)
        emb = Area(m.big, f.at).take(H, NB, HD)
        xm = f.take(2, H, P)
        cm = f.take(2, H, P)
        kdt = f.take(3, H, HD)
        rm = f.take(H, HD)
        em = f.take(H, HD)
        nkm = f.take(C_PAIRS, NB, NB * NS)
        state = f.take(C_PAIRS, HD)

        def head(ap, h, n):
            r = (h % 2) * HD
            return ap[r:r + HD, h // 2, 0:n]

        def at(ap, h, width, n):
            c = (h % 2) * 512 + (h // 2) * width
            return ap[:, c:c + n]

        def heads(ap, width, n):
            return ap.rearrange("p (r q c) -> p q r c", r=2, c=width)[:, 0:C_PAIRS, :, 0:n]

        def by_pair(ap):
            return ap.rearrange("p (q r) c -> p q r c", r=2)

        def half(ap, r, n):
            return ap.rearrange("p (r q c) -> p r q c", r=2, c=P)[r * HD:(r + 1) * HD, r, 0:C_PAIRS, 0:n]

        def levels(n):
            return 7 if n == P else 2

        @block.tensor
        def _(pe):
            for g, (t0, n, tt) in enumerate(GROUPS):
                tri = m.mix("tri") if n == P else m.mix("tri_s")
                if g:
                    pe.wait_ge(s["gp_ready"], g)
                    pe.wait_ge(s["kb_ready"], g)
                    pe.wait_ge(s["masked"], g)
                for h in range(H):
                    pe.matmul(at(ps1, h, P, n), m.decay[0:n, tt, h:h + 1].broadcast_to([n, P]), tri[0:n, 0:n],
                              start=True, stop=True)
                pe.matmul(ps3[0:n, 0:H], tri[0:n, 0:n], m.decay[0:n, tt, :], start=True, stop=True)
                for h in range(H):
                    mm = pe.matmul(at(ps2, h, P, n), m.beta[0:n, tt, h:h + 1].broadcast_to([n, P]),
                                   m.ident[0:n, 0:n], start=True, stop=True)
                mm.then_inc(s["ps_a"], 1)
                pe.wait_ge(s["kb_ready"], g + 1)
                pe.wait_ge(s["gcol_out"], g + 1)
                for h in range(H):
                    k = head(m.qkv[:, 3:6, t0:t0 + n], h, n)
                    pe.matmul(at(ps3, h, P, n)[0:n], k, head(kb, h, n), start=True, stop=True)
                    mm = pe.matmul(at(ps4, h, P, n)[0:n], k, head(m.qkv[:, 0:3, t0:t0 + n], h, n), start=True, stop=True)
                mm.then_inc(s["raw_ready"], 1)
            pe.wait_ge(s["masked"], 3)
            turn = 0
            last_turn = [None, None]
            for g0 in ((0, 1), (2,)):
                for lv in range(levels(GROUPS[g0[0]][1])):
                    for b, g in enumerate(g0):
                        n = GROUPS[g][1]
                        px, pt = (ps1, ps2) if b == 0 else (ps3, ps4)
                        pe.wait_ge(s["scaled"], turn + 1)
                        if last_turn[b] is not None:
                            pe.wait_ge(s["tu_done"], last_turn[b] + 1)
                        last_turn[b] = turn
                        for h in range(H):
                            mm = pe.matmul(at(px, h, P, n)[0:n], cm[0:n, b, h, 0:n], tm[g][0:n, h, 0:n], start=True, stop=True)
                        mm.then_inc(s["x_ready"], 1)
                        pe.wait_ge(s["x_out"], turn + 1)
                        for h in range(H):
                            pe.matmul(at(pt, h, P, n)[0:n], um[g][0:n, h, 0:n], xm[0:n, b, h, 0:n], start=True, stop=True)
                            mm = pe.matmul(at(px, h, P, n)[0:n], xm[0:n, b, h, 0:n], um[g][0:n, h, 0:n], start=True, stop=True)
                        mm.then_inc(s["tu_ready"], 1)
                        turn += 1
            for g, (t0, n, tt) in enumerate(GROUPS):
                pe.wait_ge(s["tu_done"], turn)
                if g:
                    pe.wait_ge(s["kd_out"], g)
                for h in range(H):
                    r = (h % 2) * HD
                    mm = pe.matmul(at(ps1, h, HD, HD)[0:n], head(kd[g][:, :, :], h, n), m.ident[r:r + HD, r:r + HD],
                                   start=True, stop=True)
                mm.then_inc(s["kd_ps"], 1)
            pe.wait_ge(s["nk_masked"], 1)
            for g, (t0, n, tt) in enumerate(GROUPS):
                if g == 0:
                    pe.wait_ge(s["kd_out"], 3)
                pe.wait_ge(s["s_out"], g + 1)
                for h in range(H):
                    r = (h % 2) * HD
                    out = at(ps2, h, HD, HD)[0:n]
                    pe.matmul(out, head(vb[g][:, :, :], h, n), m.ident[r:r + HD, r:r + HD], start=True, stop=False)
                    if n == P:
                        mm = pe.matmul(out, head(nke[g][:, :, :], h, n), state[r:r + HD, h // 2, :], start=False, stop=True)
                    else:
                        for b in range(NB):
                            mm = pe.matmul(out, nkm[r:r + HD, h // 2, b, :], m.state0[r:r + HD, A_PAIRS + h // 2, b, :],
                                           start=False, stop=(b == NB - 1))
                mm.then_inc(s["r_ps"], 1)
                pe.wait_ge(s["r_out"], g + 1)
                for h in range(H):
                    mm = pe.matmul(at(ps3, h, HD, HD)[0:n], um[g][0:n, h, 0:n], rm[0:n, h, :], start=True, stop=True)
                mm.then_inc(s["e_ps"], 1)
                pe.wait_ge(s["e_out"], g + 1)
                if g:
                    pe.wait_ge(s["act_step"], g)
                for h in range(H):
                    r = (h % 2) * HD
                    out = ps4[r:r + HD, (h // 2) * P:(h // 2) * P + n]
                    pe.matmul(out, em[0:n, h, :], ptm[g][0:n, h, 0:n], start=True, stop=False)
                    if n == P:
                        mm = pe.matmul(out, state[r:r + HD, h // 2, :], head(qe[g][:, :, :], h, n), start=False, stop=True)
                    else:
                        for b in range(NB):
                            mm = pe.matmul(out[:, NS * b:NS * b + NS], m.state0[r:r + HD, A_PAIRS + h // 2, b, :],
                                           head(qe[g][:, :, :], h, n)[:, NS * b:NS * b + NS], start=False, stop=(b == NB - 1))
                mm.then_inc(s["o_ps"], 1)
                if n == P:
                    for h in range(H):
                        r = (h % 2) * HD
                        mm = pe.matmul(ps1[r:r + HD, (h // 2) * HD:(h // 2 + 1) * HD], kdt[0:n, g, h, :], em[0:n, h, :],
                                       start=True, stop=True)
                    mm.then_inc(s["s_ps"], 1)
                else:
                    pe.wait_ge(s["em_ready"], 1)
                    for h in range(H):
                        r = (h % 2) * HD
                        bank = (ps1[:, 0:512], ps1[:, 512:1024], ps2[:, 0:512])[h // 2]
                        mm = pe.matmul(bank[r:r + HD, :], kdt[0:n, g, h, :], emb[0:n, h, :, :], start=True, stop=True)
                    mm.then_inc(s["s_ps"], 1)

        @block.scalar
        def _(act):
            for g, (t0, n, tt) in enumerate(GROUPS):
                act.wait_ge(s["ps_a"], g + 1)
                for r in range(2):
                    i = act.activation(gp[r * HD:(r + 1) * HD, :, 0:n], half(ps1, r, n), ACT.Copy)
                i.then_inc(s["gp_ready"], 1)
                act.wait_ge(s["gp_ready"], g + 1)
                act.activation(eg[g][:, :, 0:n], gp[:, :, 0:n], ACT.Exp).then_inc(s["eg_ready"], 1)
                act.wait_ge(s["dt_ready"], g + 1)
                act.activation(dt[0:n, :, 0:n], dt[0:n, :, 0:n], ACT.Exp).then_inc(s["dte_ready"], 1)
                act.wait_ge(s["glast_ready"], g + 1)
                act.activation(gl[:, :, 0:n], gl[:, :, 0:n], ACT.Exp).then_inc(s["glast_exp"], 1)
                act.wait_ge(s["kd_mul"], g + 1)
            turn = 0
            for g0 in ((0, 1), (2,)):
                for lv in range(levels(GROUPS[g0[0]][1])):
                    for b, g in enumerate(g0):
                        n = GROUPS[g][1]
                        px = ps1 if b == 0 else ps3
                        act.wait_ge(s["x_ready"], turn + 1)
                        act.activation(by_pair(xm[0:n, b, :, 0:n]), heads(px, P, n)[0:n], ACT.Copy).then_inc(s["x_out"], 1)
                        turn += 1
            for g, (t0, n, tt) in enumerate(GROUPS):
                act.wait_ge(s["kd_ps"], g + 1)
                act.activation(by_pair(kdt[0:n, g, :, :]), heads(ps1, HD, HD)[0:n], ACT.Copy).then_inc(s["kd_out"], 1)
            for g, (t0, n, tt) in enumerate(GROUPS):
                act.wait_ge(s["r_ps"], g + 1)
                act.activation(by_pair(rm[0:n, :, :]), heads(ps2, HD, HD)[0:n], ACT.Copy).then_inc(s["r_out"], 1)
                act.wait_ge(s["e_ps"], g + 1)
                if g:
                    act.wait_ge(s["s_ps"], g)
                act.activation(by_pair(em[0:n, :, :]), heads(ps3, HD, HD)[0:n], ACT.Copy).then_inc(s["e_out"], 1)
                act.wait_ge(s["o_ps"], g + 1)
                i = act.activation(m.mixed[:, 5:8, t0:t0 + n],
                                   ps4[:, 0:3 * P].rearrange("p (q c) -> p q c", q=3)[:, :, 0:n], ACT.Copy)
                i.then_inc(s["act_step"], 1)
                act.wait_ge(s["act_step"], g + 1)

        @block.vector
        def _(v):
            link = Chain(v, s["step"])
            for g, (t0, n, tt) in enumerate(GROUPS):
                neg = m.mix("neg") if n == P else m.mix("neg_s")
                last = n - 1
                v.wait_ge(s["ps_a"], g + 1)
                v.tensor_copy(gcol[0:n, g, :], ps3[0:n, 0:H]).then_inc(s["gcol_out"], 1)
                v.wait_ge(s["gcol_out"], g + 1)
                v.wait_ge(s["gp_ready"], g + 1)
                for h in range(H):
                    i = v.scalar_tensor_tensor(dt[0:n, h, 0:n], at(ps1, h, P, n)[0:n], gcol[0:n, g, h:h + 1],
                                               neg[0:n, 0:n], ALU.subtract, ALU.add)
                i.then_inc(s["dt_ready"], 1)
                for r in range(2):
                    rows = slice(r * HD, (r + 1) * HD)
                    link(v.tensor_tensor(kb[rows, :, 0:n], m.qkv[rows, 3:6, t0:t0 + n], half(ps2, r, n), ALU.mult))
                    link(v.tensor_tensor(vb[g][rows, :, 0:n], m.qkv[rows, 6:9, t0:t0 + n], half(ps2, r, n), ALU.mult))
                v.sem_inc(s["kb_ready"], 1)
                v.wait_ge(s["gp_ready"], g + 1)
                if n == P:
                    link(v.tensor_tensor(gl[:, :, 0:n], gp[:, :, last:n].broadcast_to([P, C_PAIRS, n]), gp[:, :, 0:n], ALU.subtract))
                else:
                    for q in range(C_PAIRS):
                        a = gp[:, q, 0:n].rearrange("p (b s) -> p b s", b=NB)
                        link(v.tensor_tensor(gl[:, q, 0:n].rearrange("p (b s) -> p b s", b=NB),
                                             a[:, :, NS - 1:NS].broadcast_to([P, NB, NS]), a, ALU.subtract))
                v.sem_inc(s["glast_ready"], 1)
                v.wait_ge(s["eg_ready"], g + 1)
                for q in range(C_PAIRS):
                    link(v.scalar_tensor_tensor(nke[g][:, q, 0:n], kb[:, q, 0:n], -1.0, eg[g][:, q, 0:n], ALU.mult, ALU.mult))
                link(v.tensor_tensor(qe[g][:, :, 0:n], m.qkv[:, 0:3, t0:t0 + n], eg[g][:, :, 0:n], ALU.mult))
                v.wait_ge(s["glast_exp"], g + 1)
                v.tensor_tensor(kd[g][:, :, 0:n], m.qkv[:, 3:6, t0:t0 + n], gl[:, :, 0:n], ALU.mult).then_inc(s["kd_mul"], 1)
                v.wait_ge(s["raw_ready"], g + 1)
                v.wait_ge(s["dte_ready"], g + 1)
                link(v.tensor_tensor(by_pair(ntm[g][0:n, :, 0:n]), heads(ps3, P, n)[0:n], by_pair(dt[0:n, :, 0:n]), ALU.mult))
                link(v.tensor_tensor(by_pair(ptm[g][0:n, :, 0:n]), heads(ps4, P, n)[0:n], by_pair(dt[0:n, :, 0:n]), ALU.mult))
                link(v.tensor_copy(tm[g][0:n, :, 0:n], spread(m.ident[0:n, 0:n], 1, H)))
                link(v.tensor_copy(um[g][0:n, :, 0:n], spread(m.ident[0:n, 0:n], 1, H)))
                v.sem_inc(s["masked"], 1)
            turn = 0
            order = []
            for g0 in ((0, 1), (2,)):
                for lv in range(levels(GROUPS[g0[0]][1])):
                    for b, g in enumerate(g0):
                        order.append((lv, b, g))

            def mask(turn):
                lv, b, g = order[turn]
                n = GROUPS[g][1]
                if turn >= 2:
                    v.wait_ge(s["x_ready"], turn - 1 if order[turn - 1][1] != b else turn)
                link(v.tensor_tensor(cm[0:n, b, :, 0:n], ntm[g][0:n, :, 0:n],
                                     spread(m.mix("levels")[0:n, lv * P:lv * P + n], 1, H), ALU.mult))
                v.sem_inc(s["scaled"], 1)

            mask(0)
            mask(1)
            for turn, (lv, b, g) in enumerate(order):
                n = GROUPS[g][1]
                px, pt = (ps1, ps2) if b == 0 else (ps3, ps4)
                v.wait_ge(s["tu_ready"], turn + 1)
                link(v.tensor_tensor(by_pair(tm[g][0:n, :, 0:n]), by_pair(tm[g][0:n, :, 0:n]), heads(pt, P, n)[0:n], ALU.subtract))
                link(v.tensor_tensor(by_pair(um[g][0:n, :, 0:n]), by_pair(um[g][0:n, :, 0:n]), heads(px, P, n)[0:n], ALU.subtract))
                v.sem_inc(s["tu_done"], 1)
                if turn + 2 < len(order):
                    mask(turn + 2)
            for q in range(C_PAIRS):
                link(v.tensor_tensor(nkm[:, q, :, :], spread(nke[2][:, q, 0:NB * NS], 1, NB),
                                     m.mix("batch_cols").rearrange("p (b t) -> p b t", b=NB), ALU.mult))
            v.sem_inc(s["nk_masked"], 1)
            link(v.memset(state[:, :, :], 0.0))
            v.sem_inc(s["s_out"], 1)
            for g, (t0, n, tt) in enumerate(GROUPS):
                if n == P:
                    v.wait_ge(s["s_ps"], g + 1)
                    for q in range(C_PAIRS):
                        link(v.scalar_tensor_tensor(state[:, q, :], state[:, q, :], eg[g][:, q, n - 1:n],
                                                    ps1[:, q * HD:(q + 1) * HD], ALU.mult, ALU.add))
                    if g == 1:
                        link(v.tensor_copy(m.states[:, A_PAIRS:, 0, :], state[:, :, :]))
                    v.sem_inc(s["s_out"], 1)
                else:
                    v.wait_ge(s["e_out"], g + 1)
                    for h in range(H):
                        link(v.tensor_tensor(emb[0:n, h, :, :], spread(em[0:n, h, :], 1, NB),
                                             spread(m.mix("batch_rows")[0:n, :], 2, HD), ALU.mult))
                    v.sem_inc(s["em_ready"], 1)
                    v.wait_ge(s["s_ps"], g + 1)
                    for q in range(C_PAIRS):
                        bank = (ps1[:, 0:512], ps1[:, 512:1024], ps2[:, 0:512])[q].rearrange("p (b v) -> p b v", b=NB)
                        last = eg[g][:, q, 0:n].rearrange("p (b s) -> p b s", b=NB)[:, :, NS - 1:NS].broadcast_to([P, NB, HD])
                        new = m.states[:, A_PAIRS + q, 1:, :]
                        link(v.tensor_tensor(new, m.state0[:, A_PAIRS + q, :, :], last, ALU.mult))
                        link(v.tensor_tensor(new, new, bank, ALU.add))


def residual(link, m, which, psum, tmp):
    v, gate = link.eng, (3 * which + 2) * KD
    for k in range(KD):
        link(v.scalar_tensor_tensor(m.x[:, k, 0:NP], psum[:, k, 0:NP], m.mod[:, gate + k, 0:1], m.x[:, k, 0:NP],
                                    ALU.mult, ALU.add))
    link(v.tensor_tensor(batched(tmp), batched(psum[:, :, NP:NT]), spread(m.mod[:, gate:gate + KD, 1:], 3, NS), ALU.mult))
    link(v.tensor_tensor(m.x[:, :, NP:NT], m.x[:, :, NP:NT], tmp, ALU.add))


def output_block(nc, m, l, stream, small_out, state_out):
    names = ("step squares_ready sums_ready root_ready normed summed x_ready squares2 sums2 root2 h_ready query_out "
             "outs_saved states_saved")
    tiles = (0, 1, 5, 6, 7)
    with signals(nc, names) as s, nc.psum_tensor("ps_w", [P, 8, 512], F32) as ps, nc.Block() as block:
        f = Area(m.big, m.free)
        sq = f.take(5, NT)
        tmp = f.take(KD, NB * NS)

        @block.sync
        def _(sp):
            sp.dma_start(small_out[l, :, :], m.outs[:, :]).then_inc(s["outs_saved"], 16)
            sp.dma_start(state_out[l, :, :], m.states.rearrange("p a b c -> p (a b c)")).then_inc(s["states_saved"], 16)
            load_tiles(sp, m, stream, l, T_OUT + RING, T_U + RING)
            sp.wait_ge(s["outs_saved"], 16)
            sp.wait_ge(s["states_saved"], 16)

        @block.scalar
        def _(act):
            act.activation(sq[:, 0:2, :], m.mixed[:, 0:2, :], ACT.Square)
            act.activation(sq[:, 2:5, :], m.mixed[:, 5:8, :], ACT.Square).then_inc(s["squares_ready"], 1)
            act.wait_ge(s["sums_ready"], 1)
            act.activation(sq[:, :, :], ps[:, 0:5, 0:NT], ACT.Sqrt, bias=m.eps, scale=1.0 / HD).then_inc(s["root_ready"], 1)
            act.wait_ge(s["x_ready"], 1)
            act.activation(m.square[:, :, :], m.x[:, :, :], ACT.Square).then_inc(s["squares2"], 1)
            act.wait_ge(s["sums2"], 1)
            act.activation(m.rms[:, :], ps[:, 0, 0:NT], ACT.Sqrt, bias=m.eps, scale=1.0 / D).then_inc(s["root2"], 1)
            for h in range(HEADS):
                m.wait_done(act, T_QUERY + h)
                act.activation(m.query[:, h, :], ps[:, (h + 1) % 8, 0:NT], ACT.Copy).then_inc(s["query_out"], 1)
            act.wait_ge(s["query_out"], HEADS)

        @block.vector
        def _(v):
            link = Chain(v, s["step"])
            v.wait_ge(s["root_ready"], 1)
            link(v.reciprocal(sq[:, :, :], sq[:, :, :]))
            for n, t in enumerate(tiles):
                g = m.par("a_norm") if t < 2 else m.par("dn_norm")
                gate = m.zact[:, 6 + t, :] if t < 2 else m.zact[:, 11 + t - 5, :]
                link(v.scalar_tensor_tensor(m.mixed[:, t, :], m.mixed[:, t, :], g, sq[:, n, :], ALU.mult, ALU.mult))
                link(v.tensor_tensor(m.mixed[:, t, :], m.mixed[:, t, :], gate, ALU.mult))
            v.sem_inc(s["normed"], 1)
            m.wait_done(v, T_QUERY - 4)
            m.wait_done(v, T_QUERY - 3)
            m.wait_done(v, T_QUERY - 2)
            m.wait_done(v, T_QUERY - 1)
            residual(link, m, 0, ps, tmp)
            v.sem_inc(s["x_ready"], 1)
            v.wait_ge(s["root2"], 1)
            link(v.reciprocal(m.rms[:, :], m.rms[:, :]))
            modulate(link, m, 1, s["h_ready"])
            v.wait_ge(s["h_ready"], 1)

        @block.tensor
        def _(pe):
            pe.wait_ge(s["squares_ready"], 1)
            for n in range(5):
                mm = pe.matmul(ps[:, n, 0:NT], m.mix("block_ones"), sq[:, n, :], start=True, stop=True)
            mm.then_inc(s["sums_ready"], 1)
            pe.wait_ge(s["normed"], 1)
            for n in range(KD):
                m.wait_tile(pe, T_OUT + n)
                w = m.tile(T_OUT + n)
                for k in range(KD):
                    mm = pe.matmul(ps[:, n, 0:NT], w[:, k, :], m.mixed[:, k, :], start=(k == 0), stop=(k == KD - 1))
                mm.then_inc(m.done[(T_OUT + n) % RING], 1)
            pe.wait_ge(s["squares2"], 1)
            for k in range(KD):
                mm = pe.matmul(ps[:, 0, 0:NT], m.ones, m.square[:, k, :], start=(k == 0), stop=(k == KD - 1))
            mm.then_inc(s["sums2"], 1)
            pe.wait_ge(s["h_ready"], 1)
            for h in range(HEADS):
                m.wait_tile(pe, T_QUERY + h)
                w = m.tile(T_QUERY + h)
                for k in range(KD):
                    mm = pe.matmul(ps[:, (h + 1) % 8, 0:NT], w[:, k, :], m.h[:, k, :], start=(k == 0), stop=(k == KD - 1))
                mm.then_inc(m.done[(T_QUERY + h) % RING], 1)


def experts_block(nc, m, l, stream):
    TT = 96
    HALF = (T_V - T_U) // RING * 5 // 8
    names = "step score_ps score_out found act_out"
    with signals(nc, names) as s, nc.psum_tensor("ps_s", [P, 2048], F32) as ps_s, \
            nc.psum_tensor("ps_u", [P, 4, 512], F32) as ps_u, nc.Block() as block:

        @block.sync
        def _(sp):
            load_many(sp, m, stream, l, T_U + RING, T_V + RING)

        @block.tensor
        def _(pe):
            for tt in range(3):
                if tt:
                    pe.wait_ge(s["score_out"], tt)
                for h in range(HEADS):
                    for side in range(2):
                        r, c = side * 64, (side * HEADS + h) * NKEYS
                        mm = pe.matmul(ps_s[0:TT, c:c + NKEYS], m.query[r:r + 64, h, tt * TT:(tt + 1) * TT],
                                       m.par("keys")[r:r + 64, :], start=True, stop=True)
                mm.then_inc(s["score_ps"], 1)
            with pe.Fori(0, NKEYS // RING) as g:
                for j in range(RING):
                    t = T_U + j
                    pe.wait_ge(m.loaded[t % RING], g * 16 + 16 * (t // RING + 1))
                    pe.wait_ge(s["act_out"], g * RING + (j + 1))
                    w = m.tile(t)
                    for k in range(KD):
                        mm = pe.matmul(ps_u[:, j, 0:NT], w[:, k, :], m.h[:, k, :], start=(k == 0), stop=(k == KD - 1))
                    mm.then_inc(m.done[t % RING], 1)

        @block.scalar
        def _(act):
            act.sem_inc(s["act_out"], RING)
            for tt in range(3):
                act.wait_ge(s["score_ps"], tt + 1)
                act.activation(m.score[0:TT, tt, :, :].rearrange("p a b -> p (a b)"), ps_s[0:TT, :], ACT.Copy).then_inc(
                    s["score_out"], 1)
            for a, b in ((0, HALF), (HALF, NKEYS // RING)):
                with act.Fori(a, b) as g:
                    for j in range(RING):
                        t = T_U + j
                        act.wait_ge(m.done[t % RING], g + (t // RING + 1))
                        act.activation(m.act[:, ds(g * RING + j, 1), :].squeeze(1), ps_u[:, j, 0:NT],
                                       ACT.Gelu_apprx_tanh).then_inc(s["act_out"], 1)
                if a == 0:
                    act.wait_ge(s["found"], 3)

        @block.vector
        def _(v):
            link = Chain(v, s["step"])
            sides = m.score[0:TT, :, :, :]
            r = slice(0, TT)

            def top16(values, best, index):
                link(v.max(best[:, 0:8], values))
                v.max_index(index[:, 0:8], best[:, 0:8], values)
                link(v.match_replace(values, best[:, 0:8], values, -3.4e38))
                link(v.max(best[:, 8:16], values))
                link(v.max_index(index[:, 8:16], best[:, 8:16], values))

            for tt in range(3):
                v.wait_ge(s["score_out"], tt + 1)
                for n in range(2 * HEADS):
                    top16(sides[:, tt, n, :], m.best[r, n, :], m.besti[r, n, :])
                link(v.tensor_copy(m.bestf[r, :, :], m.besti[r, :, :]))
                b = m.best[r, :, :].rearrange("p (s h) k -> p s h k", s=2)
                c = m.cand[r, :, :].rearrange("p h (a b) -> p h a b", a=TOPK)
                link(v.tensor_tensor(c, spread(b[:, 0, :, :], 3, TOPK), spread(b[:, 1, :, :], 2, TOPK), ALU.add))
                score = m.sel[r, 2, tt, :].rearrange("p (h k) -> p h k", h=HEADS)
                pos = m.pos[r, :].rearrange("p (h k) -> p h k", h=HEADS)
                for h in range(HEADS):
                    top16(m.cand[r, h, :], score[:, h, :], pos[:, h, :])
                link(v.tensor_tensor(m.posf[r, :].rearrange("p (h k) -> p h k", h=HEADS), score,
                                     score[:, :, 0:1].broadcast_to([TT, HEADS, TOPK]), ALU.subtract))
                link(v.tensor_copy(m.sel[r, 2, tt, :], m.posf[r, :]))
                for side, op, arg in ((0, ALU.logical_shift_right, 4), (1, ALU.bitwise_and, 15)):
                    link(v.tensor_single_scalar(m.posp[r, :], m.pos[r, :], arg, op))
                    link(v.tensor_copy(m.posf[r, :], m.posp[r, :]))
                    link(v.tensor_tensor(m.hit[r, :, :], spread(m.posf[r, :], 2, TOPK), spread(m.iota[r, 0:TOPK], 1, HEADS * TOPK),
                                         ALU.is_equal))
                    keys = m.bestf[r, side * HEADS:(side + 1) * HEADS, :]
                    hit = m.hit[r, :, :].rearrange("p (h k) a -> p h k a", h=HEADS)
                    link(v.tensor_tensor(hit, hit, spread(keys, 2, TOPK), ALU.mult))
                    link(v.tensor_reduce(m.sel[r, side, tt, :], m.hit[r, :, :], AX, ALU.add))
                v.sem_inc(s["found"], 1)


def gates_block(nc, m, l):
    TT = 96
    GROUP = 4
    TURN = 12
    names = "step exp_ready gates_ready turned turned_out act_step first_ready second_ready cols_ready gate_ps weighted held"
    with signals(nc, names) as s, nc.psum_tensor("ps_t", [P, 2, 512], F32) as ps_t, \
            nc.psum_tensor("ps_g", [P, 3, GROUP, P], F32) as ps_g, nc.Block() as block:
        e = m.sel[0:TT, 2, :, :].rearrange("p t (h k) -> p t h k", h=HEADS)
        total = m.rms[0:TT, 0:3 * HEADS].rearrange("p (t h) -> p t h", h=HEADS)
        half = TURN // 2

        @block.scalar
        def _(act):
            act.activation(m.sel[0:TT, 2, :, :], m.sel[0:TT, 2, :, :], ACT.Exp).then_inc(s["exp_ready"], 1)
            for kind in range(3):
                act.wait_ge(s["turned"], kind + 1)
                act.activation(m.selT[:, kind, :], ps_t[:, kind % 2, 0:NT], ACT.Copy).then_inc(s["turned_out"], 1)
            act.wait_ge(s["turned_out"], 3)

        @block.tensor
        def _(pe):
            pe.sem_inc(s["gate_ps"], 3)
            for kind in range(3):
                if kind == 2:
                    pe.wait_ge(s["turned_out"], 1)
                    pe.wait_ge(s["gates_ready"], 1)
                for tt in range(3):
                    mm = pe.transpose(ps_t[:, kind % 2, tt * TT:(tt + 1) * TT], m.sel[0:TT, kind, tt, :], m.ident[0:TT, 0:TT])
                mm.then_inc(s["turned"], 1)
            with pe.Fori(0, NT // TURN) as i:
                for g in range(TURN // GROUP):
                    pe.wait_ge(s["weighted"], i * 3 + (g + 1))
                    for c in range(GROUP):
                        j = g * GROUP + c
                        if c % 2 == 0:
                            pe.wait_ge(s["first_ready"], i * half + (j // 2 + 1 + 3))
                            pe.wait_ge(s["second_ready"], i * half + (j // 2 + 1 + 3))
                        mm = pe.matmul(ps_g[:, g, c, :], m.onehot[:, 0, j % 6, :], m.onehot[:, 1, j % 6, :], start=True, stop=True)
                        if c % 2:
                            mm.then_inc(s["gate_ps"], 1)

        @block.gpsimd
        def _(pool):
            pool.sem_inc(s["second_ready"], 3)
            pool.wait_ge(s["turned_out"], 3)
            with pool.Fori(0, NT // TURN) as i:
                hold(pool, s["second_ready"], i * half + 3, s["held"])
                pool.tensor_copy(m.cols[:, :], m.selT[:, 1, ds(i * TURN, TURN)]).then_inc(s["cols_ready"], 1)
                hold(pool, s["cols_ready"], i + 1, s["held"])
                for j in range(TURN):
                    if j % 2 == 0:
                        hold(pool, s["gate_ps"], i * half + (j // 2 + 1), s["held"])
                    o = pool.tensor_scalar(m.onehot[:, 1, j % 6, :], m.iota, m.cols[:, j:j + 1], None, ALU.is_equal)
                    if j % 2:
                        o.then_inc(s["second_ready"], 1)

        @block.vector
        def _(v):
            link = Chain(v, s["step"])
            v.wait_ge(s["exp_ready"], 1)
            link(v.tensor_reduce(total, e, AX, ALU.add))
            link(v.reciprocal(total, total))
            v.tensor_tensor(e, e, spread(total, 3, TOPK), ALU.mult).then_inc(s["gates_ready"], 1)
            v.wait_ge(s["turned_out"], 3)
            v.sem_inc(s["first_ready"], 3)
            v.sem_inc(s["weighted"], 3)

            def onehots(i, j):
                v.wait_ge(s["gate_ps"], i * half + (j // 2 + 1))
                for c in (j, j + 1):
                    o = v.tensor_scalar(m.onehot[:, 0, c % 6, :], m.iota, m.selT[:, 0, ds(i * TURN + c, 1)],
                                        m.selT[:, 2, ds(i * TURN + c, 1)], ALU.is_equal, ALU.mult)
                o.then_inc(s["first_ready"], 1)

            with v.Fori(0, NT // TURN) as i:
                for g in range(TURN // GROUP):
                    onehots(i, g * GROUP)
                    onehots(i, g * GROUP + 2)
                    v.wait_ge(s["gate_ps"], i * half + (2 * g + 2 + 3))
                    a = m.act[:, :, ds(i * TURN + g * GROUP, GROUP)]
                    v.tensor_tensor(a, a, ps_g[:, g, :, :].rearrange("p t e -> p e t"), ALU.mult).then_inc(s["weighted"], 1)


def combine_block(nc, m, l, stream):
    names = "step zeroed summed"
    with signals(nc, names) as s, nc.psum_tensor("ps_y", [P, 8, 512], F32) as ps, nc.Block() as block:
        tmp = m.h[:, :, 0:NB * NS]
        zero = m.sel[:, 0, 0, :]

        @block.sync
        def _(sp):
            load_many(sp, m, stream, l, T_V + RING, TILES)

        @block.tensor
        def _(pe):
            pe.wait_ge(s["zeroed"], 1)
            for k in range(KD):
                pe.matmul(ps[:, k, 0:NT], zero, m.h[:, k, :], start=True, stop=False)
            with pe.Fori(0, NKEYS // RING) as g:
                for j in range(RING):
                    t = T_V + j
                    pe.wait_ge(m.loaded[t % RING], g * 16 + 16 * (t // RING + 1))
                    w = m.tile(t)
                    for k in range(KD):
                        mm = pe.matmul(ps[:, k, 0:NT], w[:, k, :], m.act[:, ds(g * RING + j, 1), :].squeeze(1),
                                       start=False, stop=False)
                    mm.then_inc(m.done[t % RING], 1)
            for k in range(KD):
                mm = pe.matmul(ps[:, k, 0:NT], zero, m.h[:, k, :], start=False, stop=True)
            mm.then_inc(s["summed"], 1)

        @block.vector
        def _(v):
            link = Chain(v, s["step"])
            v.memset(zero, 0.0).then_inc(s["zeroed"], 1)
            v.wait_ge(s["summed"], 1)
            residual(link, m, 1, ps, tmp)


def final_block(nc, m, y_out):
    with signals(nc, "step squares_ready sums_ready root_ready y_ready saved") as s, \
            nc.psum_tensor("ps_f", [P, 512], F32) as ps, nc.Block() as block:
        @block.scalar
        def _(act):
            act.activation(m.square[:, :, :], m.x[:, :, :], ACT.Square).then_inc(s["squares_ready"], 1)
            act.wait_ge(s["sums_ready"], 1)
            act.activation(m.rms[:, :], ps[:, 0:NT], ACT.Sqrt, bias=m.eps, scale=1.0 / D).then_inc(s["root_ready"], 1)

        @block.tensor
        def _(pe):
            pe.wait_ge(s["squares_ready"], 1)
            for k in range(KD):
                mm = pe.matmul(ps[:, 0:NT], m.ones, m.square[:, k, :], start=(k == 0), stop=(k == KD - 1))
            mm.then_inc(s["sums_ready"], 1)

        @block.vector
        def _(v):
            link = Chain(v, s["step"])
            v.wait_ge(s["root_ready"], 1)
            link(v.reciprocal(m.rms[:, :], m.rms[:, :]))
            for k in range(KD):
                i = v.scalar_tensor_tensor(m.h[:, k, :], m.x[:, k, :], m.par("final")[:, k:k + 1], m.rms[:, :],
                                           ALU.mult, ALU.mult)
            i.then_inc(s["y_ready"], 1)

        @block.sync
        def _(sp):
            sp.wait_ge(s["y_ready"], 1)
            sp.dma_start(y_out, m.h[:, :, :]).then_inc(s["saved"], 16)
            sp.wait_ge(s["saved"], 16)


def build(nc, stream, small_in, mixc_in, keep_in, state_in, x_in, c_in, y_out, small_out, state_out):
    with ExitStack() as ctx:
        m = Memory(nc, ctx)
        setup_block(nc, m, x_in, c_in, keep_in)
        with nc.Fori(0, DEPTH) as l:
            project_block(nc, m, l, stream, small_in, mixc_in, state_in)
            local_block(nc, m, l, stream)
            hgrn_block(nc, m, l)
            delta_block(nc, m, l)
            output_block(nc, m, l, stream, small_out, state_out)
            experts_block(nc, m, l, stream)
            gates_block(nc, m, l)
            combine_block(nc, m, l, stream)
            for sem in m.loaded + m.done:
                nc.sync.sem_clear(sem)
            nc.all_engine_barrier()
        final_block(nc, m, y_out)


def host_layout(a):
    import numpy as np
    f = np.float32

    def cols(w):
        n = w.shape[2] // P
        return w.reshape(DEPTH, KD, P, n, P).transpose(0, 3, 2, 1, 4).reshape(DEPTH, n, P, D)

    stream = np.zeros((DEPTH, TILES, P, D), f)
    stream[:, T_ADA:T_IN] = cols(a["w_ada"])
    stream[:, T_IN:T_BETA] = cols(a["w_in"][:, :, :IN_TILES * P])[:, Z_ORDER]
    stream[:, T_BETA].reshape(DEPTH, P, KD, P)[:, :, :, :12] = \
        a["w_in"][:, :, IN_TILES * P:].reshape(DEPTH, KD, P, 12).transpose(0, 2, 1, 3)
    gate = stream[:, T_GATE].reshape(DEPTH, P, 8, P)
    for g, name in enumerate(("lru_wa", "lru_wx")):
        for t in range(B_TILES):
            for r in range(2):
                rows = slice(r * HD, (r + 1) * HD)
                gate[:, rows, g * B_TILES + t, rows] = a[name][:, 2 * t + r]
    stream[:, T_OUT:T_QUERY] = cols(a["w_out"])
    stream[:, T_QUERY:T_U] = cols(a["peer_wq"])
    stream[:, T_U:T_V] = a["peer_u"].reshape(DEPTH, NKEYS, NKEYS, KD, P).transpose(0, 2, 4, 3, 1).reshape(DEPTH, NKEYS, P, D)
    stream[:, T_V:] = a["peer_v"].reshape(DEPTH, NKEYS, NKEYS, D).transpose(0, 2, 1, 3)

    small = np.zeros((DEPTH, P, SMALL_W), f)

    def put(name, value):
        small[:, :, SMALL[name][0]:SMALL[name][1]] = value

    def feat(v):
        return v.reshape(DEPTH, -1, P).transpose(0, 2, 1)

    put("norm1", feat(a["norm1_g"]))
    put("norm2", feat(a["norm2_g"]))
    put("b_ada", feat(a["b_ada"]))
    put("lru_w", a["lru_conv_w"].reshape(DEPTH, CONV, B_TILES, P).transpose(0, 3, 2, 1).reshape(DEPTH, P, -1))
    put("lru_b", feat(a["lru_conv_b"]))
    put("dn_w", a["dn_conv_w"].reshape(DEPTH, CONV, 9, P).transpose(0, 3, 2, 1).reshape(DEPTH, P, -1))
    put("ba", feat(a["lru_ba"]))
    put("bx", feat(a["lru_bx"]))
    put("lru_L", feat(a["lru_L"]))
    put("a_norm", np.concatenate([a["a_norm_g"]] * 2, 1)[:, :, None])
    put("dn_norm", np.concatenate([a["dn_norm_g"]] * 2, 1)[:, :, None])
    put("a_log", a["dn_A_log"][:, None, :])
    put("dt_bias", a["dn_dt_bias"][:, None, :])
    put("final", a["final_norm_g"].reshape(KD, P).T[None])
    put("lb", np.concatenate([a["lb_param"][n].reshape(A_PAIRS, P).T for n in range(DEPTH)], 1)[None])
    put("lb_on", (np.arange(DEPTH) > 0).astype(f)[:, None, None])
    put("keys", np.concatenate([a["peer_k1"], a["peer_k2"]], 2).transpose(0, 2, 1))
    put("lru_h", a["state_lru_h"].reshape(DEPTH, NB, B_TILES, P).transpose(0, 3, 2, 1).reshape(DEPTH, P, -1))
    for name, key, n in (("lru_conv", "state_lru_conv", B_TILES), ("dn_conv", "state_dn_conv", 9)):
        put(name, a[key].reshape(DEPTH, NB, CONV - 1, n, P).transpose(0, 4, 3, 1, 2).reshape(DEPTH, P, -1))

    mixc = np.zeros((P, MIXC_W), f)

    def const(name, value):
        v = np.asarray(value, f)
        mixc[:v.shape[0], MIXC[name][0]:MIXC[name][1]] = v

    j, i = np.arange(P)[:, None], np.arange(P)[None, :]
    const("block_ones", j // HD == i // HD)
    const("levels", np.concatenate([(j >> (b + 1) == i >> (b + 1)) & ((j >> b) % 2 == 0) & ((i >> b) % 2 == 1)
                                    for b in range(7)], 1))
    same = (j // NS == i // NS) & (j <= i)
    const("tri", j <= i)
    const("tri_s", same[:32, :32])
    const("neg", np.where(j <= i, 0.0, -1e30))
    const("neg_s", np.where(same, 0.0, -1e30)[:32, :32])
    const("block_rows", j // 8 == np.arange(P // 8)[None, :])
    tok = np.arange(NB * NS) // NS
    const("batch_cols", np.tile((np.arange(NB)[:, None] == tok[None, :]).reshape(1, -1), (P, 1)))
    const("batch_rows", tok[:, None] == np.arange(NB)[None, :])
    keep = np.concatenate([np.eye(P), np.ones((P, P)), np.tile(np.arange(P), (P, 1)), np.full((P, 1), EPS)], 1).astype(f)

    def heads(v, n):
        return v.reshape(DEPTH, NB, n, 2, HD, HD).transpose(0, 3, 4, 2, 1, 5).reshape(DEPTH, P, -1)

    state = np.concatenate([heads(a["state_hgrn"], A_PAIRS), heads(a["state_dn"], C_PAIRS)], 2)
    x = np.concatenate([a["x_prompt"].reshape(NP, D), a["x_sample"].reshape(NB * NS, D)], 0)
    c = np.concatenate([a["c_prompt"], a["c_sample"]], 0)
    return {"stream": stream, "small": small, "mixc": mixc, "keep": keep, "state": np.ascontiguousarray(state),
            "x": np.ascontiguousarray(x.reshape(NT, KD, P).transpose(2, 1, 0)),
            "c": np.ascontiguousarray(c.reshape(1 + NB, KD, P).transpose(2, 1, 0))}


OUTPUTS = {"y": (P, KD, NT), "small_out": (DEPTH, P, OUTS_W), "state_out": (DEPTH, P, STATE_W)}


def host_outputs(r):
    import numpy as np
    y = r["y"].transpose(2, 1, 0).reshape(NT, D)
    so = {k: r["small_out"][:, :, a:b] for k, (a, b) in OUTS.items()}
    st = r["state_out"].reshape(DEPTH, 2, HD, A_PAIRS + C_PAIRS, 1 + NB, HD).transpose(0, 4, 3, 1, 2, 5)

    def heads(b0, b1, q0, q1):
        v = st[:, b0:b1, q0:q1]
        return np.ascontiguousarray(v.reshape(DEPTH, b1 - b0, 2 * (q1 - q0), HD, HD))

    def conv(v, n, nb):
        return np.ascontiguousarray(v.reshape(DEPTH, P, n, nb, 3).transpose(0, 3, 4, 2, 1).reshape(DEPTH, nb, 3, n * P))

    def vec(v, nb):
        return np.ascontiguousarray(v.reshape(DEPTH, P, B_TILES, nb).transpose(0, 3, 2, 1).reshape(DEPTH, nb, B_TILES * P))

    ap, cp = A_PAIRS, A_PAIRS + C_PAIRS
    return (np.ascontiguousarray(y[:NP].reshape(1, NP, D)), np.ascontiguousarray(y[NP:].reshape(NB, NS, D)),
            heads(0, 1, 0, ap), vec(so["p_h"], 1), conv(so["p_lc"], B_TILES, 1), heads(0, 1, ap, cp), conv(so["p_dc"], 9, 1),
            heads(1, 1 + NB, 0, ap), vec(so["s_h"], NB), conv(so["s_lc"], B_TILES, NB), heads(1, 1 + NB, ap, cp),
            conv(so["s_dc"], 9, NB))


def kernel(**inputs):
    import numpy as np
    import concourse.bacc as bacc
    from concourse.bass_utils import run_bass_kernel_spmd

    arrays = host_layout({k: np.asarray(v) for k, v in inputs.items()})
    nc = bacc.Bacc("TRN2", target_bir_lowering=False, num_devices=1)
    ins = [nc.dram_tensor(f"in_{k}", v.shape, F32, kind="ExternalInput").ap() for k, v in arrays.items()]
    outs = [nc.dram_tensor(f"out_{k}", v, F32, kind="ExternalOutput").ap() for k, v in OUTPUTS.items()]
    build(nc, *ins, *outs)
    r = run_bass_kernel_spmd(nc, [{f"in_{k}": v for k, v in arrays.items()}], core_ids=[0]).results[0]
    return host_outputs({k: r[f"out_{k}"] for k in OUTPUTS})
```

```python
from contextlib import ExitStack, contextmanager

import concourse.bass as bass
from concourse import mybir

F32 = mybir.dt.float32
BF16 = mybir.dt.bfloat16
F32R = mybir.dt.float32r
U32 = mybir.dt.uint32
ALU = mybir.AluOpType
ACT = mybir.ActivationFunctionType
AX = mybir.AxisListType.X
ds = bass.ds

P = 128
D = 1024
KD = D // P
DEPTH = 2
NP = 256
NB, NS = 8, 4
NT = NP + NB * NS
EPS = 1e-6
HD = 64
CONV = 4
A_PAIRS, B_TILES, C_PAIRS = 2, 3, 3
C_HEADS = 6
HEADS, NKEYS, TOPK = 8, 128, 16

RING = 3
PARTS = 3
EARLY_ADA = 2
IN_TILES = 26
T_ADA = 0
T_IN = T_ADA + EARLY_ADA * KD
T_BETA = T_IN + IN_TILES
T_SHIFT2 = T_BETA + 1
T_GATE = T_SHIFT2 + KD
T_SCALE2 = T_GATE + 1
T_GATE1 = T_SCALE2 + KD
T_OUT = T_GATE1 + KD
T_GATE2 = T_OUT + KD
T_QUERY = T_GATE2 + KD
T_U = T_QUERY + KD
T_V = T_U + NKEYS
TILES = T_V + NKEYS
SILU_Z = [0, 1, 6, 7, 23, 24, 25]
PLAIN_Z = [4, 5, 8, 9, 10, 14, 15, 16, 17, 18, 19, 20, 21, 22]
SIGM_Z = [2, 3]
GELU_Z = [11, 12, 13]
Z_ORDER = SILU_Z + PLAIN_Z + SIGM_Z + GELU_Z

XP = CONV - 1 + NP
XS = CONV - 1 + NS
XW = XP + NB * XS
YW = XW - (CONV - 1)
SS = NS + 1
SW = NP + NB * SS

SMALL = {}
_at = 0
for _name, _n in (("norm1", KD), ("norm2", KD), ("b_ada", 6 * KD), ("lru_w", B_TILES * CONV), ("lru_b", B_TILES),
                  ("dn_w", 9 * CONV), ("ba", B_TILES), ("bx", B_TILES), ("lru_L", B_TILES), ("a_norm", 1),
                  ("dn_norm", 1), ("a_log", C_HEADS), ("dt_bias", C_HEADS), ("final", KD), ("lb", DEPTH * A_PAIRS),
                  ("lb_on", 1), ("keys", NKEYS), ("lru_h", B_TILES * NB),
                  ("lru_conv", B_TILES * NB * (CONV - 1)), ("dn_conv", 9 * NB * (CONV - 1))):
    SMALL[_name] = (_at, _at + _n)
    _at += _n
SMALL_W = _at
MIXC = {}
_at = 0
for _name, _n in (("block_ones", P), ("levels", 7 * P), ("tri", P), ("tri_s", 32), ("neg", P), ("neg_s", 32),
                  ("batch_cols", NB * 32), ("batch_rows", NB), ("block_rows", P // 8)):
    MIXC[_name] = (_at, _at + _n)
    _at += _n
MIXC_W = _at
KEEP_W = 3 * P + 1
OUTS = {}
_at = 0
for _name, _n in (("p_h", B_TILES), ("s_h", B_TILES * NB), ("p_lc", B_TILES * 3), ("s_lc", B_TILES * NB * 3),
                  ("p_dc", 9 * 3), ("s_dc", 9 * NB * 3)):
    OUTS[_name] = (_at, _at + _n)
    _at += _n
OUTS_W = _at
STATE_W = (A_PAIRS + C_PAIRS) * (1 + NB) * HD
LOG1P = [1.0 / k for k in (13, 11, 9, 7, 5, 3)]


class Chain:

    def __init__(self, eng, sem, base=0):
        self.eng, self.sem, self.base, self.n = eng, sem, base, 0

    def __call__(self, ins):
        self.n += 1
        ins.then_inc(self.sem, 1)
        self.eng.wait_ge(self.sem, self.base + self.n)


def hold(eng, sem, value, spare):
    eng.wait_ge(sem, value)
    eng.sem_inc(spare, 1)


class Area:

    def __init__(self, tensor, at=0):
        self.tensor, self.at = tensor, at

    def take(self, *shape, dtype=None):
        n = 1
        for s in shape:
            n *= s
        ap = self.tensor[:, self.at:self.at + n]
        self.at += n
        assert self.at <= self.tensor.shape[1]
        if dtype is not None:
            ap = ap.bitcast(dtype)
        names = "abcd"[:len(shape)]
        if len(shape) > 1:
            ap = ap.rearrange(f"p ({' '.join(names)}) -> p {' '.join(names)}", **dict(zip(names, shape)))
        return ap


def spread(ap, axis, n):
    ap = ap.unsqueeze(axis)
    shape = list(ap.shape)
    shape[axis] = n
    return ap.broadcast_to(shape)


def batched(ap):
    return ap.rearrange("p k (b s) -> p k b s", b=NB)


@contextmanager
def signals(nc, names):
    with ExitStack() as ctx:
        sems = {n: ctx.enter_context(nc.semaphore(n)) for n in names.split()}
        yield sems
        for s in sems.values():
            nc.sync.sem_clear(s)
        nc.all_engine_barrier()


class Memory:

    def __init__(self, nc, ctx):
        def sb(name, shape, dtype=F32):
            return ctx.enter_context(nc.sbuf_tensor(name, shape, dtype))

        self.x = sb("x_res", [P, KD, NT])
        self.ring = sb("ring", [P, RING, D])
        self.parts = sb("parts", [P, PARTS, 2, D // 2], F32R)
        self.keep = sb("keep", [P, KEEP_W])
        self.small = sb("small", [P, SMALL_W])
        self.mod = sb("mod", [P, 6 * KD, 1 + NB])
        self.gain = sb("gain", [P, 2, KD, 1 + NB])
        self.cond = sb("cond", [P, KD, 1 + NB])
        self.rms = sb("rms", [P, NT])
        self.sel = sb("sel", [P, 3, 3, HEADS * TOPK])
        self.big = sb("big", [P, NKEYS * NT])
        self.act = self.big[:, :].rearrange("p (e t) -> p e t", t=NT)
        self.ident = self.keep[:, 0:P]
        self.ones = self.keep[:, P:2 * P]
        self.iota = self.keep[:, 2 * P:3 * P]
        self.eps = self.keep[:, 3 * P:3 * P + 1]
        self.loaded = [ctx.enter_context(nc.semaphore(f"tile_loaded{i}")) for i in range(RING)]
        self.done = [ctx.enter_context(nc.semaphore(f"tile_done{i}")) for i in range(RING)]
        a = Area(self.big)
        self.mixc = a.take(MIXC_W)
        self.zact = a.take(14, NT)
        self.tok = a.take(3, 2 * C_HEADS)
        self.beta = a.take(3, C_HEADS)
        self.decay = a.take(3, C_HEADS)
        self.qkv = a.take(9, NT)
        self.mixed = a.take(KD, NT)
        self.outs = a.take(OUTS_W)
        self.states = a.take(A_PAIRS + C_PAIRS, 1 + NB, HD)
        self.state0 = a.take(A_PAIRS + C_PAIRS, NB, HD)
        self.after_local = a.at
        self.xb = a.take(B_TILES, XW)
        self.xc = a.take(9, XW)
        self.square = a.take(KD, NT)
        self.free = a.at
        self.h = Area(self.big, NKEYS * NT - KD * NT).take(KD, NT)
        t = Area(self.big, 80 * NT)
        self.query = t.take(HEADS, NT)
        self.score = t.take(3, 2 * HEADS, NKEYS)
        self.cand = t.take(HEADS, TOPK * TOPK)
        self.best = t.take(2 * HEADS, TOPK)
        self.besti = t.take(2 * HEADS, TOPK, dtype=U32)
        self.bestf = t.take(2 * HEADS, TOPK)
        self.pos = t.take(HEADS * TOPK, dtype=U32)
        self.posp = t.take(HEADS * TOPK, dtype=U32)
        self.posf = t.take(HEADS * TOPK)
        self.hit = t.take(HEADS * TOPK, TOPK)

    def par(self, name):
        return self.small[:, SMALL[name][0]:SMALL[name][1]]

    def mix(self, name):
        return self.mixc[:, MIXC[name][0]:MIXC[name][1]]

    def out(self, name):
        return self.outs[:, OUTS[name][0]:OUTS[name][1]]

    def tile(self, n):
        return self.ring[:, n % RING, :].rearrange("p (k n) -> p k n", k=KD)

    def wait_tile(self, eng, n):
        eng.wait_ge(self.loaded[n % RING], 16 * (n // RING + 1))

    def wait_done(self, eng, n):
        eng.wait_ge(self.done[n % RING], n // RING + 1)


def load_tiles(eng, m, stream, l, first, end):
    for n in range(first, end):
        if n >= RING:
            m.wait_done(eng, n - RING)
        eng.dma_start(m.ring[:, n % RING, :], stream[l, n, :, :]).then_inc(m.loaded[n % RING], 16)


def load_many(eng, m, stream, l, first, end):
    turns = (end - first) // RING
    with eng.Fori(0, turns) as g:
        for j in range(RING):
            n = first + j
            eng.wait_ge(m.done[n % RING], g + n // RING)
            eng.dma_start(m.ring[:, n % RING, :], stream[l, g * RING + n, :, :]).then_inc(m.loaded[n % RING], 16)
    load_tiles(eng, m, stream, l, first + turns * RING, end)


def normalise(link, m):
    link(link.eng.reciprocal(m.rms[:, :], m.rms[:, :]))
    link(link.eng.tensor_tensor(m.h[:, :, :], m.x[:, :, :], spread(m.rms[:, :], 1, KD), ALU.mult))


def modulate(link, m, which, last=None):
    v, shift = link.eng, 3 * which * KD
    for k in range(KD):
        link(v.tensor_scalar(m.h[:, k, 0:NP], m.h[:, k, 0:NP], m.gain[:, which, k, 0:1],
                             m.mod[:, shift + k, 0:1], ALU.mult, ALU.add))
    hs = batched(m.h[:, :, NP:NT])
    link(v.tensor_tensor(hs, hs, spread(m.gain[:, which, :, 1:], 3, NS), ALU.mult))
    v.tensor_tensor(hs, hs, spread(m.mod[:, shift:shift + KD, 1:], 3, NS), ALU.add).then_inc(last, 1)


def part(m, q, side):
    return m.parts[:, q % PARTS, side, :].rearrange("p (k n) -> p k n", k=KD // 2)


def half_tile(m, t, half):
    return m.ring[:, t % RING, half * D // 2:(half + 1) * D // 2]


def split_high(eng, m, s, first, g, j, half):
    t, q = first + j, 2 * j + half
    if half == 0:
        eng.wait_ge(m.loaded[t % RING], g * 16 + 16 * (t // RING + 1))
    eng.wait_ge(s["parts_used"], g * 2 * RING + (q + 1))
    eng.activation(m.parts[:, q % PARTS, 0, :], half_tile(m, t, half), ACT.Copy).then_inc(s["hi_ready"], 1)


def split_low(eng, m, s, first, g, j, half):
    t, q = first + j, 2 * j + half
    eng.wait_ge(s["hi_ready"], g * 2 * RING + (q + 1))
    eng.tensor_tensor(m.parts[:, q % PARTS, 1, :], half_tile(m, t, half), m.parts[:, q % PARTS, 0, :].bitcast(F32),
                      ALU.subtract).then_inc(m.done[t % RING] if half else s["lo_ready"], 1)


def wait_low(eng, m, s, first, g, j, half):
    t = first + j
    if half:
        eng.wait_ge(m.done[t % RING], g + (t // RING + 1))
    else:
        eng.wait_ge(s["lo_ready"], g * RING + (j + 1))


def each_tile(eng, first, end, body):
    assert first % RING == 0
    turns = end // RING
    with eng.Fori(first // RING, turns) as g:
        for j in range(RING):
            body(g, j)
    for n in range(turns * RING, end):
        body(turns, n % RING)


def split_product(pe, m, s, first, g, j, hr, out):
    for half in range(2):
        hi, lo = part(m, 2 * j + half, 0), part(m, 2 * j + half, 1)
        pe.wait_ge(s["hi_ready"], g * 2 * RING + (2 * j + half + 1))
        for k in range(KD // 2):
            kk = half * KD // 2 + k
            for side in range(2):
                pe.matmul(out, hi[:, k, :], hr[:, side, kk, :], start=(kk + side == 0), stop=False)
        wait_low(pe, m, s, first, g, j, half)
        for k in range(KD // 2):
            kk = half * KD // 2 + k
            mm = pe.matmul(out, lo[:, k, :], hr[:, 0, kk, :], start=False, stop=(kk == KD - 1))
        mm.then_inc(s["parts_used"], 1)


def cond_rows(pe, m, first, out):
    for k in range(KD):
        m.wait_tile(pe, first + k)
        for half in range(2):
            mm = pe.matmul(out[:, half, :], m.cond[:, k, :], half_tile(m, first + k, half), start=(k == 0), stop=(k == KD - 1))
        mm.then_inc(m.done[(first + k) % RING], 1)


def turn_rows(pe, m, rows, out):
    for k in range(KD):
        mm = pe.transpose(out[:, 9 * k:9 * k + 9], rows[:, k * P:(k + 1) * P], m.ident[0:9, 0:9])
    return mm


def add_bias(link, m, first, end, psum):
    link(link.eng.tensor_tensor(m.mod[:, first * KD:end * KD, :],
                                psum[:, 0:(end - first) * KD * 9].rearrange("p (t c) -> p t c", c=9),
                                spread(m.par("b_ada")[:, first * KD:end * KD], 2, 1 + NB), ALU.add))


def norm_gain(link, m, which):
    scale = m.mod[:, (3 * which + 1) * KD:(3 * which + 2) * KD, :]
    link(link.eng.scalar_tensor_tensor(m.gain[:, which, :, :], scale, 1.0, spread(m.par(("norm1", "norm2")[which]), 2, 1 + NB),
                                       ALU.add, ALU.mult))


def setup_block(nc, m, x_in, c_in, keep_in):
    with signals(nc, "in_loaded cond_ready") as s, nc.Block() as block:
        @block.sync
        def _(sp):
            sp.dma_start(m.cond[:, :, :], c_in).then_inc(s["in_loaded"], 16)
            sp.dma_start(m.keep[:, :], keep_in).then_inc(s["in_loaded"], 16)
            sp.dma_start(m.x[:, :, :], x_in).then_inc(s["in_loaded"], 16)

        @block.scalar
        def _(act):
            act.wait_ge(s["in_loaded"], 48)
            act.activation(m.cond[:, :, :], m.cond[:, :, :], ACT.Silu).then_inc(s["cond_ready"], 1)
            act.wait_ge(s["cond_ready"], 1)


def project_block(nc, m, l, hr, stream, small_in, mixc_in, state_in):
    names = ("small_loaded mixc_loaded states_loaded squares_ready sums_ready root_ready mod_summed mod_ready "
             "h_ready step z_out pads_ready rows_out hi_ready lo_ready parts_used h_hi h_lo")
    with signals(nc, names) as s, nc.psum_tensor("ps_z", [P, 4, 512], F32) as ps_z, \
            nc.psum_tensor("ps_sum", [P, 512], F32) as ps_sum, nc.psum_tensor("ps_mod", [P, 512], F32) as ps_mod, \
            nc.Block() as block:
        tok_ps = ps_sum
        rows = Area(m.big, m.free).take(2, D)[0:9, :, :]

        @block.sync
        def _(sp):
            load_tiles(sp, m, stream, l, 0, RING)
            sp.dma_start(m.small[:, :], small_in[l, :, :]).then_inc(s["small_loaded"], 16)
            sp.dma_start(m.mixc[:, :], mixc_in).then_inc(s["mixc_loaded"], 16)
            sp.dma_start(m.state0[:, :, :, :].rearrange("p a b c -> p (a b c)"), state_in[l, :, :]).then_inc(
                s["states_loaded"], 16)
            load_many(sp, m, stream, l, RING, T_SHIFT2 + RING)
            sp.wait_ge(s["mixc_loaded"], 16)
            sp.wait_ge(s["states_loaded"], 16)

        @block.scalar
        def _(act):
            act.activation(m.square[:, :, :], m.x[:, :, :], ACT.Square).then_inc(s["squares_ready"], 1)
            act.wait_ge(s["sums_ready"], 1)
            act.activation(m.rms[:, :], ps_sum[:, 0:NT], ACT.Sqrt, bias=m.eps, scale=1.0 / D).then_inc(s["root_ready"], 1)
            for c in range(EARLY_ADA):
                m.wait_done(act, (c + 1) * KD - 1)
                if c >= 2:
                    act.wait_ge(s["mod_summed"], c - 1)
                act.activation(rows[:, c % 2, :], ps_z[0:9, 2 * (c % 2):2 * (c % 2) + 2, :].rearrange("p a b -> p (a b)"),
                               ACT.Copy).then_inc(s["rows_out"], 1)
            act.sem_inc(s["parts_used"], PARTS)
            for q in range(PARTS):
                split_high(act, m, s, T_IN, 0, q // 2, q % 2)
            act.wait_ge(s["h_ready"], 1)
            for k in (slice(0, KD // 2), slice(KD // 2, KD)):
                act.activation(hr[:, 0, k, :], m.h[:, k, :], ACT.Copy).then_inc(s["h_hi"], 1)
            for n, z in enumerate(Z_ORDER):
                for q in range(PARTS + 2 * n, min(PARTS + 2 * n + 2, 2 * IN_TILES)):
                    split_high(act, m, s, T_IN, 0, q // 2, q % 2)
                act.wait_ge(s["parts_used"], 2 * (n + 1) + PARTS)
                src = ps_z[:, n % 4, 0:NT]
                if z in PLAIN_Z and z not in (4, 5):
                    ext = m.xb[:, z - 8, :] if z < 14 else m.xc[:, z - 14, :]
                    act.activation(ext[:, CONV - 1:XP], src[:, 0:NP], ACT.Copy)
                    act.activation(ext[:, XP:XW].rearrange("p (b s) -> p b s", b=NB)[:, :, CONV - 1:],
                                   src[:, NP:NT].rearrange("p (b s) -> p b s", b=NB), ACT.Copy).then_inc(s["z_out"], 1)
                else:
                    f = ACT.Silu if z in SILU_Z else ACT.Sigmoid if z in SIGM_Z else ACT.Gelu_apprx_tanh if z in GELU_Z else ACT.Copy
                    slot = z if z < 8 else z - 3 if z < 14 else z - 12
                    act.activation(m.zact[:, slot, :], src, f).then_inc(s["z_out"], 1)
            m.wait_done(act, T_BETA)
            act.activation(m.tok[:, 0:2, :], tok_ps[:, 0:4 * C_HEADS].rearrange("p (t c) -> p t c", t=2), ACT.Copy)
            act.wait_ge(s["pads_ready"], 4)
            act.activation(m.tok[0:32, 2, :], tok_ps[0:32, 4 * C_HEADS:6 * C_HEADS], ACT.Copy).then_inc(s["z_out"], 1)
            act.wait_ge(s["z_out"], IN_TILES + 1)

        @block.gpsimd
        def _(pool):
            pool.wait_ge(s["small_loaded"], 16)
            for ext, name, n in ((m.xb, "lru_conv", B_TILES), (m.xc, "dn_conv", 9)):
                pool.tensor_copy(ext[:, :, XP:XW].rearrange("p k (b s) -> p k b s", b=NB)[:, :, :, 0:CONV - 1],
                                 m.par(name).rearrange("p (k b s) -> p k b s", k=n, b=NB)).then_inc(s["pads_ready"], 1)
            pool.memset(m.xb[:, :, 0:CONV - 1], 0.0)
            pool.memset(m.xc[:, :, 0:CONV - 1], 0.0).then_inc(s["pads_ready"], 1)
            pool.memset(m.tok[:, 2, :], 0.0).then_inc(s["pads_ready"], 1)
            pool.wait_ge(s["pads_ready"], 4)

        @block.vector
        def _(v):
            link = Chain(v, s["step"])
            v.wait_ge(s["root_ready"], 1)
            normalise(link, m)
            v.wait_ge(s["small_loaded"], 16)
            v.wait_ge(s["mod_summed"], EARLY_ADA)
            add_bias(link, m, 0, EARLY_ADA, ps_mod)
            norm_gain(link, m, 0)
            modulate(link, m, 0, s["h_ready"])
            v.wait_ge(s["h_ready"], 1)
            for n, k in enumerate((slice(0, KD // 2), slice(KD // 2, KD))):
                v.wait_ge(s["h_hi"], n + 1)
                v.tensor_tensor(hr[:, 1, k, :], m.h[:, k, :], hr[:, 0, k, :].bitcast(F32), ALU.subtract).then_inc(s["h_lo"], 1)
            for n in range(IN_TILES):
                for half in range(2):
                    split_low(v, m, s, T_IN, 0, n, half)

        @block.tensor
        def _(pe):
            pe.wait_ge(s["squares_ready"], 1)
            for k in range(KD):
                mm = pe.matmul(ps_sum[:, 0:NT], m.ones, m.square[:, k, :], start=(k == 0), stop=(k == KD - 1))
            mm.then_inc(s["sums_ready"], 1)
            def turn(c):
                pe.wait_ge(s["rows_out"], c + 1)
                turn_rows(pe, m, rows[:, c % 2, :], ps_mod[:, c * 9 * KD:]).then_inc(s["mod_summed"], 1)

            for c in range(EARLY_ADA):
                if c >= 2:
                    pe.wait_ge(s["rows_out"], c - 1)
                cond_rows(pe, m, T_ADA + c * KD, ps_z[0:9, 2 * (c % 2):2 * (c % 2) + 2, :])
                if c:
                    turn(c - 1)
            turn(EARLY_ADA - 1)
            pe.wait_ge(s["h_hi"], 2)
            pe.wait_ge(s["h_lo"], 2)
            for n in range(IN_TILES):
                if n >= 4:
                    pe.wait_ge(s["z_out"], n - 3)
                split_product(pe, m, s, T_IN, 0, n, hr, ps_z[:, n % 4, 0:NT])
            m.wait_tile(pe, T_BETA)
            pe.wait_ge(s["root_ready"], 1)
            w = m.tile(T_BETA)
            for t, (a, b) in enumerate(((0, 128), (128, 256), (256, 288))):
                for k in range(KD):
                    mm = pe.matmul(tok_ps[0:b - a, 12 * t:12 * t + 12], m.h[:, k, a:b], w[:, k, 0:12],
                                   start=(k == 0), stop=(k == KD - 1))
            mm.then_inc(m.done[T_BETA % RING], 1)


def local_block(nc, m, l, stream):
    names = ("step act_step conv_b conv_c xb_ready gates_out soft_in soft_exp decay_ready a_ready root_in root_ready "
             "qkv_ready qk_squares qk_sums qk_root tail resets_ready outs_ready rows_out mod_summed")
    with signals(nc, names) as s, nc.psum_tensor("ps_q", [P, 8, 512], F32) as ps, \
            nc.sbuf_tensor("row_buffer", [P, 2, D], F32) as row_buffer, nc.Block() as block:
        f = Area(m.big, m.free)
        yb = f.take(B_TILES, XW)
        yc = f.take(9, XW)
        xcb = f.take(B_TILES, NT)
        rgate = f.take(B_TILES, NT)
        igate = f.take(B_TILES, NT)
        a = f.take(B_TILES, NT)
        th = f.take(B_TILES, NT)
        aext = f.take(B_TILES, SW)
        bext = f.take(B_TILES, SW)
        hext = f.take(B_TILES, SW)
        sp_in = f.take(B_TILES + 3 * C_HEADS)
        sp_w = f.take(B_TILES + 3 * C_HEADS)
        sp_s = f.take(B_TILES + 3 * C_HEADS)
        sp_z = f.take(B_TILES + 3 * C_HEADS)
        sp_p = f.take(B_TILES + 3 * C_HEADS)
        alog = f.take(C_HEADS)
        sq = f.take(6, NT)
        rows = row_buffer[0:9, :, :]

        def ysamp(y):
            return y[:, :, XP:XW].rearrange("p k (b s) -> p k b s", b=NB)[:, :, :, 0:NS]

        @block.sync
        def _(sp):
            load_many(sp, m, stream, l, T_SHIFT2 + RING, T_GATE1 + RING)

        @block.tensor
        def _(pe):
            cond_rows(pe, m, T_SHIFT2, ps[0:9, 6:8, :])
            m.wait_tile(pe, T_GATE)
            pe.wait_ge(s["xb_ready"], 2)
            w = m.ring[:, T_GATE % RING, :]
            for g in range(2):
                for t in range(B_TILES):
                    n = g * B_TILES + t
                    mm = pe.matmul(ps[:, n, 0:NT], w[:, n * P:(n + 1) * P], xcb[:, t, :], start=True, stop=True)
            mm.then_inc(m.done[T_GATE % RING], 1)
            pe.wait_ge(s["rows_out"], 1)
            cond_rows(pe, m, T_SCALE2, ps[0:9, 6:8, :])
            pe.wait_ge(s["qk_squares"], 1)
            pe.wait_ge(s["gates_out"], 2)
            for n in range(6):
                mm = pe.matmul(ps[:, n, 0:NT], m.mix("block_ones"), sq[:, n, :], start=True, stop=True)
            mm.then_inc(s["qk_sums"], 1)
            pe.wait_ge(s["rows_out"], 2)
            turn_rows(pe, m, rows[:, 0, :], ps[:, 6, :])
            turn_rows(pe, m, rows[:, 1, :], ps[:, 6, 9 * KD:]).then_inc(s["mod_summed"], 1)

        @block.scalar
        def _(act):
            act.wait_ge(s["soft_in"], 1)
            act.activation(sp_w, sp_w, ACT.Exp, scale=-1.0)
            act.activation(alog, m.par("a_log"), ACT.Exp).then_inc(s["soft_exp"], 1)
            act.activation(m.beta[:, :, :], m.tok[:, :, 0:C_HEADS], ACT.Sigmoid)

            def rows_out(n, last):
                m.wait_done(act, last)
                act.activation(rows[:, n, :], ps[0:9, 6:8, :].rearrange("p a b -> p (a b)"), ACT.Copy).then_inc(s["rows_out"], 1)

            rows_out(0, T_GATE - 1)
            m.wait_done(act, T_GATE)
            for g, (dst, bias) in enumerate(((rgate, "ba"), (igate, "bx"))):
                for t in range(B_TILES):
                    i = act.activation(dst[:, t, :], ps[:, g * B_TILES + t, 0:NT], ACT.Sigmoid,
                                       bias=m.par(bias)[:, t:t + 1])
                i.then_inc(s["gates_out"], 1)
            act.wait_ge(s["gates_out"], 2)
            act.wait_ge(s["decay_ready"], 1)
            for t in range(B_TILES):
                act.activation(th[:, t, :], rgate[:, t, :], ACT.Tanh, scale=sp_in[:, t:t + 1])
            for t in range(B_TILES):
                i = act.activation(a[:, t, :], rgate[:, t, :], ACT.Exp, scale=sp_in[:, t:t + 1])
            i.then_inc(s["a_ready"], 1)
            act.wait_ge(s["conv_c"], 1)
            act.activation(m.qkv[:, :, 0:NP], yc[:, :, 0:NP], ACT.Silu)
            act.activation(batched(m.qkv[:, :, NP:NT]), ysamp(yc), ACT.Silu).then_inc(s["qkv_ready"], 1)
            act.wait_ge(s["qkv_ready"], 1)
            act.activation(sq[:, :, :], m.qkv[:, 0:6, :], ACT.Square).then_inc(s["qk_squares"], 1)
            rows_out(1, T_GATE1 - 1)
            act.wait_ge(s["root_in"], 1)
            act.activation(th[:, :, :], th[:, :, :], ACT.Sqrt, scale=-1.0).then_inc(s["root_ready"], 1)
            act.wait_ge(s["qk_sums"], 1)
            act.activation(sq[:, :, :], ps[:, 0:6, 0:NT], ACT.Sqrt, bias=m.eps).then_inc(s["qk_root"], 1)

        @block.gpsimd
        def _(pool):
            pool.memset(aext[:, :, 0:1], 0.0)
            pool.memset(aext[:, :, NP:SW].rearrange("p k (b s) -> p k b s", b=NB)[:, :, :, 0:1], 0.0)
            pool.tensor_copy(bext[:, :, NP:SW].rearrange("p k (b s) -> p k b s", b=NB)[:, :, :, 0],
                             m.par("lru_h").rearrange("p (k b) -> p k b", k=B_TILES)).then_inc(s["resets_ready"], 1)
            for ext, pn, sn, n in ((m.xb, "p_lc", "s_lc", B_TILES), (m.xc, "p_dc", "s_dc", 9)):
                pool.tensor_copy(m.out(pn).rearrange("p (k c) -> p k c", k=n), ext[:, :, XP - 3:XP])
                i = pool.tensor_copy(m.out(sn).rearrange("p (k b c) -> p k b c", k=n, b=NB),
                                 ext[:, :, XP:XW].rearrange("p k (b s) -> p k b s", b=NB)[:, :, :, NS:NS + 3])
            i.then_inc(s["outs_ready"], 1)
            pool.wait_ge(s["outs_ready"], 1)
            pool.wait_ge(s["resets_ready"], 1)

        @block.vector
        def _(v):
            link = Chain(v, s["step"])

            def conv(y, ext, t, w, bias=None):
                if bias is None:
                    link(v.tensor_scalar(y[:, t, 0:YW], ext[:, t, 0:YW], w[:, 4 * t:4 * t + 1], None, ALU.mult))
                else:
                    link(v.tensor_scalar(y[:, t, 0:YW], ext[:, t, 0:YW], w[:, 4 * t:4 * t + 1], bias, ALU.mult, ALU.add))
                for k in range(1, CONV):
                    link(v.scalar_tensor_tensor(y[:, t, 0:YW], ext[:, t, k:k + YW], w[:, 4 * t + k:4 * t + k + 1],
                                                y[:, t, 0:YW], ALU.mult, ALU.add))

            nsp = B_TILES
            link(v.tensor_scalar(sp_in[:, 0:nsp], m.par("lru_L"), -1.0, None, ALU.mult))
            link(v.tensor_tensor(sp_in[:, nsp:].rearrange("p (t h) -> p t h", t=3), m.tok[:, :, C_HEADS:],
                                 spread(m.par("dt_bias"), 1, 3), ALU.add))
            link(v.tensor_scalar(sp_w, sp_in, -1.0, None, ALU.mult))
            v.tensor_tensor(sp_w, sp_w, sp_in, ALU.max).then_inc(s["soft_in"], 1)
            v.wait_ge(s["soft_in"], 1)
            for t in range(B_TILES):
                conv(yb, m.xb, t, m.par("lru_w"), m.par("lru_b")[:, t:t + 1])
            v.tensor_copy(xcb[:, :, 0:NP], yb[:, :, 0:NP]).then_inc(s["xb_ready"], 1)
            v.tensor_copy(batched(xcb[:, :, NP:NT]), ysamp(yb)).then_inc(s["xb_ready"], 1)
            v.wait_ge(s["soft_exp"], 1)
            link(v.tensor_scalar(sp_z, sp_w, 2.0, None, ALU.add))
            link(v.reciprocal(sp_z, sp_z))
            link(v.tensor_tensor(sp_s, sp_w, sp_z, ALU.mult))
            link(v.tensor_tensor(sp_z, sp_s, sp_s, ALU.mult))
            link(v.tensor_scalar(sp_p, sp_z, 1.0 / 15, None, ALU.mult))
            for c in LOG1P:
                link(v.scalar_tensor_tensor(sp_p, sp_p, c, sp_z, ALU.add, ALU.mult))
            link(v.scalar_tensor_tensor(sp_p, sp_p, 1.0, sp_s, ALU.add, ALU.mult))
            link(v.tensor_scalar(sp_s, sp_in, 0.0, None, ALU.max))
            link(v.scalar_tensor_tensor(sp_in, sp_p, 2.0, sp_s, ALU.mult, ALU.add))
            link(v.scalar_tensor_tensor(m.decay[:, :, :], sp_in[:, nsp:].rearrange("p (t h) -> p t h", t=3), -1.0,
                                        spread(alog, 1, 3), ALU.mult, ALU.mult))
            v.tensor_scalar(sp_in[:, 0:nsp], sp_in[:, 0:nsp], -8.0, None, ALU.mult).then_inc(s["decay_ready"], 1)
            for t in range(9):
                conv(yc, m.xc, t, m.par("dn_w"))
            v.sem_inc(s["conv_c"], 1)
            v.wait_ge(s["a_ready"], 1)
            v.wait_ge(s["resets_ready"], 1)
            link(v.tensor_tensor(xcb[:, :, :], xcb[:, :, :], igate[:, :, :], ALU.mult))
            link(v.tensor_tensor(igate[:, :, :], a[:, :, :], a[:, :, :], ALU.mult))
            v.scalar_tensor_tensor(th[:, :, :], igate[:, :, :], 1.0, th[:, :, :], ALU.add, ALU.mult).then_inc(s["root_in"], 1)
            link(v.tensor_copy(aext[:, :, 1:NP], a[:, :, 1:NP]))
            link(v.tensor_copy(aext[:, :, NP:SW].rearrange("p k (b s) -> p k b s", b=NB)[:, :, :, 1:], batched(a[:, :, NP:NT])))
            v.wait_ge(s["root_ready"], 1)
            link(v.tensor_tensor(bext[:, :, 0:NP], th[:, :, 0:NP], xcb[:, :, 0:NP], ALU.mult))
            link(v.tensor_tensor(bext[:, :, NP:SW].rearrange("p k (b s) -> p k b s", b=NB)[:, :, :, 1:],
                                 batched(th[:, :, NP:NT]), batched(xcb[:, :, NP:NT]), ALU.mult))
            link(v.tensor_tensor_scan(flat(hext), flat(aext), flat(bext), 0.0, ALU.mult, ALU.add))
            hs = hext[:, :, NP:SW].rearrange("p k (b s) -> p k b s", b=NB)
            link(v.tensor_tensor(m.mixed[:, 2:5, 0:NP], hext[:, :, 0:NP], m.zact[:, 8:11, 0:NP], ALU.mult))
            link(v.tensor_tensor(batched(m.mixed[:, 2:5, NP:NT]), hs[:, :, :, 1:], batched(m.zact[:, 8:11, NP:NT]), ALU.mult))
            link(v.tensor_copy(m.out("p_h"), hext[:, :, NP - 1]))
            link(v.tensor_copy(m.out("s_h").rearrange("p (k b) -> p k b", k=B_TILES), hs[:, :, :, NS]))
            v.wait_ge(s["qk_root"], 1)
            link(v.reciprocal(sq[:, :, :], sq[:, :, :]))
            link(v.scalar_tensor_tensor(flat(m.qkv[:, 0:3, :]), flat(m.qkv[:, 0:3, :]), HD ** -0.5, flat(sq[:, 0:3, :]),
                                        ALU.mult, ALU.mult))
            link(v.tensor_tensor(m.qkv[:, 3:6, :], m.qkv[:, 3:6, :], sq[:, 3:6, :], ALU.mult))
            v.wait_ge(s["mod_summed"], 1)
            add_bias(link, m, 3, 5, ps[:, 6, :])
            norm_gain(link, m, 1)


def hgrn_block(nc, m, l):
    C = 8
    BLOCKS = NP // C
    TB = P // C
    TOK = ((0, P), (P, P), (NP, NB * NS))
    names = ("step pool_step lb_ready lb_out f_ready gates_ready qt_ready pairs_ready sums_ready kt_ready turned "
             "kt_out values_done vm_ready u_ready u_out scan_ready inter_ready products_ready")
    with signals(nc, names) as s, nc.psum_tensor("ps_sums", [P, 2, 2, 512], F32) as ps_sums, \
            nc.psum_tensor("ps_outer", [P, 4, 512], F32) as ps_outer, nc.Block() as block:
        f = Area(m.big, m.after_local)
        lb = f.take(A_PAIRS)
        omlb = f.take(A_PAIRS)
        gate = [None] + [f.take(A_PAIRS, NT) for _ in range(1, C)]
        key = f.take(A_PAIRS, NT)
        q = f.take(A_PAIRS, NT)
        start0 = f.take(A_PAIRS, NT)
        start1 = f.take(A_PAIRS, NT)
        since = f.take(A_PAIRS, NT)
        qt = f.take(A_PAIRS, NT)
        kt = f.take(A_PAIRS, NT)
        pair_p = f.take(2, 2 * NP)
        pair_s = f.take(2, 2 * NB * NS)
        prod_p = f.take(2 * NP)
        prod_s = f.take(2 * NB * NS)
        ktt = f.take(3, A_PAIRS, P)
        vtok = f.take(3, A_PAIRS * P)
        vm = f.take(2, 4, TB // 2, HD)
        after = f.take(A_PAIRS, BLOCKS, HD)
        v = m.zact[:, 4:6, :]
        o = m.mixed[:, 0:2, :]

        def blocks(x, sample, lo, hi):
            x, c = (x[:, :, NP:NT], NS) if sample else (x[:, :, 0:NP], C)
            return x.rearrange("p a (n c) -> p a n c", c=c)[:, :, :, lo:hi]

        def compact(x, sample, d):
            n = NS - d if sample else C - d
            w = A_PAIRS * (NB if sample else BLOCKS) * n
            return x[:, 0:w].rearrange("p (a n c) -> p a n c", a=A_PAIRS, c=n)

        def kinds(d):
            return (False, True) if d < NS else (False,)

        def length(sample):
            return NS if sample else C

        @block.scalar
        def _(act):
            act.wait_ge(s["lb_ready"], 1)
            act.activation(lb, lb, ACT.Sigmoid).then_inc(s["lb_out"], 1)
            for tt in range(3):
                n = TOK[tt][1]
                act.wait_ge(s["turned"], tt + 1)
                act.activation(flat(ktt[0:n, tt, :, :]), ps_outer[0:n, tt, 0:2 * P], ACT.Copy)
                act.activation(vtok[0:n, tt, :], ps_outer[0:n, tt, 2 * P:4 * P], ACT.Copy).then_inc(s["kt_out"], 1)
            act.wait_ge(s["scan_ready"], 4)
            act.activation(m.states[:, 0:A_PAIRS, 0, :], after[:, :, BLOCKS - 1, :], ACT.Copy)

        @block.gpsimd
        def _(pool):
            link = Chain(pool, s["pool_step"])
            pool.wait_ge(s["f_ready"], 1)
            for d in range(2, C):
                for sample in kinds(d):
                    n = length(sample)
                    link(pool.tensor_tensor(blocks(gate[d], sample, d, n), blocks(gate[d - 1], sample, d, n),
                                            blocks(gate[1], sample, 1, n - d + 1), ALU.mult))
                pool.sem_inc(s["pairs_ready"], 1)
            for sample in (False, True):
                n = length(sample)
                link(pool.tensor_copy(blocks(kt, sample, n - 1, n), blocks(key, sample, n - 1, n)))
                for d in range(1, n):
                    link(pool.tensor_tensor(blocks(kt, sample, n - 1 - d, n - d), blocks(key, sample, n - 1 - d, n - d),
                                            blocks(gate[d], sample, n - 1, n), ALU.mult))
            pool.sem_inc(s["kt_ready"], 1)
            pool.wait_ge(s["gates_ready"], 1)
            pool.tensor_tensor(qt[:, :, :], q[:, :, :], since[:, :, :], ALU.mult).then_inc(s["qt_ready"], 1)

            def mask_v(turn):
                if turn < 4:
                    tt, hb, n = turn // 2, turn % 2, P
                    mask = m.mix("block_rows")[:, hb * TB // 2:(hb + 1) * TB // 2]
                else:
                    tt, n, mask = 2, NB * NS, m.mix("batch_rows")[0:NB * NS, :]
                if turn >= 2:
                    pool.wait_ge(s["u_ready"], 2 * turn - 2)
                for h in range(4):
                    i = pool.tensor_tensor(vm[0:n, turn % 2, h, :, :],
                                         spread(vtok[0:n, tt, h * HD:(h + 1) * HD], 1, TB // 2),
                                         spread(mask[0:n], 2, HD), ALU.mult)
                i.then_inc(s["vm_ready"], 1)

            pool.wait_ge(s["kt_out"], 3)
            for turn in range(5):
                mask_v(turn)

        @block.tensor
        def _(pe):
            def distance(d):
                pe.wait_ge(s["products_ready"], d + 1)
                for sample in kinds(d):
                    w = A_PAIRS * (NB * (NS - d) if sample else BLOCKS * (C - d))
                    src = (pair_s if sample else pair_p)[:, d % 2, 0:w]
                    mm = pe.matmul(ps_sums[:, d % 2, int(sample), 0:w], m.mix("block_ones"), src, start=True, stop=True)
                mm.then_inc(s["sums_ready"], 1)

            distance(0)
            distance(1)
            pe.wait_ge(s["kt_ready"], 1)
            for tt, (t0, n) in enumerate(TOK):
                for pair in range(A_PAIRS):
                    pe.transpose(ps_outer[0:n, tt, pair * P:(pair + 1) * P], kt[:, pair, t0:t0 + n], m.ident)
                for pair in range(A_PAIRS):
                    mm = pe.transpose(ps_outer[0:n, tt, (2 + pair) * P:(3 + pair) * P], v[:, pair, t0:t0 + n], m.ident)
                mm.then_inc(s["turned"], 1)
            for d in range(2, C):
                distance(d)
            def inter(pair, r, t, n, state):
                rows = slice(r * HD, (r + 1) * HD)
                return pe.matmul(ps_sums[rows, 0, pair, t:t + n], state[rows], qt[rows, pair, t:t + n], start=True, stop=True)

            def read_states(turn):
                pe.wait_ge(s["scan_ready"], turn + 1)
                for b in range(turn * TB // 2 + 1, min((turn + 1) * TB // 2 + 1, BLOCKS)):
                    for pair in range(A_PAIRS):
                        for r in range(2):
                            mm = inter(pair, r, C * b, C, after[:, pair, b - 1, :])
                return mm

            for turn in range(4):
                tt = turn // 2
                pe.wait_ge(s["vm_ready"], turn + 1)
                for pair in range(A_PAIRS):
                    n = 2 * turn + pair
                    if n >= 4:
                        pe.wait_ge(s["u_out"], n - 3)
                    for r in range(2):
                        rows = slice(r * HD, (r + 1) * HD)
                        mm = pe.matmul(ps_outer[rows, n % 4, :], ktt[:, tt, pair, rows],
                                       vm[:, turn % 2, 2 * pair + r, :, :], start=True, stop=True)
                    mm.then_inc(s["u_ready"], 1)
                if turn == 0:
                    pe.wait_ge(s["qt_ready"], 1)
                    pe.wait_ge(s["values_done"], 1)
                    for b in range(NB):
                        for pair in range(A_PAIRS):
                            for r in range(2):
                                inter(pair, r, NP + NS * b, NS, m.state0[:, pair, b, :])
                if turn >= 2:
                    read_states(turn - 2)
            read_states(2)
            pe.wait_ge(s["vm_ready"], 5)
            pe.wait_ge(s["u_out"], 8)
            for pair in range(A_PAIRS):
                for r in range(2):
                    rows = slice(r * HD, (r + 1) * HD)
                    mm = pe.matmul(ps_outer[rows, pair, :], ktt[0:NB * NS, 2, pair, rows], vm[0:NB * NS, 0, 2 * pair + r, :, :],
                                   start=True, stop=True)
            mm.then_inc(s["u_ready"], 1)
            mm = read_states(3)
            mm.then_inc(s["inter_ready"], 1)

        @block.vector
        def _(ve):
            link = Chain(ve, s["step"])
            ve.tensor_tensor(lb, m.par("lb")[:, A_PAIRS:2 * A_PAIRS], m.par("lb")[:, 0:A_PAIRS], ALU.subtract).then_inc(
                s["lb_ready"], 1)
            ve.wait_ge(s["lb_out"], 1)
            link(ve.tensor_scalar(lb, lb, m.par("lb_on"), None, ALU.mult))
            link(ve.tensor_scalar(omlb, lb, -1.0, 1.0, ALU.mult, ALU.add))
            for pair in range(A_PAIRS):
                link(ve.tensor_scalar(gate[1][:, pair, :], m.zact[:, 2 + pair, :], omlb[:, pair:pair + 1],
                                      lb[:, pair:pair + 1], ALU.mult, ALU.add))
            link(ve.tensor_scalar(key[:, :, :], gate[1][:, :, :], -1.0, 1.0, ALU.mult, ALU.add))
            ve.sem_inc(s["f_ready"], 1)
            link(ve.tensor_scalar(q[:, :, :], m.zact[:, 0:2, :], HD ** -0.5, None, ALU.mult))

            def pairs(d):
                if d >= 2:
                    ve.wait_ge(s["pairs_ready"], d - 1)
                for sample in kinds(d):
                    n = length(sample)
                    dst = compact((pair_s if sample else pair_p)[:, d % 2, :], sample, d)
                    if d == 0:
                        link(ve.tensor_tensor(dst, blocks(q, sample, 0, n), blocks(key, sample, 0, n), ALU.mult))
                    else:
                        link(ve.tensor_tensor(dst, blocks(q, sample, d, n), blocks(gate[d], sample, d, n), ALU.mult))
                        link(ve.tensor_tensor(dst, dst, blocks(key, sample, 0, n - d), ALU.mult))
                ve.sem_inc(s["products_ready"], 1)

            def values(d):
                ve.wait_ge(s["sums_ready"], d + 1)
                for sample in kinds(d):
                    n = length(sample)
                    a = compact(ps_sums[:, d % 2, int(sample), :], sample, d)
                    if d == 0:
                        link(ve.tensor_tensor(blocks(o, sample, 0, n), a, blocks(v, sample, 0, n), ALU.mult))
                    else:
                        tmp = compact(prod_s if sample else prod_p, sample, d)
                        link(ve.tensor_tensor(tmp, a, blocks(v, sample, 0, n - d), ALU.mult))
                        link(ve.tensor_tensor(blocks(o, sample, d, n), blocks(o, sample, d, n), tmp, ALU.add))

            pairs(0)
            pairs(1)
            values(0)
            link(ve.tensor_copy(start0[:, :, :], gate[1][:, :, :]))
            link(ve.memset(start1[:, :, :], 0.0))
            for sample in (False, True):
                link(ve.memset(blocks(start0, sample, 0, 1), 0.0))
                link(ve.tensor_copy(blocks(start1, sample, 0, 1), blocks(gate[1], sample, 0, 1)))
            ve.tensor_tensor_scan(flat(since), flat(start0), flat(start1), 0.0, ALU.mult, ALU.add).then_inc(
                s["gates_ready"], 1)
            for d in range(2, C):
                pairs(d)
                values(d - 1)
            values(C - 1)
            ve.sem_inc(s["values_done"], 1)
            for turn in range(4):
                ve.wait_ge(s["u_ready"], 2 * turn + 2)
                for j in range(TB // 2):
                    b = turn * TB // 2 + j
                    for pair in range(A_PAIRS):
                        new, add = after[:, pair, b, :], ps_outer[:, (2 * turn + pair) % 4, j * HD:(j + 1) * HD]
                        if b == 0:
                            i = ve.tensor_copy(new, add)
                        else:
                            i = ve.scalar_tensor_tensor(new, after[:, pair, b - 1, :],
                                                        since[:, pair, C * b + C - 1:C * b + C], add, ALU.mult, ALU.add)
                        link(i)
                ve.sem_inc(s["scan_ready"], 1)
                ve.sem_inc(s["u_out"], 2)
            ve.wait_ge(s["u_ready"], 9)
            for pair in range(A_PAIRS):
                new = m.states[:, pair, 1:, :]
                last = blocks(since, True, NS - 1, NS)[:, pair, :, :].broadcast_to([P, NB, HD])
                link(ve.tensor_tensor(new, m.state0[:, pair, :, :], last, ALU.mult))
                link(ve.tensor_tensor(new, new, ps_outer[:, pair, :].rearrange("p (b v) -> p b v", b=NB), ALU.add))
            ve.wait_ge(s["inter_ready"], 1)
            link(ve.tensor_tensor(o[:, :, C:], o[:, :, C:], ps_sums[:, 0, :, C:NT], ALU.add))


def flat(ap):
    return ap.rearrange("p a b -> p (a b)")


def delta_block(nc, m, l):
    GROUPS = ((0, P, 0), (P, P, 1), (NP, NB * NS, 2))
    names = ("step act_step ps_a ps_b ps_c ps_d gcol_out eg_ready kb_ready raw_ready pair_free x_ready x_out tu_ready "
             "tu_done kd_ps kd_out r_ps r_out e_ps e_out o_ps s_ps s_out a_free em_ready dt_ready dte_ready gp_ready "
             "glast_ready glast_exp scaled masked kd_mul r_sum nk_masked")
    H = C_HEADS
    with signals(nc, names) as s, nc.psum_tensor("ps_1", [P, 1024], F32) as ps1, \
            nc.psum_tensor("ps_2", [P, 1024], F32) as ps2, nc.psum_tensor("ps_3", [P, 1024], F32) as ps3, \
            nc.psum_tensor("ps_4", [P, 1024], F32) as ps4, nc.Block() as block:
        f = Area(m.big, m.after_local)

        def by_group(tiles):
            return [f.take(tiles, n) for _, n, _ in GROUPS]

        gcol = f.take(3, H)
        dt = f.take(H, P)
        gp = f.take(C_PAIRS, P)
        eg = by_group(C_PAIRS)
        gl = f.take(C_PAIRS, P)
        kb = f.take(C_PAIRS, P)
        vb = by_group(C_PAIRS)
        nke = by_group(C_PAIRS)
        qe = by_group(C_PAIRS)
        kd = by_group(C_PAIRS)
        ntm = by_group(H)
        ptm = by_group(H)
        tm = by_group(H)
        um = by_group(H)
        emb = Area(m.big, f.at).take(H, NB, HD)
        xm = f.take(2, H, P)
        cm = f.take(2, H, P)
        kdt = f.take(3, H, HD)
        rm = f.take(H, HD)
        em = f.take(H, HD)
        nkm = f.take(C_PAIRS, NB, NB * NS)
        state = f.take(C_PAIRS, HD)

        def head(ap, h, n):
            r = (h % 2) * HD
            return ap[r:r + HD, h // 2, 0:n]

        def at(ap, h, width, n):
            c = (h % 2) * 512 + (h // 2) * width
            return ap[:, c:c + n]

        def heads(ap, width, n):
            return ap.rearrange("p (r q c) -> p q r c", r=2, c=width)[:, 0:C_PAIRS, :, 0:n]

        def by_pair(ap):
            return ap.rearrange("p (q r) c -> p q r c", r=2)

        def half(ap, r, n):
            return ap.rearrange("p (r q c) -> p r q c", r=2, c=P)[r * HD:(r + 1) * HD, r, 0:C_PAIRS, 0:n]

        def levels(n):
            return 7 if n == P else 2

        @block.tensor
        def _(pe):
            for g, (t0, n, tt) in enumerate(GROUPS):
                tri = m.mix("tri") if n == P else m.mix("tri_s")
                if g:
                    pe.wait_ge(s["gp_ready"], g)
                    pe.wait_ge(s["kb_ready"], g)
                    pe.wait_ge(s["masked"], g)
                for h in range(H):
                    pe.matmul(at(ps1, h, P, n), m.decay[0:n, tt, h:h + 1].broadcast_to([n, P]), tri[0:n, 0:n],
                              start=True, stop=True)
                pe.matmul(ps3[0:n, 0:H], tri[0:n, 0:n], m.decay[0:n, tt, :], start=True, stop=True)
                for h in range(H):
                    mm = pe.matmul(at(ps2, h, P, n), m.beta[0:n, tt, h:h + 1].broadcast_to([n, P]),
                                   m.ident[0:n, 0:n], start=True, stop=True)
                mm.then_inc(s["ps_a"], 1)
                pe.wait_ge(s["kb_ready"], g + 1)
                pe.wait_ge(s["gcol_out"], g + 1)
                for h in range(H):
                    k = head(m.qkv[:, 3:6, t0:t0 + n], h, n)
                    pe.matmul(at(ps3, h, P, n)[0:n], k, head(kb, h, n), start=True, stop=True)
                    mm = pe.matmul(at(ps4, h, P, n)[0:n], k, head(m.qkv[:, 0:3, t0:t0 + n], h, n), start=True, stop=True)
                mm.then_inc(s["raw_ready"], 1)
            pe.wait_ge(s["masked"], 3)
            turn = 0
            last_turn = [None, None]
            for g0 in ((0, 1), (2,)):
                for lv in range(levels(GROUPS[g0[0]][1])):
                    for b, g in enumerate(g0):
                        n = GROUPS[g][1]
                        px, pt = (ps1, ps2) if b == 0 else (ps3, ps4)
                        pe.wait_ge(s["scaled"], turn + 1)
                        if last_turn[b] is not None:
                            pe.wait_ge(s["tu_done"], last_turn[b] + 1)
                        last_turn[b] = turn
                        for r in range(2):
                            for h in range(r, H, 2):
                                mm = pe.matmul(at(px, h, P, n)[0:n], cm[0:n, b, h, 0:n], tm[g][0:n, h, 0:n], start=True, stop=True)
                            mm.then_inc(s["x_ready"], 1)
                        for r in range(2):
                            pe.wait_ge(s["x_out"], 2 * turn + r + 1)
                            for h in range(r, H, 2):
                                if lv < levels(n) - 1:
                                    pe.matmul(at(pt, h, P, n)[0:n], um[g][0:n, h, 0:n], xm[0:n, b, h, 0:n], start=True, stop=True)
                                mm = pe.matmul(at(px, h, P, n)[0:n], xm[0:n, b, h, 0:n], um[g][0:n, h, 0:n], start=True, stop=True)
                        mm.then_inc(s["tu_ready"], 1)
                        turn += 1
            for g, (t0, n, tt) in enumerate(GROUPS):
                pe.wait_ge(s["tu_done"], turn)
                if g:
                    pe.wait_ge(s["kd_out"], g)
                for h in range(H):
                    r = (h % 2) * HD
                    mm = pe.matmul(at(ps1, h, HD, HD)[0:n], head(kd[g][:, :, :], h, n), m.ident[r:r + HD, r:r + HD],
                                   start=True, stop=True)
                mm.then_inc(s["kd_ps"], 1)
            pe.wait_ge(s["nk_masked"], 1)
            for g, (t0, n, tt) in enumerate(GROUPS):
                if g == 0:
                    pe.wait_ge(s["kd_out"], 3)
                pe.wait_ge(s["s_out"], g + 1)
                for h in range(H):
                    r = (h % 2) * HD
                    out = at(ps2, h, HD, HD)[0:n]
                    pe.matmul(out, head(vb[g][:, :, :], h, n), m.ident[r:r + HD, r:r + HD], start=True, stop=False)
                    if n == P:
                        mm = pe.matmul(out, head(nke[g][:, :, :], h, n), state[r:r + HD, h // 2, :], start=False, stop=True)
                    else:
                        for b in range(NB):
                            mm = pe.matmul(out, nkm[r:r + HD, h // 2, b, :], m.state0[r:r + HD, A_PAIRS + h // 2, b, :],
                                           start=False, stop=(b == NB - 1))
                mm.then_inc(s["r_ps"], 1)
                pe.wait_ge(s["r_out"], g + 1)
                for h in range(H):
                    mm = pe.matmul(at(ps3, h, HD, HD)[0:n], um[g][0:n, h, 0:n], rm[0:n, h, :], start=True, stop=True)
                mm.then_inc(s["e_ps"], 1)
                pe.wait_ge(s["e_out"], g + 1)
                if g:
                    pe.wait_ge(s["act_step"], g)
                for h in range(H):
                    r = (h % 2) * HD
                    out = ps4[r:r + HD, (h // 2) * P:(h // 2) * P + n]
                    pe.matmul(out, em[0:n, h, :], ptm[g][0:n, h, 0:n], start=True, stop=False)
                    if n == P:
                        mm = pe.matmul(out, state[r:r + HD, h // 2, :], head(qe[g][:, :, :], h, n), start=False, stop=True)
                    else:
                        for b in range(NB):
                            mm = pe.matmul(out[:, NS * b:NS * b + NS], m.state0[r:r + HD, A_PAIRS + h // 2, b, :],
                                           head(qe[g][:, :, :], h, n)[:, NS * b:NS * b + NS], start=False, stop=(b == NB - 1))
                mm.then_inc(s["o_ps"], 1)
                if n == P:
                    for h in range(H):
                        r = (h % 2) * HD
                        mm = pe.matmul(ps1[r:r + HD, (h // 2) * HD:(h // 2 + 1) * HD], kdt[0:n, g, h, :], em[0:n, h, :],
                                       start=True, stop=True)
                    mm.then_inc(s["s_ps"], 1)
                else:
                    pe.wait_ge(s["em_ready"], 1)
                    for h in range(H):
                        r = (h % 2) * HD
                        bank = (ps1[:, 0:512], ps1[:, 512:1024], ps2[:, 0:512])[h // 2]
                        mm = pe.matmul(bank[r:r + HD, :], kdt[0:n, g, h, :], emb[0:n, h, :, :], start=True, stop=True)
                    mm.then_inc(s["s_ps"], 1)

        @block.scalar
        def _(act):
            for g, (t0, n, tt) in enumerate(GROUPS):
                act.wait_ge(s["ps_a"], g + 1)
                for r in range(2):
                    i = act.activation(gp[r * HD:(r + 1) * HD, :, 0:n], half(ps1, r, n), ACT.Copy)
                i.then_inc(s["gp_ready"], 1)
                act.wait_ge(s["gp_ready"], g + 1)
                act.activation(eg[g][:, :, 0:n], gp[:, :, 0:n], ACT.Exp).then_inc(s["eg_ready"], 1)
                act.wait_ge(s["dt_ready"], g + 1)
                act.activation(dt[0:n, :, 0:n], dt[0:n, :, 0:n], ACT.Exp).then_inc(s["dte_ready"], 1)
                act.wait_ge(s["glast_ready"], g + 1)
                act.activation(gl[:, :, 0:n], gl[:, :, 0:n], ACT.Exp).then_inc(s["glast_exp"], 1)
                act.wait_ge(s["kd_mul"], g + 1)
            turn = 0
            for g0 in ((0, 1), (2,)):
                for lv in range(levels(GROUPS[g0[0]][1])):
                    for b, g in enumerate(g0):
                        n = GROUPS[g][1]
                        px = ps1 if b == 0 else ps3
                        for r in range(2):
                            act.wait_ge(s["x_ready"], 2 * turn + r + 1)
                            act.activation(by_pair(xm[0:n, b, :, 0:n])[:, :, r, :], heads(px, P, n)[0:n, :, r, :],
                                           ACT.Copy).then_inc(s["x_out"], 1)
                        turn += 1
            for g, (t0, n, tt) in enumerate(GROUPS):
                act.wait_ge(s["kd_ps"], g + 1)
                act.activation(by_pair(kdt[0:n, g, :, :]), heads(ps1, HD, HD)[0:n], ACT.Copy).then_inc(s["kd_out"], 1)
            for g, (t0, n, tt) in enumerate(GROUPS):
                act.wait_ge(s["r_ps"], g + 1)
                act.activation(by_pair(rm[0:n, :, :]), heads(ps2, HD, HD)[0:n], ACT.Copy).then_inc(s["r_out"], 1)
                act.wait_ge(s["e_ps"], g + 1)
                if g:
                    act.wait_ge(s["s_ps"], g)
                act.activation(by_pair(em[0:n, :, :]), heads(ps3, HD, HD)[0:n], ACT.Copy).then_inc(s["e_out"], 1)
                act.wait_ge(s["o_ps"], g + 1)
                i = act.activation(m.mixed[:, 5:8, t0:t0 + n],
                                   ps4[:, 0:3 * P].rearrange("p (q c) -> p q c", q=3)[:, :, 0:n], ACT.Copy)
                i.then_inc(s["act_step"], 1)
                act.wait_ge(s["act_step"], g + 1)

        @block.vector
        def _(v):
            link = Chain(v, s["step"])
            for g, (t0, n, tt) in enumerate(GROUPS):
                neg = m.mix("neg") if n == P else m.mix("neg_s")
                last = n - 1
                v.wait_ge(s["ps_a"], g + 1)
                v.tensor_copy(gcol[0:n, g, :], ps3[0:n, 0:H]).then_inc(s["gcol_out"], 1)
                v.wait_ge(s["gcol_out"], g + 1)
                v.wait_ge(s["gp_ready"], g + 1)
                for h in range(H):
                    i = v.scalar_tensor_tensor(dt[0:n, h, 0:n], at(ps1, h, P, n)[0:n], gcol[0:n, g, h:h + 1],
                                               neg[0:n, 0:n], ALU.subtract, ALU.add)
                i.then_inc(s["dt_ready"], 1)
                for r in range(2):
                    rows = slice(r * HD, (r + 1) * HD)
                    link(v.tensor_tensor(kb[rows, :, 0:n], m.qkv[rows, 3:6, t0:t0 + n], half(ps2, r, n), ALU.mult))
                    link(v.tensor_tensor(vb[g][rows, :, 0:n], m.qkv[rows, 6:9, t0:t0 + n], half(ps2, r, n), ALU.mult))
                v.sem_inc(s["kb_ready"], 1)
                v.wait_ge(s["gp_ready"], g + 1)
                if n == P:
                    link(v.tensor_tensor(gl[:, :, 0:n], gp[:, :, last:n].broadcast_to([P, C_PAIRS, n]), gp[:, :, 0:n], ALU.subtract))
                else:
                    for q in range(C_PAIRS):
                        a = gp[:, q, 0:n].rearrange("p (b s) -> p b s", b=NB)
                        link(v.tensor_tensor(gl[:, q, 0:n].rearrange("p (b s) -> p b s", b=NB),
                                             a[:, :, NS - 1:NS].broadcast_to([P, NB, NS]), a, ALU.subtract))
                v.sem_inc(s["glast_ready"], 1)
                v.wait_ge(s["eg_ready"], g + 1)
                for q in range(C_PAIRS):
                    link(v.scalar_tensor_tensor(nke[g][:, q, 0:n], kb[:, q, 0:n], -1.0, eg[g][:, q, 0:n], ALU.mult, ALU.mult))
                link(v.tensor_tensor(qe[g][:, :, 0:n], m.qkv[:, 0:3, t0:t0 + n], eg[g][:, :, 0:n], ALU.mult))
                v.wait_ge(s["glast_exp"], g + 1)
                v.tensor_tensor(kd[g][:, :, 0:n], m.qkv[:, 3:6, t0:t0 + n], gl[:, :, 0:n], ALU.mult).then_inc(s["kd_mul"], 1)
                v.wait_ge(s["raw_ready"], g + 1)
                v.wait_ge(s["dte_ready"], g + 1)
                link(v.tensor_tensor(by_pair(ntm[g][0:n, :, 0:n]), heads(ps3, P, n)[0:n], by_pair(dt[0:n, :, 0:n]), ALU.mult))
                link(v.tensor_tensor(by_pair(ptm[g][0:n, :, 0:n]), heads(ps4, P, n)[0:n], by_pair(dt[0:n, :, 0:n]), ALU.mult))
                link(v.tensor_copy(tm[g][0:n, :, 0:n], spread(m.ident[0:n, 0:n], 1, H)))
                link(v.tensor_copy(um[g][0:n, :, 0:n], spread(m.ident[0:n, 0:n], 1, H)))
                v.sem_inc(s["masked"], 1)
            turn = 0
            order = []
            for g0 in ((0, 1), (2,)):
                for lv in range(levels(GROUPS[g0[0]][1])):
                    for b, g in enumerate(g0):
                        order.append((lv, b, g))

            def mask(turn):
                lv, b, g = order[turn]
                n = GROUPS[g][1]
                if turn >= 2:
                    v.wait_ge(s["x_ready"], 2 * (turn - 1 if order[turn - 1][1] != b else turn))
                link(v.tensor_tensor(cm[0:n, b, :, 0:n], ntm[g][0:n, :, 0:n],
                                     spread(m.mix("levels")[0:n, lv * P:lv * P + n], 1, H), ALU.mult))
                v.sem_inc(s["scaled"], 1)

            mask(0)
            mask(1)
            for turn, (lv, b, g) in enumerate(order):
                n = GROUPS[g][1]
                px, pt = (ps1, ps2) if b == 0 else (ps3, ps4)
                v.wait_ge(s["tu_ready"], turn + 1)
                if lv < levels(n) - 1:
                    link(v.tensor_tensor(by_pair(tm[g][0:n, :, 0:n]), by_pair(tm[g][0:n, :, 0:n]), heads(pt, P, n)[0:n], ALU.subtract))
                link(v.tensor_tensor(by_pair(um[g][0:n, :, 0:n]), by_pair(um[g][0:n, :, 0:n]), heads(px, P, n)[0:n], ALU.subtract))
                v.sem_inc(s["tu_done"], 1)
                if turn + 2 < len(order):
                    mask(turn + 2)
            for q in range(C_PAIRS):
                link(v.tensor_tensor(nkm[:, q, :, :], spread(nke[2][:, q, 0:NB * NS], 1, NB),
                                     m.mix("batch_cols").rearrange("p (b t) -> p b t", b=NB), ALU.mult))
            v.sem_inc(s["nk_masked"], 1)
            link(v.memset(state[:, :, :], 0.0))
            v.sem_inc(s["s_out"], 1)
            for g, (t0, n, tt) in enumerate(GROUPS):
                if n == P:
                    v.wait_ge(s["s_ps"], g + 1)
                    for q in range(C_PAIRS):
                        link(v.scalar_tensor_tensor(state[:, q, :], state[:, q, :], eg[g][:, q, n - 1:n],
                                                    ps1[:, q * HD:(q + 1) * HD], ALU.mult, ALU.add))
                    if g == 1:
                        link(v.tensor_copy(m.states[:, A_PAIRS:, 0, :], state[:, :, :]))
                    v.sem_inc(s["s_out"], 1)
                else:
                    v.wait_ge(s["e_out"], g + 1)
                    for h in range(H):
                        link(v.tensor_tensor(emb[0:n, h, :, :], spread(em[0:n, h, :], 1, NB),
                                             spread(m.mix("batch_rows")[0:n, :], 2, HD), ALU.mult))
                    v.sem_inc(s["em_ready"], 1)
                    v.wait_ge(s["s_ps"], g + 1)
                    for q in range(C_PAIRS):
                        bank = (ps1[:, 0:512], ps1[:, 512:1024], ps2[:, 0:512])[q].rearrange("p (b v) -> p b v", b=NB)
                        last = eg[g][:, q, 0:n].rearrange("p (b s) -> p b s", b=NB)[:, :, NS - 1:NS].broadcast_to([P, NB, HD])
                        new = m.states[:, A_PAIRS + q, 1:, :]
                        link(v.tensor_tensor(new, m.state0[:, A_PAIRS + q, :, :], last, ALU.mult))
                        link(v.tensor_tensor(new, new, bank, ALU.add))


def residual(link, m, which, psum, tmp):
    v, gate = link.eng, (3 * which + 2) * KD
    for k in range(KD):
        link(v.scalar_tensor_tensor(m.x[:, k, 0:NP], psum[:, k, 0:NP], m.mod[:, gate + k, 0:1], m.x[:, k, 0:NP],
                                    ALU.mult, ALU.add))
    link(v.tensor_tensor(batched(tmp), batched(psum[:, :, NP:NT]), spread(m.mod[:, gate:gate + KD, 1:], 3, NS), ALU.mult))
    link(v.tensor_tensor(m.x[:, :, NP:NT], m.x[:, :, NP:NT], tmp, ALU.add))


def output_block(nc, m, l, hr, stream, small_out, state_out):
    names = ("step squares_ready sums_ready root_ready normed summed x_ready squares2 sums2 root2 h_ready query_out "
             "outs_saved states_saved hi_ready rows_out rows_turned mod_read")
    tiles = (0, 1, 5, 6, 7)
    with signals(nc, names) as s, nc.psum_tensor("ps_w", [P, 8, 512], F32) as ps, nc.Block() as block:
        f = Area(m.big, m.free)
        sq = f.take(5, NT)
        tmp = f.take(KD, NB * NS)
        rows = f.take(D)[0:9, :]

        @block.sync
        def _(sp):
            sp.dma_start(small_out[l, :, :], m.outs[:, :]).then_inc(s["outs_saved"], 16)
            sp.dma_start(state_out[l, :, :], m.states.rearrange("p a b c -> p (a b c)")).then_inc(s["states_saved"], 16)
            load_tiles(sp, m, stream, l, T_GATE1 + RING, T_U + RING)
            sp.wait_ge(s["outs_saved"], 16)
            sp.wait_ge(s["states_saved"], 16)

        @block.scalar
        def _(act):
            def rows_out(last):
                m.wait_done(act, last)
                act.activation(rows, ps[0:9, 5:7, :].rearrange("p a b -> p (a b)"), ACT.Copy).then_inc(s["rows_out"], 1)

            act.activation(sq[:, 0:2, :], m.mixed[:, 0:2, :], ACT.Square)
            act.activation(sq[:, 2:5, :], m.mixed[:, 5:8, :], ACT.Square).then_inc(s["squares_ready"], 1)
            act.wait_ge(s["sums_ready"], 1)
            act.activation(sq[:, :, :], ps[:, 0:5, 0:NT], ACT.Sqrt, bias=m.eps, scale=1.0 / HD).then_inc(s["root_ready"], 1)
            rows_out(T_OUT - 1)
            act.wait_ge(s["x_ready"], 1)
            act.activation(m.square[:, :, :], m.x[:, :, :], ACT.Square).then_inc(s["squares2"], 1)
            act.wait_ge(s["sums2"], 1)
            act.activation(m.rms[:, :], ps[:, 0, 0:NT], ACT.Sqrt, bias=m.eps, scale=1.0 / D).then_inc(s["root2"], 1)
            rows_out(T_QUERY - 1)
            act.wait_ge(s["h_ready"], 1)
            act.activation(hr[:, 0, :, :], m.h[:, :, :], ACT.Copy).then_inc(s["hi_ready"], 1)
            for h in range(HEADS):
                m.wait_done(act, T_QUERY + h)
                act.activation(m.query[:, h, :], ps[:, (h + 1) % 8, 0:NT], ACT.Copy).then_inc(s["query_out"], 1)
            act.wait_ge(s["query_out"], HEADS)
            act.wait_ge(s["hi_ready"], 1)

        @block.vector
        def _(v):
            link = Chain(v, s["step"])
            v.wait_ge(s["root_ready"], 1)
            link(v.reciprocal(sq[:, :, :], sq[:, :, :]))
            for n, t in enumerate(tiles):
                g = m.par("a_norm") if t < 2 else m.par("dn_norm")
                gate = m.zact[:, 6 + t, :] if t < 2 else m.zact[:, 11 + t - 5, :]
                link(v.scalar_tensor_tensor(m.mixed[:, t, :], m.mixed[:, t, :], g, sq[:, n, :], ALU.mult, ALU.mult))
                link(v.tensor_tensor(m.mixed[:, t, :], m.mixed[:, t, :], gate, ALU.mult))
            v.sem_inc(s["normed"], 1)
            v.wait_ge(s["rows_turned"], 1)
            add_bias(link, m, 2, 3, ps[:, 7, :])
            v.sem_inc(s["mod_read"], 1)
            m.wait_done(v, T_GATE2 - 1)
            residual(link, m, 0, ps, tmp)
            v.sem_inc(s["x_ready"], 1)
            v.wait_ge(s["root2"], 1)
            normalise(link, m)
            modulate(link, m, 1, s["h_ready"])
            v.wait_ge(s["h_ready"], 1)
            v.wait_ge(s["rows_turned"], 2)
            add_bias(link, m, 5, 6, ps[:, 0, :])
            v.sem_inc(s["mod_read"], 1)
            v.wait_ge(s["hi_ready"], 1)
            link(v.tensor_tensor(hr[:, 1, :, :], m.h[:, :, :], hr[:, 0, :, :].bitcast(F32), ALU.subtract))

        @block.tensor
        def _(pe):
            pe.wait_ge(s["squares_ready"], 1)
            for n in range(5):
                mm = pe.matmul(ps[:, n, 0:NT], m.mix("block_ones"), sq[:, n, :], start=True, stop=True)
            mm.then_inc(s["sums_ready"], 1)
            cond_rows(pe, m, T_GATE1, ps[0:9, 5:7, :])
            pe.wait_ge(s["rows_out"], 1)
            turn_rows(pe, m, rows, ps[:, 7, :]).then_inc(s["rows_turned"], 1)
            pe.wait_ge(s["normed"], 1)
            for n in range(KD):
                m.wait_tile(pe, T_OUT + n)
                if n == 7:
                    pe.wait_ge(s["mod_read"], 1)
                w = m.tile(T_OUT + n)
                for k in range(KD):
                    mm = pe.matmul(ps[:, n, 0:NT], w[:, k, :], m.mixed[:, k, :], start=(k == 0), stop=(k == KD - 1))
                mm.then_inc(m.done[(T_OUT + n) % RING], 1)
            pe.wait_ge(s["squares2"], 1)
            for k in range(KD):
                mm = pe.matmul(ps[:, 0, 0:NT], m.ones, m.square[:, k, :], start=(k == 0), stop=(k == KD - 1))
            mm.then_inc(s["sums2"], 1)
            cond_rows(pe, m, T_GATE2, ps[0:9, 5:7, :])
            pe.wait_ge(s["rows_out"], 2)
            turn_rows(pe, m, rows, ps[:, 0, :]).then_inc(s["rows_turned"], 1)
            pe.wait_ge(s["h_ready"], 1)
            for h in range(HEADS):
                m.wait_tile(pe, T_QUERY + h)
                if (h + 1) % 8 == 0:
                    pe.wait_ge(s["mod_read"], 2)
                w = m.tile(T_QUERY + h)
                for k in range(KD):
                    mm = pe.matmul(ps[:, (h + 1) % 8, 0:NT], w[:, k, :], m.h[:, k, :], start=(k == 0), stop=(k == KD - 1))
                mm.then_inc(m.done[(T_QUERY + h) % RING], 1)


def experts_block(nc, m, l, hr, stream):
    TT = 96
    TURNS = NKEYS // RING
    HALF = TURNS * 5 // 8
    assert HALF * RING <= 80
    names = "step score_ps score_out found act_out hi_ready lo_ready parts_used"
    with signals(nc, names) as s, nc.psum_tensor("ps_s", [P, 2048], F32) as ps_s, \
            nc.psum_tensor("ps_u", [P, RING, 512], F32) as ps_u, nc.Block() as block:

        @block.sync
        def _(sp):
            load_many(sp, m, stream, l, T_U + RING, T_V + RING)

        @block.tensor
        def _(pe):
            def tile(g, j):
                pe.wait_ge(s["act_out"], g * RING + (j + 1))
                split_product(pe, m, s, T_U, g, j, hr, ps_u[:, j, 0:NT])

            assert RING == 3
            for tt in range(3):
                if tt:
                    pe.wait_ge(s["score_out"], tt)
                for h in range(HEADS):
                    for side in range(2):
                        r, c = side * 64, (side * HEADS + h) * NKEYS
                        mm = pe.matmul(ps_s[0:TT, c:c + NKEYS], m.query[r:r + 64, h, tt * TT:(tt + 1) * TT],
                                       m.par("keys")[r:r + 64, :], start=True, stop=True)
                mm.then_inc(s["score_ps"], 1)
                tile(0, tt)
            each_tile(pe, RING, NKEYS, tile)

        @block.scalar
        def _(act):
            act.sem_inc(s["act_out"], RING)
            act.sem_inc(s["parts_used"], PARTS)

            def scores(tt):
                act.wait_ge(s["score_ps"], tt + 1)
                act.activation(m.score[0:TT, tt, :, :].rearrange("p a b -> p (a b)"), ps_s[0:TT, :], ACT.Copy).then_inc(
                    s["score_out"], 1)

            def gelu(g, j):
                act.wait_ge(s["parts_used"], g * 2 * RING + (2 * (j + 1) + PARTS))
                act.activation(m.act[:, ds(g * RING + j, 1), :].squeeze(1), ps_u[:, j, 0:NT],
                               ACT.Gelu_apprx_tanh).then_inc(s["act_out"], 1)

            def tile(g, j):
                split_high(act, m, s, T_U, g, j + 2, 0)
                gelu(g, j)
                split_high(act, m, s, T_U, g, j + 2, 1)

            for q in range(PARTS):
                split_high(act, m, s, T_U, 0, q // 2, q % 2)
            scores(0)
            split_high(act, m, s, T_U, 0, 1, 1)
            scores(1)
            tile(0, 0)
            scores(2)
            tile(0, 1)
            tile(0, 2)
            each_tile(act, RING, HALF * RING, tile)
            act.wait_ge(s["found"], 3)
            each_tile(act, HALF * RING, NKEYS - 2, tile)
            for n in (NKEYS - 2, NKEYS - 1):
                gelu(n // RING, n % RING)

        @block.gpsimd
        def _(pool):
            def tile(g, j):
                for half in range(2):
                    split_low(pool, m, s, T_U, g, j, half)

            each_tile(pool, 0, NKEYS, tile)

        @block.vector
        def _(v):
            link = Chain(v, s["step"])
            sides = m.score[0:TT, :, :, :]
            r = slice(0, TT)

            def top16(values, best, index):
                link(v.max(best[:, 0:8], values))
                v.max_index(index[:, 0:8], best[:, 0:8], values)
                link(v.match_replace(values, best[:, 0:8], values, -3.4e38))
                link(v.max(best[:, 8:16], values))
                link(v.max_index(index[:, 8:16], best[:, 8:16], values))

            for tt in range(3):
                v.wait_ge(s["score_out"], tt + 1)
                for n in range(2 * HEADS):
                    top16(sides[:, tt, n, :], m.best[r, n, :], m.besti[r, n, :])
                link(v.tensor_copy(m.bestf[r, :, :], m.besti[r, :, :]))
                b = m.best[r, :, :].rearrange("p (s h) k -> p s h k", s=2)
                c = m.cand[r, :, :].rearrange("p h (a b) -> p h a b", a=TOPK)
                link(v.tensor_tensor(c, spread(b[:, 0, :, :], 3, TOPK), spread(b[:, 1, :, :], 2, TOPK), ALU.add))
                score = m.sel[r, 2, tt, :].rearrange("p (h k) -> p h k", h=HEADS)
                pos = m.pos[r, :].rearrange("p (h k) -> p h k", h=HEADS)
                for h in range(HEADS):
                    top16(m.cand[r, h, :], score[:, h, :], pos[:, h, :])
                link(v.tensor_tensor(m.posf[r, :].rearrange("p (h k) -> p h k", h=HEADS), score,
                                     score[:, :, 0:1].broadcast_to([TT, HEADS, TOPK]), ALU.subtract))
                link(v.tensor_copy(m.sel[r, 2, tt, :], m.posf[r, :]))
                for side, op, arg in ((0, ALU.logical_shift_right, 4), (1, ALU.bitwise_and, 15)):
                    link(v.tensor_single_scalar(m.posp[r, :], m.pos[r, :], arg, op))
                    link(v.tensor_copy(m.posf[r, :], m.posp[r, :]))
                    link(v.tensor_tensor(m.hit[r, :, :], spread(m.posf[r, :], 2, TOPK), spread(m.iota[r, 0:TOPK], 1, HEADS * TOPK),
                                         ALU.is_equal))
                    keys = m.bestf[r, side * HEADS:(side + 1) * HEADS, :]
                    hit = m.hit[r, :, :].rearrange("p (h k) a -> p h k a", h=HEADS)
                    link(v.tensor_tensor(hit, hit, spread(keys, 2, TOPK), ALU.mult))
                    link(v.tensor_reduce(m.sel[r, side, tt, :], m.hit[r, :, :], AX, ALU.add))
                v.sem_inc(s["found"], 1)


def gates_block(nc, m, l):
    TT = 96
    GROUP = 4
    TURN = 12
    SETS = TURN // GROUP
    TURNS = NT // TURN
    names = "step exp_ready gates_ready turned turned_out first_ready distance_ready square_ready second_ready gate_ps weighted"
    with signals(nc, names) as s, nc.sbuf_tensor("selT", [P, 3, NT], F32) as selT, \
            nc.sbuf_tensor("onehot", [P, 2, SETS, GROUP, P], F32) as onehot, nc.psum_tensor("ps_t", [P, 2, 512], F32) as ps_t, \
            nc.psum_tensor("ps_g", [P, SETS, GROUP, P], F32) as ps_g, nc.Block() as block:
        e = m.sel[0:TT, 2, :, :].rearrange("p t (h k) -> p t h k", h=HEADS)
        total = m.rms[0:TT, 0:3 * HEADS].rearrange("p (t h) -> p t h", h=HEADS)
        first, second = onehot[:, 0, :, :, :], onehot[:, 1, :, :, :]

        @block.scalar
        def _(act):
            act.activation(m.sel[0:TT, 2, :, :], m.sel[0:TT, 2, :, :], ACT.Exp).then_inc(s["exp_ready"], 1)
            for kind in range(3):
                act.wait_ge(s["turned"], kind + 1)
                act.activation(selT[:, kind, :], ps_t[:, kind % 2, 0:NT], ACT.Copy).then_inc(s["turned_out"], 1)

            def group(i, g):
                q = i * SETS + (g + 1)
                act.wait_ge(s["distance_ready"], q)
                act.activation(second[:, g, :, :], second[:, g, :, :], ACT.Square).then_inc(s["square_ready"], 1)
                act.wait_ge(s["square_ready"], q)
                act.activation(second[:, g, :, :], second[:, g, :, :], ACT.Relu, bias=m.ones[:, 0:1], scale=-1.0).then_inc(
                    s["second_ready"], 1)

            with act.Fori(0, TURNS) as i:
                for g in range(SETS):
                    group(i, g)

        @block.tensor
        def _(pe):
            pe.sem_inc(s["gate_ps"], SETS)
            for kind in range(3):
                if kind == 2:
                    pe.wait_ge(s["turned_out"], 1)
                    pe.wait_ge(s["gates_ready"], 1)
                for tt in range(3):
                    mm = pe.transpose(ps_t[:, kind % 2, tt * TT:(tt + 1) * TT], m.sel[0:TT, kind, tt, :], m.ident[0:TT, 0:TT])
                mm.then_inc(s["turned"], 1)
            with pe.Fori(0, TURNS) as i:
                for g in range(SETS):
                    pe.wait_ge(s["weighted"], i * SETS + (g + 1))
                    pe.wait_ge(s["second_ready"], i * SETS + (g + 1))
                    for c in range(GROUP):
                        if c % 2 == 0:
                            pe.wait_ge(s["first_ready"], i * (TURN // 2) + (g * GROUP // 2 + c // 2 + 1))
                        mm = pe.matmul(ps_g[:, g, c, :], first[:, g, c, :], second[:, g, c, :], start=True, stop=True)
                    mm.then_inc(s["gate_ps"], 1)

        @block.gpsimd
        def _(pool):
            pool.wait_ge(s["turned_out"], 3)
            with pool.Fori(0, TURNS) as i:
                for g in range(SETS):
                    pool.wait_ge(s["gate_ps"], i * SETS + (g + 1))
                    pool.tensor_tensor(second[:, g, :, :], spread(m.iota, 1, GROUP),
                                       spread(selT[:, 1, ds(i * TURN + g * GROUP, GROUP)], 2, P),
                                       ALU.subtract).then_inc(s["distance_ready"], 1)

        @block.vector
        def _(v):
            link = Chain(v, s["step"])
            v.wait_ge(s["exp_ready"], 1)
            link(v.tensor_reduce(total, e, AX, ALU.add))
            link(v.reciprocal(total, total))
            v.tensor_tensor(e, e, spread(total, 3, TOPK), ALU.mult).then_inc(s["gates_ready"], 1)
            v.wait_ge(s["turned_out"], 3)
            v.sem_inc(s["weighted"], SETS)

            def onehots(i, g):
                set_ = g % SETS
                v.wait_ge(s["gate_ps"], i * SETS + (g + 1))
                for c in range(GROUP):
                    t = g * GROUP + c
                    o = v.tensor_scalar(first[:, set_, c, :], m.iota, selT[:, 0, ds(i * TURN + t, 1)],
                                        selT[:, 2, ds(i * TURN + t, 1)], ALU.is_equal, ALU.mult)
                    if c % 2:
                        o.then_inc(s["first_ready"], 1)

            def weigh(i, g):
                v.wait_ge(s["gate_ps"], i * SETS + (g + 1 + SETS))
                a = m.act[:, :, ds(i * TURN + g * GROUP, GROUP)]
                v.tensor_tensor(a, a, ps_g[:, g, :, :].rearrange("p t e -> p e t"), ALU.mult).then_inc(s["weighted"], 1)

            onehots(0, 0)
            with v.Fori(0, TURNS - 1) as i:
                for g in range(SETS):
                    onehots(i, g + 1)
                    weigh(i, g)
            for g in range(SETS):
                if g + 1 < SETS:
                    onehots(TURNS - 1, g + 1)
                weigh(TURNS - 1, g)


def combine_block(nc, m, l, stream):
    AHEAD = 3
    assert RING % AHEAD == 0 and PARTS == 3
    names = "step zeroed summed hi_ready lo_ready parts_used act_hi act_lo"
    with signals(nc, names) as s, nc.psum_tensor("ps_y", [P, 8, 512], F32) as ps, \
            nc.sbuf_tensor("act_parts", [P, AHEAD, 2, NT], F32R) as act_parts, \
            nc.sbuf_tensor("zeros", [P, NT], BF16) as zeros, \
            nc.sbuf_tensor("gated", [P, KD, NB * NS], F32) as tmp, nc.Block() as block:

        def column(g, j):
            return m.act[:, ds(g * RING + j, 1), :].squeeze(1)

        @block.sync
        def _(sp):
            load_many(sp, m, stream, l, T_V + RING, TILES)

        @block.tensor
        def _(pe):
            pe.wait_ge(s["zeroed"], 1)
            for k in range(KD):
                pe.matmul(ps[:, k, 0:NT], zeros[:, 0:P], zeros[:, :], start=True, stop=False)

            def tile(g, j):
                pe.wait_ge(s["act_hi"], g * RING + (j + 1))
                for half in range(2):
                    hi, lo = part(m, 2 * j + half, 0), part(m, 2 * j + half, 1)
                    pe.wait_ge(s["hi_ready"], g * 2 * RING + (2 * j + half + 1))
                    for side in range(2):
                        if side and half == 0:
                            pe.wait_ge(s["act_lo"], g * RING + (j + 1))
                        for k in range(KD // 2):
                            pe.matmul(ps[:, half * KD // 2 + k, 0:NT], hi[:, k, :], act_parts[:, j % AHEAD, side, :],
                                      start=False, stop=False)
                    wait_low(pe, m, s, T_V, g, j, half)
                    for k in range(KD // 2):
                        mm = pe.matmul(ps[:, half * KD // 2 + k, 0:NT], lo[:, k, :], act_parts[:, j % AHEAD, 0, :],
                                       start=False, stop=False)
                    mm.then_inc(s["parts_used"], 1)

            each_tile(pe, 0, NKEYS, tile)
            for k in range(KD):
                mm = pe.matmul(ps[:, k, 0:NT], zeros[:, 0:P], zeros[:, :], start=False, stop=True)
            mm.then_inc(s["summed"], 1)

        @block.scalar
        def _(act):
            act.sem_inc(s["parts_used"], PARTS)

            def tile(g, j):
                act.wait_ge(s["parts_used"], g * 2 * RING + (2 * j + PARTS - 2))
                act.activation(act_parts[:, j % AHEAD, 0, :], column(g, j), ACT.Copy).then_inc(s["act_hi"], 1)
                for half in range(2):
                    split_high(act, m, s, T_V, g, j, half)

            each_tile(act, 0, NKEYS, tile)

        @block.gpsimd
        def _(pool):
            def tile(g, j):
                pool.wait_ge(s["act_hi"], g * RING + (j + 1))
                pool.tensor_tensor(act_parts[:, j % AHEAD, 1, :], column(g, j), act_parts[:, j % AHEAD, 0, :].bitcast(F32),
                                   ALU.subtract).then_inc(s["act_lo"], 1)

            each_tile(pool, 0, NKEYS, tile)

        @block.vector
        def _(v):
            link = Chain(v, s["step"])
            v.memset(zeros[:, :], 0.0).then_inc(s["zeroed"], 1)

            def tile(g, j):
                for half in range(2):
                    split_low(v, m, s, T_V, g, j, half)

            each_tile(v, 0, NKEYS, tile)
            v.wait_ge(s["summed"], 1)
            residual(link, m, 1, ps, tmp[:, :, :])


def final_block(nc, m, y_out):
    with signals(nc, "step squares_ready sums_ready root_ready y_ready saved") as s, \
            nc.psum_tensor("ps_f", [P, 512], F32) as ps, nc.Block() as block:
        @block.scalar
        def _(act):
            act.activation(m.square[:, :, :], m.x[:, :, :], ACT.Square).then_inc(s["squares_ready"], 1)
            act.wait_ge(s["sums_ready"], 1)
            act.activation(m.rms[:, :], ps[:, 0:NT], ACT.Sqrt, bias=m.eps, scale=1.0 / D).then_inc(s["root_ready"], 1)

        @block.tensor
        def _(pe):
            pe.wait_ge(s["squares_ready"], 1)
            for k in range(KD):
                mm = pe.matmul(ps[:, 0:NT], m.ones, m.square[:, k, :], start=(k == 0), stop=(k == KD - 1))
            mm.then_inc(s["sums_ready"], 1)

        @block.vector
        def _(v):
            link = Chain(v, s["step"])
            v.wait_ge(s["root_ready"], 1)
            link(v.reciprocal(m.rms[:, :], m.rms[:, :]))
            for k in range(KD):
                i = v.scalar_tensor_tensor(m.h[:, k, :], m.x[:, k, :], m.par("final")[:, k:k + 1], m.rms[:, :],
                                           ALU.mult, ALU.mult)
            i.then_inc(s["y_ready"], 1)

        @block.sync
        def _(sp):
            sp.wait_ge(s["y_ready"], 1)
            sp.dma_start(y_out, m.h[:, :, :]).then_inc(s["saved"], 16)
            sp.wait_ge(s["saved"], 16)


def build(nc, stream, small_in, mixc_in, keep_in, state_in, x_in, c_in, y_out, small_out, state_out):
    with ExitStack() as ctx:
        m = Memory(nc, ctx)
        setup_block(nc, m, x_in, c_in, keep_in)
        with nc.Fori(0, DEPTH) as l:
            with nc.sbuf_tensor("x_parts", [P, 2, KD, NT], F32R) as hr:
                project_block(nc, m, l, hr, stream, small_in, mixc_in, state_in)
            local_block(nc, m, l, stream)
            hgrn_block(nc, m, l)
            delta_block(nc, m, l)
            with nc.sbuf_tensor("h_parts", [P, 2, KD, NT], F32R) as hr:
                output_block(nc, m, l, hr, stream, small_out, state_out)
                experts_block(nc, m, l, hr, stream)
            gates_block(nc, m, l)
            combine_block(nc, m, l, stream)
            for sem in m.loaded + m.done:
                nc.sync.sem_clear(sem)
            nc.all_engine_barrier()
        final_block(nc, m, y_out)


def host_layout(a):
    import numpy as np
    f = np.float32

    def cols(w):
        n = w.shape[2] // P
        return w.reshape(DEPTH, KD, P, n, P).transpose(0, 3, 2, 1, 4).reshape(DEPTH, n, P, D)

    stream = np.zeros((DEPTH, TILES, P, D), f)
    ada = a["w_ada"].reshape(DEPTH, KD, P, 6, D).transpose(0, 3, 1, 2, 4)
    stream[:, T_ADA:T_IN] = ada[:, :EARLY_ADA].reshape(DEPTH, -1, P, D)
    for first, which in ((T_SHIFT2, 3), (T_SCALE2, 4), (T_GATE1, 2), (T_GATE2, 5)):
        stream[:, first:first + KD] = ada[:, which]
    stream[:, T_IN:T_BETA] = cols(a["w_in"][:, :, :IN_TILES * P])[:, Z_ORDER]
    stream[:, T_BETA].reshape(DEPTH, P, KD, P)[:, :, :, :12] = \
        a["w_in"][:, :, IN_TILES * P:].reshape(DEPTH, KD, P, 12).transpose(0, 2, 1, 3)
    gate = stream[:, T_GATE].reshape(DEPTH, P, 8, P)
    for g, name in enumerate(("lru_wa", "lru_wx")):
        for t in range(B_TILES):
            for r in range(2):
                rows = slice(r * HD, (r + 1) * HD)
                gate[:, rows, g * B_TILES + t, rows] = a[name][:, 2 * t + r]
    stream[:, T_OUT:T_GATE2] = cols(a["w_out"])
    stream[:, T_QUERY:T_U] = cols(a["peer_wq"])
    stream[:, T_U:T_V] = a["peer_u"].reshape(DEPTH, NKEYS, NKEYS, KD, P).transpose(0, 2, 4, 3, 1).reshape(DEPTH, NKEYS, P, D)
    stream[:, T_V:] = a["peer_v"].reshape(DEPTH, NKEYS, NKEYS, D).transpose(0, 2, 1, 3)

    small = np.zeros((DEPTH, P, SMALL_W), f)

    def put(name, value):
        small[:, :, SMALL[name][0]:SMALL[name][1]] = value

    def feat(v):
        return v.reshape(DEPTH, -1, P).transpose(0, 2, 1)

    put("norm1", feat(a["norm1_g"]))
    put("norm2", feat(a["norm2_g"]))
    put("b_ada", feat(a["b_ada"]))
    put("lru_w", a["lru_conv_w"].reshape(DEPTH, CONV, B_TILES, P).transpose(0, 3, 2, 1).reshape(DEPTH, P, -1))
    put("lru_b", feat(a["lru_conv_b"]))
    put("dn_w", a["dn_conv_w"].reshape(DEPTH, CONV, 9, P).transpose(0, 3, 2, 1).reshape(DEPTH, P, -1))
    put("ba", feat(a["lru_ba"]))
    put("bx", feat(a["lru_bx"]))
    put("lru_L", feat(a["lru_L"]))
    put("a_norm", np.concatenate([a["a_norm_g"]] * 2, 1)[:, :, None])
    put("dn_norm", np.concatenate([a["dn_norm_g"]] * 2, 1)[:, :, None])
    put("a_log", a["dn_A_log"][:, None, :])
    put("dt_bias", a["dn_dt_bias"][:, None, :])
    put("final", a["final_norm_g"].reshape(KD, P).T[None])
    put("lb", np.concatenate([a["lb_param"][n].reshape(A_PAIRS, P).T for n in range(DEPTH)], 1)[None])
    put("lb_on", (np.arange(DEPTH) > 0).astype(f)[:, None, None])
    put("keys", np.concatenate([a["peer_k1"], a["peer_k2"]], 2).transpose(0, 2, 1))
    put("lru_h", a["state_lru_h"].reshape(DEPTH, NB, B_TILES, P).transpose(0, 3, 2, 1).reshape(DEPTH, P, -1))
    for name, key, n in (("lru_conv", "state_lru_conv", B_TILES), ("dn_conv", "state_dn_conv", 9)):
        put(name, a[key].reshape(DEPTH, NB, CONV - 1, n, P).transpose(0, 4, 3, 1, 2).reshape(DEPTH, P, -1))

    mixc = np.zeros((P, MIXC_W), f)

    def const(name, value):
        v = np.asarray(value, f)
        mixc[:v.shape[0], MIXC[name][0]:MIXC[name][1]] = v

    j, i = np.arange(P)[:, None], np.arange(P)[None, :]
    const("block_ones", j // HD == i // HD)
    const("levels", np.concatenate([(j >> (b + 1) == i >> (b + 1)) & ((j >> b) % 2 == 0) & ((i >> b) % 2 == 1)
                                    for b in range(7)], 1))
    same = (j // NS == i // NS) & (j <= i)
    const("tri", j <= i)
    const("tri_s", same[:32, :32])
    const("neg", np.where(j <= i, 0.0, -1e30))
    const("neg_s", np.where(same, 0.0, -1e30)[:32, :32])
    const("block_rows", j // 8 == np.arange(P // 8)[None, :])
    tok = np.arange(NB * NS) // NS
    const("batch_cols", np.tile((np.arange(NB)[:, None] == tok[None, :]).reshape(1, -1), (P, 1)))
    const("batch_rows", tok[:, None] == np.arange(NB)[None, :])
    keep = np.concatenate([np.eye(P), np.ones((P, P)), np.tile(np.arange(P), (P, 1)), np.full((P, 1), EPS)], 1).astype(f)

    def heads(v, n):
        return v.reshape(DEPTH, NB, n, 2, HD, HD).transpose(0, 3, 4, 2, 1, 5).reshape(DEPTH, P, -1)

    state = np.concatenate([heads(a["state_hgrn"], A_PAIRS), heads(a["state_dn"], C_PAIRS)], 2)
    x = np.concatenate([a["x_prompt"].reshape(NP, D), a["x_sample"].reshape(NB * NS, D)], 0)
    c = np.concatenate([a["c_prompt"], a["c_sample"]], 0)
    return {"stream": stream, "small": small, "mixc": mixc, "keep": keep, "state": np.ascontiguousarray(state),
            "x": np.ascontiguousarray(x.reshape(NT, KD, P).transpose(2, 1, 0)),
            "c": np.ascontiguousarray(c.reshape(1 + NB, KD, P).transpose(2, 1, 0))}


OUTPUTS = {"y": (P, KD, NT), "small_out": (DEPTH, P, OUTS_W), "state_out": (DEPTH, P, STATE_W)}


def host_outputs(r):
    import numpy as np
    y = r["y"].transpose(2, 1, 0).reshape(NT, D)
    so = {k: r["small_out"][:, :, a:b] for k, (a, b) in OUTS.items()}
    st = r["state_out"].reshape(DEPTH, 2, HD, A_PAIRS + C_PAIRS, 1 + NB, HD).transpose(0, 4, 3, 1, 2, 5)

    def heads(b0, b1, q0, q1):
        v = st[:, b0:b1, q0:q1]
        return np.ascontiguousarray(v.reshape(DEPTH, b1 - b0, 2 * (q1 - q0), HD, HD))

    def conv(v, n, nb):
        return np.ascontiguousarray(v.reshape(DEPTH, P, n, nb, 3).transpose(0, 3, 4, 2, 1).reshape(DEPTH, nb, 3, n * P))

    def vec(v, nb):
        return np.ascontiguousarray(v.reshape(DEPTH, P, B_TILES, nb).transpose(0, 3, 2, 1).reshape(DEPTH, nb, B_TILES * P))

    ap, cp = A_PAIRS, A_PAIRS + C_PAIRS
    return (np.ascontiguousarray(y[:NP].reshape(1, NP, D)), np.ascontiguousarray(y[NP:].reshape(NB, NS, D)),
            heads(0, 1, 0, ap), vec(so["p_h"], 1), conv(so["p_lc"], B_TILES, 1), heads(0, 1, ap, cp), conv(so["p_dc"], 9, 1),
            heads(1, 1 + NB, 0, ap), vec(so["s_h"], NB), conv(so["s_lc"], B_TILES, NB), heads(1, 1 + NB, ap, cp),
            conv(so["s_dc"], 9, NB))


def kernel(**inputs):
    import numpy as np
    import concourse.bacc as bacc
    from concourse.bass_utils import run_bass_kernel_spmd

    arrays = host_layout({k: np.asarray(v) for k, v in inputs.items()})
    nc = bacc.Bacc("TRN2", target_bir_lowering=False, num_devices=1)
    ins = [nc.dram_tensor(f"in_{k}", v.shape, F32, kind="ExternalInput").ap() for k, v in arrays.items()]
    outs = [nc.dram_tensor(f"out_{k}", v, F32, kind="ExternalOutput").ap() for k, v in OUTPUTS.items()]
    build(nc, *ins, *outs)
    r = run_bass_kernel_spmd(nc, [{f"in_{k}": v for k, v in arrays.items()}], core_ids=[0]).results[0]
    return host_outputs({k: r[f"out_{k}"] for k in OUTPUTS})
```
